# Optimizing a Trainium2 kernel written in Bass

```python
import math
import jax, jax.numpy as jnp
from jax import lax
import numpy as np

D_MODEL = 2048
BATCH = 1
SEQ = 256
DEPTH = 1
DEC_BATCH = 8
DEC_SEQ = 4
PAST_LEN = 2048
PAGE_SIZE = 128

MIX_WIDTH = D_MODEL
MLSTM_WIDTH = MIX_WIDTH // 2
MLSTM_HEADS = 4
MLSTM_HEAD_DIM = MLSTM_WIDTH // MLSTM_HEADS
MLSTM_CHUNK = 64
SSM_WIDTH = MIX_WIDTH - MLSTM_WIDTH
SSM_GROUP = 16
SSM_GROUPS = SSM_WIDTH // SSM_GROUP
SSM_STATE = 64
PLE_DIM = 256
PEER_HEADS = 8
PEER_KEYS = 128
PEER_EXPERTS = PEER_KEYS * PEER_KEYS
PEER_TOPK = 16
PEER_KEY_DIM = 128
PEER_BLOCK = 128
EPS = 1e-6

OFF_Q = 0
OFF_K = OFF_Q + MLSTM_WIDTH
OFF_V = OFF_K + MLSTM_WIDTH
OFF_O = OFF_V + MLSTM_WIDTH
OFF_I = OFF_O + MLSTM_WIDTH
OFF_F = OFF_I + MLSTM_HEADS
OFF_U = OFF_F + MLSTM_HEADS
IN_COLS = OFF_U + SSM_WIDTH

kernel_name = 'hymba_mlstm_s5_peer_decode_step'

def rmsnorm(x, g):
    x32 = x.astype(jnp.float32)
    y = x32 * lax.rsqrt(jnp.mean(x32 * x32, axis=-1, keepdims=True) + EPS)
    return (y * g.astype(jnp.float32)).astype(x.dtype)

def mlstm_chunkwise(q, k, v, ig, lf, C0, n0, m0):
    f32 = jnp.float32
    Bt, S, H, dh = q.shape
    L = math.gcd(S, MLSTM_CHUNK)
    nc = S // L

    def to_chunks(t):
        t = t.astype(f32).reshape((Bt, nc, L, H) + t.shape[3:])
        return jnp.swapaxes(jnp.moveaxis(t, 1, 0), 2, 3)

    qc, kc, vc, igc, lfc = (to_chunks(t) for t in (q, k, v, ig, lf))
    causal = jnp.tril(jnp.ones((L, L), dtype=bool))

    def step(carry, inp):
        C, n, m = carry
        qb, kb, vb, igb, lfb = inp
        b = jnp.cumsum(lfb, axis=-1)
        dmat = jnp.where(causal, b[..., :, None] - b[..., None, :] + igb[..., None, :], -jnp.inf)
        inter = b + m[..., None]
        m_t = jnp.maximum(inter, jnp.max(dmat, axis=-1))
        w_intra = jnp.exp(dmat - m_t[..., None])
        w_inter = jnp.exp(inter - m_t)
        s = jnp.einsum('bhtd,bhsd->bhts', qb, kb) * w_intra
        num = w_inter[..., None] * jnp.einsum('bhtd,bhde->bhte', qb, C) + jnp.einsum('bhts,bhse->bhte', s, vb)
        den = w_inter * jnp.einsum('bhtd,bhd->bht', qb, n) + jnp.sum(s, axis=-1)
        hb = num / jnp.maximum(jnp.abs(den), jnp.exp(-m_t))[..., None]
        b_last = b[..., -1]
        dec = b_last[..., None] - b + igb
        m_new = jnp.maximum(b_last + m, jnp.max(dec, axis=-1))
        kw = kb * jnp.exp(dec - m_new[..., None])[..., None]
        sc = jnp.exp(b_last + m - m_new)
        C_new = sc[..., None, None] * C + jnp.einsum('bhsd,bhse->bhde', kw, vb)
        n_new = sc[..., None] * n + jnp.sum(kw, axis=-2)
        return (C_new, n_new, m_new), hb

    (C1, n1, m1), hs = lax.scan(step, (C0.astype(f32), n0.astype(f32), m0.astype(f32)),
                                (qc, kc, vc, igc, lfc))
    hs = jnp.swapaxes(jnp.moveaxis(hs, 0, 1), 2, 3).reshape(Bt, S, H, dh)
    return hs, C1, n1, m1

def _complex_affine_combine(e1, e2):
    a1r, a1i, b1r, b1i = e1
    a2r, a2i, b2r, b2i = e2
    return (a2r * a1r - a2i * a1i,
            a2r * a1i + a2i * a1r,
            a2r * b1r - a2i * b1i + b2r,
            a2r * b1i + a2i * b1r + b2i)

def s5_scan(u, A_re, A_im, B_re, B_im, C_re, C_im, Dd, log_dt, s0_re, s0_im):
    f32 = jnp.float32
    u = u.astype(f32)
    A_re, A_im, B_re, B_im, C_re, C_im, Dd, log_dt, s0_re, s0_im = (
        t.astype(f32) for t in (A_re, A_im, B_re, B_im, C_re, C_im, Dd, log_dt, s0_re, s0_im))
    dt = jnp.exp(log_dt)[:, None]
    mag = jnp.exp(dt * A_re)
    ab_re = mag * jnp.cos(dt * A_im)
    ab_im = mag * jnp.sin(dt * A_im)
    den = A_re * A_re + A_im * A_im
    xr = ab_re - 1.0
    f_re = (xr * A_re + ab_im * A_im) / den
    f_im = (ab_im * A_re - xr * A_im) / den
    Bb_re = f_re[..., None] * B_re - f_im[..., None] * B_im
    Bb_im = f_re[..., None] * B_im + f_im[..., None] * B_re
    bu_re = jnp.einsum('gpc,bsgc->bsgp', Bb_re, u)
    bu_im = jnp.einsum('gpc,bsgc->bsgp', Bb_im, u)
    bu_re = bu_re.at[:, 0].add(ab_re * s0_re - ab_im * s0_im)
    bu_im = bu_im.at[:, 0].add(ab_re * s0_im + ab_im * s0_re)
    a_re = jnp.broadcast_to(ab_re, bu_re.shape)
    a_im = jnp.broadcast_to(ab_im, bu_im.shape)
    _, _, st_re, st_im = lax.associative_scan(_complex_affine_combine, (a_re, a_im, bu_re, bu_im), axis=1)
    y = (jnp.einsum('gcp,bsgp->bsgc', C_re, st_re) - jnp.einsum('gcp,bsgp->bsgc', C_im, st_im)
         + Dd * u)
    return y, st_re[:, -1], st_im[:, -1]

def peer_ffn(c, w_q, keys, U, V):
    f32 = jnp.float32
    T, D = c.shape
    half = PEER_KEY_DIM // 2
    q = (c @ w_q).astype(f32).reshape(T, PEER_HEADS, PEER_KEY_DIM)
    kf = keys.astype(f32)
    s1 = jnp.einsum('thd,hkd->thk', q[..., :half], kf[:, 0])
    s2 = jnp.einsum('thd,hkd->thk', q[..., half:], kf[:, 1])
    v1, i1 = lax.top_k(s1, PEER_TOPK)
    v2, i2 = lax.top_k(s2, PEER_TOPK)
    cand = (v1[..., :, None] + v2[..., None, :]).reshape(T, PEER_HEADS, PEER_TOPK * PEER_TOPK)
    vs, ic = lax.top_k(cand, PEER_TOPK)
    e1 = jnp.take_along_axis(i1, ic // PEER_TOPK, axis=-1)
    e2 = jnp.take_along_axis(i2, ic % PEER_TOPK, axis=-1)
    idx = e1 * PEER_KEYS + e2
    g = jax.nn.softmax(vs, axis=-1)

    nb = -(-T // PEER_BLOCK)
    pad = nb * PEER_BLOCK - T
    cp = jnp.pad(c, ((0, pad), (0, 0))).reshape(nb, PEER_BLOCK, D)
    ip = jnp.pad(idx, ((0, pad), (0, 0), (0, 0))).reshape(nb, PEER_BLOCK, PEER_HEADS, PEER_TOPK)
    gp = jnp.pad(g, ((0, pad), (0, 0), (0, 0))).reshape(nb, PEER_BLOCK, PEER_HEADS, PEER_TOPK)

    def block(args):
        xb, ib, gb = args
        ub = jnp.take(U, ib, axis=0)
        act = jax.nn.gelu(jnp.einsum('thkd,td->thk', ub, xb).astype(f32)) * gb
        vb = jnp.take(V, ib, axis=0)
        return jnp.einsum('thk,thkd->td', act.astype(V.dtype), vb).astype(c.dtype)

    out = lax.map(block, (cp, ip, gp))
    return out.reshape(nb * PEER_BLOCK, D)[:T]

def hybrid_layer(h, p, C0, n0, m0, s0r, s0i, prm):
    f32 = jnp.float32
    Bt, S, _ = h.shape
    H, dh = MLSTM_HEADS, MLSTM_HEAD_DIM
    a = rmsnorm(h, prm['norm_mix'])
    z = a @ prm['w_in']
    q = z[..., OFF_Q:OFF_K].reshape(Bt, S, H, dh)
    k = z[..., OFF_K:OFF_V].reshape(Bt, S, H, dh) * (dh ** -0.5)
    v = z[..., OFF_V:OFF_O].reshape(Bt, S, H, dh)
    o = jax.nn.sigmoid(z[..., OFF_O:OFF_I].astype(f32))
    ig = z[..., OFF_I:OFF_F].astype(f32) + prm['b_igate'].astype(f32)
    lf = jax.nn.log_sigmoid(z[..., OFF_F:OFF_U].astype(f32) + prm['b_fgate'].astype(f32))
    u = z[..., OFF_U:].reshape(Bt, S, SSM_GROUPS, SSM_GROUP)

    hm, C1, n1, m1 = mlstm_chunkwise(q, k, v, ig, lf, C0, n0, m0)
    hm = hm * lax.rsqrt(jnp.mean(hm * hm, axis=-1, keepdims=True) + EPS)
    hm = hm.reshape(Bt, S, MLSTM_WIDTH) * prm['mlstm_norm'].astype(f32) * o

    ys, s1r, s1i = s5_scan(u, prm['ssm_A_re'], prm['ssm_A_im'], prm['ssm_B_re'], prm['ssm_B_im'],
                           prm['ssm_C_re'], prm['ssm_C_im'], prm['ssm_D'], prm['ssm_log_dt'], s0r, s0i)
    ys = jax.nn.gelu(ys.reshape(Bt, S, SSM_WIDTH))
    ys = ys * jax.nn.sigmoid(ys @ prm['w_glu'].astype(f32) + prm['b_glu'].astype(f32))

    mix = jnp.concatenate([hm, ys], axis=-1).astype(h.dtype) @ prm['w_out']
    h = h + mix
    c = rmsnorm(h, prm['norm_ffn'])
    h = h + peer_ffn(c.reshape(Bt * S, D_MODEL), prm['peer_w_q'], prm['peer_keys'],
                     prm['peer_u'], prm['peer_v']).reshape(Bt, S, D_MODEL)
    gate = jax.nn.sigmoid((rmsnorm(h, prm['norm_ple']) @ prm['w_ple_gate']).astype(f32))
    e = (p @ prm['w_ple_proj']).astype(f32)
    h = h + (e * gate).astype(h.dtype)
    return h, (C1, n1, m1, s1r, s1i)

def setup_inputs(seed: int = 0) -> dict:
    key = jax.random.key(seed)
    ks = jax.random.split(key, 40)
    f32 = jnp.float32
    L = DEPTH
    G, P = SSM_GROUPS, SSM_STATE

    def nrm(i, shape, scale):
        return jax.random.normal(ks[i], shape, f32) * scale

    return {
        'x_prompt': nrm(0, (BATCH, SEQ, D_MODEL), 1.0),
        'x_sample': nrm(1, (DEC_BATCH, DEC_SEQ, D_MODEL), 1.0),
        'state_mlstm_C': nrm(2, (L, DEC_BATCH, MLSTM_HEADS, MLSTM_HEAD_DIM, MLSTM_HEAD_DIM), 0.02),
        'state_mlstm_n': nrm(3, (L, DEC_BATCH, MLSTM_HEADS, MLSTM_HEAD_DIM), 0.1),
        'state_mlstm_m': nrm(4, (L, DEC_BATCH, MLSTM_HEADS), 1.0),
        'state_ssm_re': nrm(5, (L, DEC_BATCH, G, P), 0.1),
        'state_ssm_im': nrm(6, (L, DEC_BATCH, G, P), 0.1),
        'p_prompt': nrm(7, (L, BATCH, SEQ, PLE_DIM), 1.0),
        'p_sample': nrm(8, (L, DEC_BATCH, DEC_SEQ, PLE_DIM), 1.0),
        'norm_mix': 1.0 + nrm(9, (L, D_MODEL), 0.02),
        'w_in': nrm(10, (L, D_MODEL, IN_COLS), D_MODEL ** -0.5),
        'b_igate': nrm(11, (L, MLSTM_HEADS), 0.1),
        'b_fgate': jnp.linspace(3.0, 6.0, MLSTM_HEADS, dtype=f32)[None] + nrm(12, (L, MLSTM_HEADS), 0.1),
        'mlstm_norm': 1.0 + nrm(13, (L, MLSTM_WIDTH), 0.02),
        'ssm_A_re': -0.5 + nrm(14, (L, G, P), 0.01),
        'ssm_A_im': math.pi * jnp.arange(P, dtype=f32) + nrm(15, (L, G, P), 0.01),
        'ssm_B_re': nrm(16, (L, G, P, SSM_GROUP), (2 * SSM_GROUP) ** -0.5),
        'ssm_B_im': nrm(17, (L, G, P, SSM_GROUP), (2 * SSM_GROUP) ** -0.5),
        'ssm_C_re': nrm(18, (L, G, SSM_GROUP, P), P ** -0.5),
        'ssm_C_im': nrm(19, (L, G, SSM_GROUP, P), P ** -0.5),
        'ssm_D': nrm(20, (L, G, SSM_GROUP), 1.0),
        'ssm_log_dt': jax.random.uniform(ks[21], (L, G), f32, math.log(1e-3), math.log(1e-1)),
        'w_glu': nrm(22, (L, SSM_WIDTH, SSM_WIDTH), SSM_WIDTH ** -0.5),
        'b_glu': nrm(23, (L, SSM_WIDTH), 0.02),
        'w_out': nrm(24, (L, MIX_WIDTH, D_MODEL), MIX_WIDTH ** -0.5),
        'norm_ffn': 1.0 + nrm(25, (L, D_MODEL), 0.02),
        'peer_w_q': nrm(26, (L, D_MODEL, PEER_HEADS * PEER_KEY_DIM), D_MODEL ** -0.5),
        'peer_keys': nrm(27, (L, PEER_HEADS, 2, PEER_KEYS, PEER_KEY_DIM // 2), (PEER_KEY_DIM // 2) ** -0.5),
        'peer_u': nrm(28, (L, PEER_EXPERTS, D_MODEL), D_MODEL ** -0.5),
        'peer_v': nrm(29, (L, PEER_EXPERTS, D_MODEL), PEER_HEADS ** -0.5),
        'norm_ple': 1.0 + nrm(30, (L, D_MODEL), 0.02),
        'w_ple_gate': nrm(31, (L, D_MODEL, D_MODEL), D_MODEL ** -0.5),
        'w_ple_proj': nrm(32, (L, PLE_DIM, D_MODEL), PLE_DIM ** -0.5),
        'norm_final': 1.0 + nrm(33, (D_MODEL,), 0.02),
    }

def reference(x_prompt, x_sample, state_mlstm_C, state_mlstm_n, state_mlstm_m, state_ssm_re, state_ssm_im,
              p_prompt, p_sample, norm_mix, w_in, b_igate, b_fgate, mlstm_norm, ssm_A_re, ssm_A_im,
              ssm_B_re, ssm_B_im, ssm_C_re, ssm_C_im, ssm_D, ssm_log_dt, w_glu, b_glu, w_out, norm_ffn,
              peer_w_q, peer_keys, peer_u, peer_v, norm_ple, w_ple_gate, w_ple_proj, norm_final):
    f32 = jnp.float32
    H, dh, G, P = MLSTM_HEADS, MLSTM_HEAD_DIM, SSM_GROUPS, SSM_STATE
    bp = x_prompt.shape[0]
    hp, hs = x_prompt, x_sample
    outs_p = [[] for _ in range(5)]
    outs_s = [[] for _ in range(5)]
    for l in range(DEPTH):
        prm = {
            'norm_mix': norm_mix[l], 'w_in': w_in[l], 'b_igate': b_igate[l], 'b_fgate': b_fgate[l],
            'mlstm_norm': mlstm_norm[l], 'ssm_A_re': ssm_A_re[l], 'ssm_A_im': ssm_A_im[l],
            'ssm_B_re': ssm_B_re[l], 'ssm_B_im': ssm_B_im[l], 'ssm_C_re': ssm_C_re[l], 'ssm_C_im': ssm_C_im[l],
            'ssm_D': ssm_D[l], 'ssm_log_dt': ssm_log_dt[l], 'w_glu': w_glu[l], 'b_glu': b_glu[l],
            'w_out': w_out[l], 'norm_ffn': norm_ffn[l], 'peer_w_q': peer_w_q[l], 'peer_keys': peer_keys[l],
            'peer_u': peer_u[l], 'peer_v': peer_v[l], 'norm_ple': norm_ple[l], 'w_ple_gate': w_ple_gate[l],
            'w_ple_proj': w_ple_proj[l],
        }
        hp, st_p = hybrid_layer(hp, p_prompt[l],
                                jnp.zeros((bp, H, dh, dh), f32), jnp.zeros((bp, H, dh), f32),
                                jnp.zeros((bp, H), f32), jnp.zeros((bp, G, P), f32),
                                jnp.zeros((bp, G, P), f32), prm)
        hs, st_s = hybrid_layer(hs, p_sample[l], state_mlstm_C[l], state_mlstm_n[l], state_mlstm_m[l],
                                state_ssm_re[l], state_ssm_im[l], prm)
        for j in range(5):
            outs_p[j].append(st_p[j])
            outs_s[j].append(st_s[j])
    y_prompt = rmsnorm(hp, norm_final)
    y_sample = rmsnorm(hs, norm_final)
    new_C_p, new_n_p, new_m_p, new_re_p, new_im_p = (jnp.stack(t) for t in outs_p)
    new_C_s, new_n_s, new_m_s, new_re_s, new_im_s = (jnp.stack(t) for t in outs_s)
    return (y_prompt, y_sample, new_C_p, new_n_p, new_m_p, new_re_p, new_im_p,
            new_C_s, new_n_s, new_m_s, new_re_s, new_im_s)


_drawn_inputs = setup_inputs


def setup_inputs(seed=0):
    import zlib

    import numpy as np

    out = dict(_drawn_inputs(seed))
    spreads = {}
    factors = {'mlstm_norm': 4.052,
     'ssm_A_re': 74.869,
     'b_glu': 35.349,
     'norm_ple': 198.537,
     'norm_final': 22.821,
     'ssm_C_re': 3.368,
     'ssm_C_im': 3.266,
     'norm_ffn': 3.743}
    for name, (base, spread) in spreads.items():
        noise = np.random.default_rng([zlib.crc32(name.encode()), seed]).standard_normal(out[name].shape)
        drawn = base * np.exp(spread * noise) if base else spread * noise
        out[name] = __import__('jax').numpy.asarray(drawn.astype(out[name].dtype))
    for name, factor in factors.items():
        out[name] = (out[name] * factor).astype(out[name].dtype)
    return out
```

```python
from contextlib import ExitStack
import math

import concourse.bass as bass
from concourse import mybir

F32 = mybir.dt.float32
U32 = mybir.dt.uint32
ALU = mybir.AluOpType
ACT = mybir.ActivationFunctionType
AX = mybir.AxisListType

P = 128
D = 2048
KD = D // P
TP, NB, NS = 256, 8, 4
TS = NB * NS
T = TP + TS
TOK = [(0, 128), (128, 128), (256, TS)]
H, DH = 4, 256
MW = H * DH
G, SP_, GC = 64, 64, 16
NJ = G * SP_ // P
CH = 16
NCH = TP // CH
PH, PK, TK = 8, 128, 16
PLE = 256
EPS = 1e-6
WB = 256
COLS_IN = 4 * MW + 2 * H + G * GC
NEG = -1.0e38

O_RE, O_IM = 0, NJ * T
O_Z = 2 * NJ * T
O_U = O_Z + 32 * T
O_MIX = O_U + 8 * T
O_EX = O_MIX + 16 * T
WORK = P * T
assert O_EX + 8 * T == WORK

STREAM, _n = {}, 0
for _name, _blocks, _kt in (("u", 4, KD), ("z", 16, KD), ("glu", 4, 8), ("out", 8, KD), ("wq", 4, KD)):
    STREAM[_name] = (_n, _blocks, _kt)
    _n += _blocks


class Own:

    def __init__(self, eng, chain):
        self.eng, self.chain, self.n, self.open, self.per = eng, chain, {}, {}, None

    def do(self, ins, sem=None):
        s = self.chain if sem is None else sem
        ins.then_inc(s, 1)
        self.n[s.name] = self.n.get(s.name, 0) + 1
        self.open[s.name] = s

    def settle(self):
        for name, s in self.open.items():
            n = self.n[name]
            if self.per is not None:
                i, per = self.per
                self.eng.wait_ge(s, i * per.get(name, 0) + n)
            else:
                self.eng.wait_ge(s, n)
        self.open = {}

    def loop(self, i, per):
        self.per, self.at = (i, per), dict(self.n)

    def leave(self, trips):
        per = self.per[1]
        for name, n in self.n.items():
            assert n - self.at.get(name, 0) == per.get(name, 0), (name, n - self.at.get(name, 0))
            self.n[name] = self.at.get(name, 0) + trips * per.get(name, 0)
        self.per = None


def build(nc, ins, outs):
    ctx = ExitStack()
    with ctx:
        def sb(name, shape, dt=F32):
            return ctx.enter_context(nc.sbuf_tensor(name, shape, dt))

        sems = {}

        def sem(name):
            if name not in sems:
                sems[name] = ctx.enter_context(nc.semaphore(name))
            return sems[name]

        hT = sb("hT", [P, KD, T])
        nT = sb("nT", [P, KD, T])
        ring = sb("ring", [P, 2, 4096])
        work = sb("work", [P, WORK])
        ident = sb("ident", [P, P])
        ones = sb("ones", [P, P])
        iota = sb("iota", [P, P])
        gv = sb("gv", [P, 88])
        rstd = sb("rstd", [P, T])
        rs = sb("rs", [P, T])
        gel = sb("gel", [P, 2, T])
        ex3 = sb("ex3", [P, 3, T])
        tri = ex3[:, 0, 0:P]
        trs = ex3[0:TS, 0, P:P + TS]
        cols = ex3[:, 0, 160:192]
        bmask = ex3[0:TS, 0, 192:192 + NB]
        par = ex3[:, 0, 200:208]
        gb8 = ex3[0:8, 0, 208:209]
        rows8 = ex3[0:8, 1, :]
        ps = [ctx.enter_context(nc.psum_tensor(f"ps{i}", [P, 512], F32)) for i in range(8)]

        def wk(off, *shape):
            n = math.prod(shape)
            ap = work[:, off:off + n]
            if len(shape) == 2:
                ap = ap.rearrange("p (a b) -> p a b", b=shape[1])
            elif len(shape) == 3:
                ap = ap.rearrange("p (a b c) -> p a b c", b=shape[1], c=shape[2])
            return ap

        def bc(ap, n):
            return ap.unsqueeze(len(ap.shape)).to_broadcast([*ap.shape, n])

        st = [wk(O_RE, NJ, T), wk(O_IM, NJ, T)]
        zT = wk(O_Z, 32, T)
        uT = wk(O_U, 8, T)
        mix = wk(O_MIX, 16, T)
        xin = wk(O_Z, 3, D)
        Bn = [wk(0, NJ, GC), wk(512, NJ, GC)]
        Bbd = [wk(1024, NJ, 2, GC), wk(2048, NJ, 2, GC)]
        Cn = [wk(3072, 8, SP_), wk(3584, 8, SP_)]
        Cbd = [wk(4096, 8, 2, SP_), wk(5120, 8, 2, SP_)]
        tB = [wk(6144 + 512 * i, NJ, GC) for i in range(4)]
        r32 = wk(8192, 16, P)
        s0r = wk(10240, 2, 2, P)
        vrow = wk(10752, 1, P)[:, 0, :]
        dtr = wk(10880, 1, 2)[:, 0, :]
        gw = wk(11008, KD, 8)
        BT = [wk(O_MIX, 8, P), wk(O_MIX + 1024, 8, P)]
        CT = [wk(O_MIX + 2048, 8, P), wk(O_MIX + 3072, 8, P)]
        abT = wk(O_MIX + 4096, 4, NJ)
        a16 = wk(O_MIX + 4224, 4, NJ)
        s0T = gel[:, :, 0:NB * NJ]
        tS = [wk(O_EX + 512 * i, NJ, 16) for i in range(4)]

        ds = bass.ds
        AB = ["ssm_A_re", "ssm_A_im"]

        send = wk(O_EX, 2, 1 + NB, NJ)
        sout = wk(O_EX + 576, 6, P)

        def pe_norm(pe, n):
            for q in range(4):
                pe.wait_ge(sem("sq_done"), 4 * n + q + 1)
                for k in range(4 * q, 4 * q + 4):
                    m = pe.matmul(ps[7][:, 0:T], ones[:], nT[:, k, :], start=(k == 0), stop=(k == KD - 1))
            m.then_inc(sem("ss_done"), 1)

        def pe_linear(pe, name, rhs):
            base, nb, kt = STREAM[name]

            def blk(i, s, first):
                pe.wait_ge(sem(f"w_in{s}"), 16 * (base // 2 + 1) + i * 16)
                for c in range(2):
                    if not first:
                        pe.wait_ge(sem("mm_freed"), i * 4 + (2 * base + 2 * s + c - 3))
                    for k in range(kt):
                        m = pe.matmul(ps[2 * s + c][:, 0:T],
                                      ring[:, s, k * WB + c * P:k * WB + (c + 1) * P], rhs[:, k, :],
                                      start=(k == 0), stop=(k == kt - 1))
                    m.then_inc(sem("mm_done"), 1)

            i0 = 0
            if base == 0:
                blk(0, 0, True)
                blk(0, 1, True)
                i0 = 1
            with pe.Fori(i0, nb // 2) as i:
                blk(i, 0, False)
                blk(i, 1, False)

        def act_norm(act, n):
            for q in range(4):
                o_act.do(act.activation(nT[:, 4 * q:4 * q + 4, :], hT[:, 4 * q:4 * q + 4, :], ACT.Square),
                         sem("sq_done"))
            act.wait_ge(sem("ms_ready"), n + 1)
            o_act.do(act.activation(rstd[:], rs[:], ACT.Sqrt), sem("sd_ready"))

        def dve_norm(v, o, n):
            v.wait_ge(sem("ss_done"), n + 1)
            o.do(v.tensor_scalar(rs[:], ps[7][:, 0:T], 1.0 / D, EPS, ALU.mult, ALU.add), sem("ms_ready"))
            v.wait_ge(sem("sd_ready"), n + 1)
            newton(v, o, rstd[:], rs[:], gel[:, 0, :])
            for k in range(KD):
                o.do(v.scalar_tensor_tensor(nT[:, k, :], hT[:, k, :], gv[:, 16 * n + k:16 * n + k + 1], rstd[:],
                                            ALU.mult, ALU.mult), sem("n_ready"))

        def newton(v, o, r, x, t):
            o.settle()
            o.do(v.reciprocal(r, r))
            o.settle()
            o.do(v.tensor_tensor(t, r, r, ALU.mult))
            o.settle()
            o.do(v.scalar_tensor_tensor(t, t, -0.5, x, ALU.mult, ALU.mult))
            o.settle()
            o.do(v.scalar_tensor_tensor(r, t, 1.5, r, ALU.add, ALU.mult))
            o.settle()

        o_act = Own(None, sem("act_own"))

        def dve_s5_setup(v, o):
            R = [r32[0:NJ, q, :] for q in range(16)]
            Ar, Ai, dre, th, mag, sn, sh, k, c, t, are, aim, fre, fim = R[:14]
            v.wait_ge(sem("s5_in"), 16 * 9)
            v.wait_ge(sem("dt_ready"), 1)
            for src, dst in ((Ar, dre), (Ai, th)):
                for g in range(2):
                    o.do(v.tensor_scalar(dst[:, g * SP_:(g + 1) * SP_], src[:, g * SP_:(g + 1) * SP_],
                                         dtr[0:NJ, g:g + 1], None, ALU.mult))
            o.settle()
            MAGIC = 1.5 * 2.0 ** 23
            o.do(v.tensor_scalar(k, th, 1.0 / (2 * math.pi), MAGIC, ALU.mult, ALU.add))
            o.settle()
            o.do(v.tensor_scalar(k, k, MAGIC, None, ALU.subtract))
            c1 = 6.28125
            c2 = 0.0019350051879882812
            c3 = 2 * math.pi - c1 - c2
            for cc in (c1, c2, c3):
                o.settle()
                o.do(v.scalar_tensor_tensor(th, k, -cc, th, ALU.mult, ALU.add))
            o.settle()
            o.do(v.tensor_scalar(th, th, 3.1415925, -3.1415925, ALU.min, ALU.max), sem("theta_ready"))
            o.do(v.tensor_reduce(par[:, 4:5], par[:, 0:4], AX.X, ALU.max))
            o.settle()
            o.do(v.tensor_scalar(par[:, 5:6], par[:, 4:5], -1.0, 1.0, ALU.mult, ALU.add))
            o.do(v.tensor_scalar(par[:, 6:7], par[:, 4:5], -1.0, None, ALU.mult))
            o.settle()
            o.do(v.tensor_scalar(par[:, 7:8], par[:, 5:6], -1.0, None, ALU.mult))
            o.settle()
            for q in range(2):
                for g in range(2):
                    o.do(v.tensor_scalar(Cbd[q][:, :, g, :], Cn[q], par[:, 4 + g + 2 * q:5 + g + 2 * q], None, ALU.mult))
                o.do(v.memset(Bbd[q], 0.0))
            v.wait_ge(sem("trig_ready"), 1)
            o.do(v.tensor_tensor(c, sh, sh, ALU.mult))
            o.do(v.tensor_tensor(aim, mag, sn, ALU.mult))
            o.do(v.tensor_tensor(fre, Ar, Ar, ALU.mult))
            o.do(v.tensor_tensor(fim, Ai, Ai, ALU.mult))
            o.settle()
            o.do(v.tensor_scalar(c, c, -2.0, 1.0, ALU.mult, ALU.add))
            o.do(v.tensor_tensor(t, fre, fim, ALU.add))
            o.settle()
            o.do(v.tensor_tensor(are, mag, c, ALU.mult))
            o.do(v.reciprocal(t, t))
            o.settle()
            o.do(v.tensor_scalar(k, are, 1.0, None, ALU.subtract))
            o.do(v.tensor_tensor(fre, aim, Ai, ALU.mult))
            o.do(v.tensor_tensor(fim, aim, Ar, ALU.mult))
            o.settle()
            o.do(v.tensor_tensor(c, k, Ar, ALU.mult))
            o.do(v.tensor_tensor(k, k, Ai, ALU.mult))
            o.settle()
            o.do(v.tensor_tensor(fre, fre, c, ALU.add))
            o.do(v.tensor_tensor(fim, fim, k, ALU.subtract))
            o.settle()
            o.do(v.tensor_tensor(fre, fre, t, ALU.mult))
            o.do(v.tensor_tensor(fim, fim, t, ALU.mult), sem("abf_rows"))
            v.wait_ge(sem("gate_done"), 1)
            v.wait_ge(sem("vec_in"), 16 * 9)
            o.do(v.tensor_scalar(rows8, ps[5][0:8, 0:T], gb8[:, 0:1], None, ALU.add), sem("gate_copied"))
            v.wait_ge(sem("abf_done"), 1)
            o.do(v.tensor_copy(abT, ps[4][:, 0:4 * NJ].rearrange("p (a b) -> p a b", a=4)), sem("abf_copied"))
            o.settle()
            fr, fi = bc(abT[:, 2, :], GC), bc(abT[:, 3, :], GC)
            o.do(v.tensor_tensor(tB[0], Bn[0], fr, ALU.mult))
            o.do(v.tensor_tensor(tB[1], Bn[1], fi, ALU.mult))
            o.do(v.tensor_tensor(tB[2], Bn[1], fr, ALU.mult))
            o.do(v.tensor_tensor(tB[3], Bn[0], fi, ALU.mult))
            o.settle()
            for q, op in ((0, ALU.subtract), (1, ALU.add)):
                for g in range(2):
                    sl = slice(g * SP_, (g + 1) * SP_)
                    o.do(v.tensor_tensor(Bbd[q][sl, :, g, :], tB[2 * q][sl], tB[2 * q + 1][sl], op))
            o.settle()
            o.do(v.tensor_copy(par[:, 0:1], par[:, 0:1]), sem("bd_ready"))
            o.do(v.tensor_copy(par[:, 1:2], par[:, 1:2]), sem("bd_ready"))

        def cmul_add(v, o, dst, a, src, tmp):
            o.do(v.tensor_tensor(tmp[0], a[0], src[0], ALU.mult))
            o.do(v.tensor_tensor(tmp[1], a[1], src[1], ALU.mult))
            o.do(v.tensor_tensor(tmp[2], a[0], src[1], ALU.mult))
            o.do(v.tensor_tensor(tmp[3], a[1], src[0], ALU.mult))
            o.settle()
            o.do(v.tensor_tensor(dst[0], dst[0], tmp[0], ALU.add))
            o.do(v.tensor_tensor(dst[1], dst[1], tmp[2], ALU.add))
            o.settle()
            o.do(v.tensor_tensor(dst[0], dst[0], tmp[1], ALU.subtract))
            o.do(v.tensor_tensor(dst[1], dst[1], tmp[3], ALU.add))
            o.settle()

        def cmul(v, o, dst, a, src, tmp):
            o.do(v.tensor_tensor(tmp[0], a[0], src[0], ALU.mult))
            o.do(v.tensor_tensor(tmp[1], a[1], src[1], ALU.mult))
            o.do(v.tensor_tensor(tmp[2], a[0], src[1], ALU.mult))
            o.do(v.tensor_tensor(tmp[3], a[1], src[0], ALU.mult))
            o.settle()
            o.do(v.tensor_tensor(dst[0], tmp[0], tmp[1], ALU.subtract))
            o.do(v.tensor_tensor(dst[1], tmp[2], tmp[3], ALU.add))
            o.settle()

        CMUL = 8

        def dve_s5_scan(v, o):
            o.settle()
            v.wait_ge(sem("s0_copied"), 1)
            a = [abT[:, 0, :], abT[:, 1, :]]
            pw = [a16[:, 0, :], a16[:, 1, :]]
            g2 = [a16[:, 2, :], a16[:, 3, :]]
            ts = [t[:, :, 0] for t in tS]
            cmul(v, o, pw, a, a, ts)
            for _ in range(3):
                cmul(v, o, pw, pw, pw, ts)
            smp = [s[:, :, TP:T].rearrange("p j (b s) -> p s j b", s=NS) for s in st]
            s0 = [s0T[:, q, :].rearrange("p (b j) -> p j b", j=NJ) for q in range(2)]
            aB = [bc(x, NB) for x in a]
            for s in range(NS):
                src = s0 if s == 0 else [x[:, s - 1] for x in smp]
                cmul_add(v, o, [x[:, s] for x in smp], aB, src, [t[:, :, 0:NB] for t in tS])
            chk = [s[:, :, 0:TP].rearrange("p j (k t) -> p t j k", t=CH) for s in st]
            aC = [bc(x, NCH).unsqueeze(1) for x in a]
            tC = [t.unsqueeze(1) for t in tS]
            with v.Fori(0, CH - 1) as i:
                o.loop(i, {"dve_own": CMUL})
                cmul_add(v, o, [x[:, ds(i + 1, 1)] for x in chk], aC, [x[:, ds(i, 1)] for x in chk], tC)
                o.leave(CH - 1)
            end = [s[:, :, CH - 1:TP:CH] for s in st]
            with v.Fori(0, NCH - 1) as i:
                o.loop(i, {"dve_own": CMUL})
                cmul_add(v, o, [x[:, :, ds(i + 1, 1)] for x in end], [x.unsqueeze(2) for x in pw],
                         [x[:, :, ds(i, 1)] for x in end], [t[:, :, 0:1] for t in tS])
                o.leave(NCH - 1)
            for q in range(2):
                o.do(v.tensor_copy(g2[q], a[q]))
            o.settle()
            n = NCH - 1
            prev = [x[:, :, 0:n].unsqueeze(1) for x in end]
            with v.Fori(0, CH - 1) as i:
                o.loop(i, {"dve_own": CMUL + 6})
                cmul_add(v, o, [x[:, ds(i, 1), :, 1:NCH] for x in chk], [bc(x, n).unsqueeze(1) for x in g2], prev,
                         [t[:, :, 0:n].unsqueeze(1) for t in tS])
                cmul(v, o, g2, g2, a, ts)
                o.leave(CH - 1)
            for q in range(2):
                o.do(v.tensor_copy(send[:, q, 0, :], st[q][:, :, TP - 1]))
                o.do(v.tensor_copy(send[:, q, 1:1 + NB, :],
                                   st[q][:, :, TP + NS - 1:T:NS].rearrange("p j b -> p b j")))
            o.settle()
            o.do(v.tensor_copy(g2[0], g2[0]), sem("s5_ready"))
            o.do(v.tensor_copy(g2[1], g2[1]), sem("send_ready"))

        CR = [wk(4096 * i, NB, 2, DH) for i in range(2)]
        ktok = wk(8192, 3, MW)
        vtok = wk(11264, 3, MW)
        kwm = wk(14336, NB, DH)
        S_ = [wk(16384 + 416 * i, 1, 416)[:, 0, :] for i in range(2)]
        n0r = wk(17216, 1, P)[:, 0, :]
        n0T = wk(17344, NB, H, 2)
        ncol = wk(17408, 9, H, 2)
        nrow = wk(17480, 1, P)[:, 0, :]
        m0b = wk(17608, NB, H)
        qn = wk(17640, 4, 2, TS)
        w0 = wk(17896, H, TS)
        ntmp = wk(18024, NB, 2)
        exf = wk(O_EX, 8, T)
        rI, rF = exf[:, 0:4, :], exf[:, 4:8, :]
        r2, r3 = uT[:, 0:4, :], uT[:, 4:8, :]
        r4, r5, r6, r7 = (nT[:, 4 * i:4 * i + 4, :] for i in range(4))
        hb, hsq = r4[:, 0:2, :], r4[:, 2:4, :]
        pC = zT[:, 0:8, 0:DH]
        mrow = rows8

        def flat(x):
            return x.rearrange("p a t -> p (a t)")

        def smp4(x):
            return x[:, :, TP:T].rearrange("p h (b s) -> p h b s", s=NS)

        def sp_mlstm(sp):
            sp.wait_ge(sem("sout_ready"), 1)
            for q, (a, b) in enumerate(((5, 10), (6, 11))):
                sp.dma_start(outs[a][0, 0].rearrange("(j g) p -> j (g p)", g=2), sout[0:NJ, q, :]).then_inc(
                    sem("s5_stored"), 16)
                sp.dma_start(outs[b][0].rearrange("b (j g) p -> (b j) (g p)", g=2).rearrange("(t r) q -> r t q", t=2),
                             sout[:, 2 + 2 * q:4 + 2 * q, :]).then_inc(sem("s5_stored"), 16)
            sp.wait_ge(sem("y_sum"), 8)
            mi = sem("ml_in")
            sp.dma_start(n0r[0:64, :], ins["state_mlstm_n"][0].rearrange("b h (c p) -> (b h c) p", p=P)).then_inc(mi, 16)
            sp.dma_start(m0b, ins["state_mlstm_m"][0].partition_broadcast(P)).then_inc(mi, 16)

            def c_load(h):
                if h >= 2:
                    sp.wait_ge(sem(f"c_out{h % 2}"), 16 * NB * (h // 2))
                for b in range(NB):
                    sp.dma_start(CR[h % 2][:, b], ins["state_mlstm_C"][0, b, h].rearrange("(c p) e -> p c e", p=P)
                                 ).then_inc(sem(f"c_in{h % 2}"), 16)

            def c_store(h):
                sp.wait_ge(sem("cn_read"), NB * (h + 1))
                for b in range(NB):
                    sp.dma_start(outs[7][0, b, h].rearrange("(c p) e -> p c e", p=P), CR[h % 2][:, b]).then_inc(
                        sem(f"c_out{h % 2}"), 16)

            c_load(0)
            c_load(1)
            for h in range(H):
                c_store(h)
                if h + 2 < H:
                    c_load(h + 2)
            for h in range(H):
                sp.wait_ge(sem("pc_copied"), h + 1)
                sp.dma_start(outs[2][0, 0, h].rearrange("(c p) e -> p c e", p=P), pC[:, 2 * h:2 * h + 2, :]).then_inc(
                    sem("ml_stored"), 16)
            sp.wait_ge(sem("nrow_copied"), 1)
            sp.dma_start(outs[3][0, 0].rearrange("h (c p) -> (h c) p", p=P), nrow[0:8, :]).then_inc(sem("ml_stored"), 16)
            sp.dma_start(outs[8][0].rearrange("b h (c p) -> (b h c) p", p=P), nrow[8:72, :]).then_inc(sem("ml_stored"), 16)
            sp.wait_ge(sem("mrow_ready"), 1)
            sp.dma_start(outs[4][0], mrow[0:1, 0:4]).then_inc(sem("ml_stored"), 16)
            sp.dma_start(outs[9].rearrange("a b h -> a (b h)"), mrow[0:1, 4:36]).then_inc(sem("ml_stored"), 16)
            sp.wait_ge(sem("s5_stored"), 64)
            sp.wait_ge(sem("ml_stored"), 16 * 8)
            for s in range(2):
                sp.wait_ge(sem(f"c_out{s}"), 16 * NB * 2)

        def pe_mlstm(pe):
            for r in range(8):
                if r == 0:
                    pe.wait_ge(sem("sout_ready"), 1)
                if r >= 4:
                    pe.wait_ge(sem("bc_copied"), r - 3)
                pe.matmul(ps[4 + r % 4][:, 0:T], ident[0:8, r:r + 1].to_broadcast([8, P]), rows8,
                          start=True, stop=True).then_inc(sem("bc_done"), 1)
            pe.wait_ge(sem("ml_in"), 32)
            pe.wait_ge(sem("bc_copied"), 5)
            pe.transpose(ps[4][:, 0:64], n0r[0:64, :], ident[0:64, 0:64]).then_inc(sem("n0_done"), 1)
            pe.wait_ge(sem("mm_freed"), 2 * (STREAM["glu"][0] + 4))
            for g in range(12):
                arr, rest = divmod(g, 6)
                i, half = divmod(rest, 2)
                t0, n = TOK[i]
                if g >= 4:
                    pe.wait_ge(sem("tok_copied"), g - 3)
                for j in range(4):
                    m = pe.transpose(ps[g % 4][0:n, j * P:(j + 1) * P],
                                     zT[:, 8 + 8 * arr + 4 * half + j, t0:t0 + n], ident[:])
                m.then_inc(sem("tok_done"), 1)
            pe.wait_ge(sem("wk_ready"), 1)
            pe.wait_ge(sem("bc_copied"), 8)
            for q, row in enumerate((rI, r7)):
                for i, (t0, n) in enumerate(TOK):
                    for h in range(H):
                        c = 12 * q + 4 * i + h
                        m = pe.matmul(ps[5][0:n, c:c + 1], row[0:1, h, t0:t0 + n], ones[0:1, 0:1], start=True, stop=True)
            m.then_inc(sem("col_done"), 1)
            pe.wait_ge(sem("col_copied"), 1)
            pe.wait_ge(sem("n0_copied"), 1)
            pe.wait_ge(sem("tok_copied"), 12)
            for h in range(H):
                qs = [zT[:, 2 * h + c, :] for c in range(2)]
                ks = [zT[:, 8 + 2 * h + c, :] for c in range(2)]
                if h >= 1:
                    pe.wait_ge(sem("sw_ready"), h)
                for c in range(2):
                    pe.matmul(ps[0][:, 0:256], ks[c][:, 0:128], qs[c][:, 0:256], start=(c == 0), stop=(c == 1))
                for c in range(2):
                    pe.matmul(ps[0][:, 256:384], ks[c][:, 128:256], qs[c][:, 128:256], start=(c == 0), stop=(c == 1))
                for c in range(2):
                    m = pe.matmul(ps[0][0:TS, 384:384 + TS], ks[c][:, TP:T], qs[c][:, TP:T], start=(c == 0), stop=(c == 1))
                m.then_inc(sem("sc_done"), 1)
                S, C, hs = S_[h % 2], CR[h % 2], h % 2
                pe.wait_ge(sem("sw_ready"), h + 1)
                pe.wait_ge(sem("qn_ready"), h + 1)
                pe.wait_ge(sem(f"c_in{h % 2}"), 16 * NB * (h // 2 + 1))
                if h >= 1:
                    pe.wait_ge(sem("hms_ready"), h)
                    pe.wait_ge(sem("hb_ready"), 2 * h)

                def both(bank, lhs, before):
                    pe.matmul(bank[:, 0:128], lhs(0), S[:, 0:128], start=True, stop=True)
                    pe.matmul(bank[:, 128:256], lhs(0), S[:, 128:256], start=True, stop=False)
                    pe.matmul(bank[:, 128:256], lhs(1), S[:, 256:384], start=False, stop=True)
                    before(bank)
                    return pe.matmul(bank[:, TP:T], lhs(2), S[0:TS, 384:416], start=False, stop=True)

                def den_before(bank):
                    for c in range(2):
                        pe.matmul(bank[:, TP:T], ones[:], qn[:, 2 + c, hs, :], start=(c == 0), stop=False)

                both(ps[1], lambda i: ones[0:TOK[i][1], :], den_before).then_inc(sem("den_done"), 1)
                for e in range(2):
                    c0 = h * DH + e * P

                    def num_before(bank):
                        for b in range(NB):
                            for c in range(2):
                                pe.matmul(bank[:, TP + NS * b:TP + NS * (b + 1)], C[:, b, c, e * P:(e + 1) * P],
                                          qn[:, c, hs, NS * b:NS * (b + 1)], start=(b == 0 and c == 0), stop=False)

                    both(ps[2 + e], lambda i: vtok[0:TOK[i][1], i, c0:c0 + P], num_before).then_inc(sem("num_done"), 1)
                pe.wait_ge(sem("kw_ready"), 1)
                if h >= 1:
                    pe.wait_ge(sem("pc_copied"), h)
                    pe.wait_ge(sem("nc_read"), h)
                for c in range(2):
                    for i in range(2):
                        pe.matmul(ps[4][:, c * DH:(c + 1) * DH], ktok[:, i, h * DH + c * P:h * DH + (c + 1) * P],
                                  vtok[:, i, h * DH:(h + 1) * DH], start=(i == 0), stop=(i == 1))
                for c in range(2):
                    for i in range(2):
                        m = pe.matmul(ps[5][:, c:c + 1], ktok[:, i, h * DH + c * P:h * DH + (c + 1) * P],
                                      ones[:, 0:1], start=(i == 0), stop=(i == 1))
                m.then_inc(sem("pc_done"), 1)
                pe.wait_ge(sem("kwm_ready"), h + 1)
                for b in range(NB):
                    at = NB * h + b
                    if at >= 2:
                        pe.wait_ge(sem("cn_read"), at - 1)
                    bank = ps[6 + at % 2]
                    for c in range(2):
                        pe.matmul(bank[:, c * DH:(c + 1) * DH], kwm[0:TS, b, c * P:(c + 1) * P],
                                  vtok[0:TS, 2, h * DH:(h + 1) * DH], start=True, stop=True)
                    for c in range(2):
                        m = pe.matmul(ps[5][:, 2 + 2 * b + c:3 + 2 * b + c], kwm[0:TS, b, c * P:(c + 1) * P],
                                      ones[0:TS, 0:1], start=True, stop=True)
                    m.then_inc(sem("cn_done"), 1)
                pe.wait_ge(sem("hsq_done"), h + 1)
                for e in range(2):
                    m = pe.matmul(ps[1][:, 0:T], ones[:], hsq[:, e, :], start=(e == 0), stop=(e == 1))
                m.then_inc(sem("hss_done"), 1)
            pe.wait_ge(sem("nc_read"), H)
            pe.transpose(ps[5][0:72, 0:P], ncol.rearrange("p a b c -> p (a b c)"), ident[:]).then_inc(sem("nrow_done"), 1)

        def act_mlstm(act, o):
            act.wait_ge(sem("s5_stored"), 64)
            for r in range(8):
                act.wait_ge(sem("bc_done"), r + 1)
                o.do(act.copy(exf[:, r, :], ps[4 + r % 4][:, 0:T]), sem("bc_copied"))
            o.settle()
            act.wait_ge(sem("glu_ready"), 8)
            o.do(act.activation(r2, rF, ACT.Abs))
            o.settle()
            o.do(act.activation(r2, r2, ACT.Exp, scale=-1.0))
            o.settle()
            o.do(act.activation(r2, r2, ACT.Ln, bias=1.0), sem("ln_ready"))
            act.wait_ge(sem("n0_done"), 1)
            o.do(act.copy(n0T.rearrange("p a b c -> p (a b c)"), ps[4][:, 0:64]), sem("n0_copied"))
            for g in range(12):
                arr, rest = divmod(g, 6)
                i, half = divmod(rest, 2)
                n = TOK[i][1]
                act.wait_ge(sem("tok_done"), g + 1)
                dst = [ktok, vtok][arr]
                o.do(act.copy(dst[0:n, i, 512 * half:512 * half + 512], ps[g % 4][0:n, 0:512]), sem("tok_copied"))
            act.wait_ge(sem("m_ready"), 1)
            o.settle()
            o.do(act.activation(r2, r6, ACT.Exp, scale=-1.0))
            o.do(act.activation(w0, w0, ACT.Exp))
            o.do(act.activation(r7, r7, ACT.Exp), sem("wk_ready"))
            for h in range(H):
                S = S_[h % 2]
                act.wait_ge(sem("sarg_ready"), h + 1)
                o.do(act.activation(S[:, 0:384], S[:, 0:384], ACT.Exp, scale=-1.0))
                o.do(act.activation(S[0:TS, 384:416], S[0:TS, 384:416], ACT.Exp, scale=-1.0), sem("sexp_ready"))
                act.wait_ge(sem("pc_done"), h + 1)
                o.do(act.copy(pC[:, 2 * h:2 * h + 2, :], ps[4][:, 0:512].rearrange("p (a b) -> p a b", a=2)),
                     sem("pc_copied"))
                act.wait_ge(sem("hb_ready"), 2 * h + 2)
                if h >= 1:
                    act.wait_ge(sem("hss_done"), h)
                o.do(act.activation(hsq, hb, ACT.Square), sem("hsq_done"))
                act.wait_ge(sem("hms_ready"), h + 1)
                o.do(act.activation(rstd[:], rs[:], ACT.Sqrt), sem("hsd_ready"))
            act.wait_ge(sem("nrow_done"), 1)
            o.do(act.copy(nrow[0:72, :], ps[5][0:72, 0:P]), sem("nrow_copied"))

        def dve_mlstm(v, o):
            v.wait_ge(sem("mm_done"), 2 * (STREAM["z"][0] + STREAM["z"][1]))
            v.wait_ge(sem("ln_ready"), 1)
            v.wait_ge(sem("ml_in"), 32)
            o.settle()
            o.do(v.memset(r7, 1.0))
            o.do(v.scalar_tensor_tensor(flat(rF), flat(rF), 0.0, flat(r2), ALU.min, ALU.subtract))
            o.settle()
            o.do(v.memset(r7[:, :, 0:1], 0.0))
            o.do(v.memset(r7[:, :, TP:T:NS], 0.0))
            o.settle()
            o.do(v.tensor_tensor_scan(flat(r3), flat(r7), flat(rF), 0.0, ALU.mult, ALU.add))
            o.settle()
            o.do(v.tensor_tensor(flat(rI), flat(rI), flat(r3), ALU.subtract))
            o.do(v.tensor_scalar(flat(r7), flat(r7), 1.0, -NEG, ALU.subtract, ALU.mult))
            o.settle()
            o.do(v.tensor_copy(flat(r4), flat(rI)))
            o.settle()
            o.do(v.tensor_scalar(r4[:, :, 0:1], r4[:, :, 0:1], 0.0, None, ALU.max))
            first = r4[:, :, TP:T:NS]
            o.do(v.tensor_tensor(first, first, m0b.rearrange("p b h -> p h b"), ALU.max))
            o.settle()
            o.do(v.tensor_tensor_scan(flat(r5), flat(r7), flat(r4), 0.0, ALU.add, ALU.max))
            o.settle()
            o.do(v.tensor_tensor(flat(r6), flat(r3), flat(r5), ALU.add))
            w4 = w0.rearrange("p h (b s) -> p h b s", s=NS)
            o.do(v.tensor_tensor(w4, bc(m0b.rearrange("p b h -> p h b"), NS), smp4(r5), ALU.subtract))
            o.do(v.tensor_tensor(r7[:, :, 0:TP], rI[:, :, 0:TP], r5[:, :, TP - 1:TP].to_broadcast([P, H, TP]),
                                 ALU.subtract))
            o.do(v.tensor_tensor(smp4(r7), smp4(rI), smp4(r5)[:, :, :, NS - 1:NS].to_broadcast([P, H, NB, NS]),
                                 ALU.subtract))
            o.settle()
            o.do(v.tensor_copy(mrow[0:1, 0:4], r6[0:1, :, TP - 1]), sem("m_ready"))
            v.wait_ge(sem("bc_done"), 8)
            o.do(v.tensor_copy(mrow[0:1, 4:36].rearrange("p (b h) -> p b h", h=H),
                               r6[0:1, :, TP + NS - 1:T:NS].rearrange("p h b -> p b h")), sem("mrow_ready"))
            v.wait_ge(sem("col_done"), 1)
            for q in range(2):
                o.do(v.tensor_copy(cols[:, 12 * q:12 * q + 8], ps[5][:, 12 * q:12 * q + 8]))
                o.do(v.tensor_copy(cols[0:TS, 12 * q + 8:12 * q + 12], ps[5][0:TS, 12 * q + 8:12 * q + 12]))
            o.settle()
            v.wait_ge(sem("tok_copied"), 12)
            for i in range(3):
                for h in range(H):
                    n = TOK[i][1]
                    a = ktok[0:n, i, h * DH:(h + 1) * DH]
                    s = sem("col_copied") if (i, h) == (0, 0) else sem("kw_ready") if (i, h) == (2, H - 1) else None
                    o.do(v.tensor_scalar(a, a, cols[0:n, 12 + 4 * i + h:13 + 4 * i + h], DH ** -0.5, ALU.mult, ALU.mult), s)
            o.settle()
            v.wait_ge(sem("n0_copied"), 1)
            for h in range(H):
                S, hs = S_[h % 2], h % 2
                if h >= 2:
                    v.wait_ge(sem("num_done"), 2 * (h - 1))
                for i, (lo, hi, t0) in enumerate(((0, 256, 0), (256, 384, 128), (384, 416, TP))):
                    n = TOK[i][1]
                    o.do(v.tensor_scalar(S[0:n, lo:hi], r5[0:n, h, t0:t0 + hi - lo], cols[0:n, 4 * i + h:4 * i + h + 1],
                                         0.0, ALU.subtract, ALU.max), sem("sarg_ready") if i == 2 else None)
                qs = zT[:, 2 * h:2 * h + 2, TP:T]
                o.do(v.tensor_tensor(qn[:, 0:2, hs, :], qs, w0[:, h:h + 1, :].to_broadcast([P, 2, TS]), ALU.mult))
                o.settle()
                for c in range(2):
                    o.do(v.tensor_tensor(qn[:, 2 + c, hs, :].rearrange("p (b s) -> p b s", s=NS),
                                         qn[:, c, hs, :].rearrange("p (b s) -> p b s", s=NS), bc(n0T[:, :, h, c], NS),
                                         ALU.mult), sem("qn_ready") if c == 1 else None)
                if h >= 1:
                    v.wait_ge(sem("cn_done"), NB * h)
                o.do(v.tensor_tensor(kwm[0:TS], ktok[0:TS, 2:3, h * DH:(h + 1) * DH].to_broadcast([TS, NB, DH]),
                                     bc(bmask, DH), ALU.mult), sem("kwm_ready"))
                v.wait_ge(sem("sexp_ready"), h + 1)
                v.wait_ge(sem("sc_done"), h + 1)
                o.do(v.scalar_tensor_tensor(S[:, 0:384], ps[0][:, 0:384], DH ** -0.5, S[:, 0:384], ALU.mult, ALU.mult))
                o.do(v.scalar_tensor_tensor(S[0:TS, 384:416], ps[0][0:TS, 384:416], DH ** -0.5, S[0:TS, 384:416],
                                            ALU.mult, ALU.mult))
                o.settle()
                o.do(v.tensor_tensor(S[:, 0:128], S[:, 0:128], tri, ALU.mult))
                o.do(v.tensor_tensor(S[:, 256:384], S[:, 256:384], tri, ALU.mult))
                o.do(v.tensor_tensor(S[0:TS, 384:416], S[0:TS, 384:416], trs, ALU.mult), sem("sw_ready"))
                v.wait_ge(sem("den_done"), h + 1)
                o.do(v.tensor_tensor(rs[:], ps[1][:, 0:T], r2[:, h, :], ALU.max))
                o.settle()
                o.do(v.scalar_tensor_tensor(rs[:], ps[1][:, 0:T], -1.0, rs[:], ALU.mult, ALU.max))
                o.settle()
                o.do(v.reciprocal(rs[:], rs[:]))
                o.settle()
                for e in range(2):
                    v.wait_ge(sem("num_done"), 2 * h + e + 1)
                    o.do(v.tensor_tensor(hb[:, e, :], ps[2 + e][:, 0:T], rs[:], ALU.mult), sem("hb_ready"))
                for b in range(NB):
                    v.wait_ge(sem("cn_done"), NB * h + b + 1)
                    cs = CR[h % 2][:, b].rearrange("p a b -> p (a b)")
                    o.do(v.scalar_tensor_tensor(cs, cs, w0[:, h, NS * b + NS - 1:NS * b + NS],
                                                ps[6 + b % 2][:, 0:512], ALU.mult, ALU.add), sem("cn_read"))
                o.do(v.tensor_copy(ncol[:, 0, h, :], ps[5][:, 0:2]))
                o.do(v.tensor_tensor(ntmp, n0T[:, :, h, :], bc(w0[:, h, NS - 1:TS:NS], 2), ALU.mult))
                o.settle()
                o.do(v.tensor_tensor(ncol[:, 1:9, h, :], ntmp, ps[5][:, 2:18].rearrange("p (a b) -> p a b", b=2),
                                     ALU.add), sem("nc_read"))
                v.wait_ge(sem("hss_done"), h + 1)
                o.do(v.tensor_scalar(rs[:], ps[1][:, 0:T], 1.0 / DH, EPS, ALU.mult, ALU.add), sem("hms_ready"))
                v.wait_ge(sem("hsd_ready"), h + 1)
                newton(v, o, rstd[:], rs[:], r7[:, 0, :])
                for e in range(2):
                    o.do(v.scalar_tensor_tensor(hb[:, e, :], hb[:, e, :], gv[:, 64 + 2 * h + e:65 + 2 * h + e], rstd[:],
                                                ALU.mult, ALU.mult))
                o.settle()
                v.wait_ge(sem("og_ready"), 1)
                for e in range(2):
                    o.do(v.tensor_tensor(mix[:, 2 * h + e, :], hb[:, e, :], zT[:, 24 + 2 * h + e, :], ALU.mult),
                         sem("hm_ready"))

        qpT = wk(0, 8, T)
        keyn = wk(2304, 16, 64)
        keyT = wk(3328, PH, PK)
        scr = wk(4352, 3, 16 * PK)
        tv = wk(10496, 16, TK)
        ti = work[:, 10752:11008].bitcast(U32).rearrange("p (a b) -> p a b", b=TK)
        tf = wk(11008, 16, TK)
        cand = wk(11264, PH, TK, TK)
        vs = wk(13312, PH, TK)
        ic = work[:, 13440:13568].bitcast(U32)
        ia = work[:, 13568:13696].bitcast(U32)
        iF = [wk(13696, 1, P)[:, 0, :], wk(13824, 1, P)[:, 0, :]]
        eq = wk(13952, PH, TK, TK)
        tok3 = wk(16000, 3, 3, P)
        gsum = wk(17152, 2, PH)
        dense = wk(0, P, T)
        ohA = [ring[:, 1, 512 * s:512 * s + 512].rearrange("p (a b) -> p a b", b=P) for s in range(2)]
        ohB = [ring[:, 1, 1024 + 512 * s:1536 + 512 * s].rearrange("p (a b) -> p a b", b=P) for s in range(2)]
        uN = [ring[:, 0, 2048 * s:2048 * s + 2048] for s in range(2)]
        uX = [ring[:, 1, 2048 * s:2048 * s + 2048] for s in range(2)]
        vR = [ring[:, s // 2, 2048 * (s % 2):2048 * (s % 2) + 2048] for s in range(4)]
        u_v = ins["peer_u"][0].rearrange("(a b) d -> a b d", b=PK)
        v_v = ins["peer_v"][0].rearrange("(a b) d -> a b d", b=PK)
        WQ_END = 2 * sum(STREAM["wq"][:2])
        NP_ = 36

        def sp_peer(sp):
            sp.wait_ge(sem("mm_done"), 2 * STREAM["wq"][0])
            sp.dma_start(keyn, ins["peer_keys"][0].rearrange("h c k d -> k (h c) d")).then_inc(sem("key_in"), 16)
            sp.wait_ge(sem("mm_done"), WQ_END)
            for s in range(2):
                sp.dma_start(uN[s], u_v[:, s, :]).then_inc(sem(f"u_in{s}"), 16)
            with sp.Fori(1, PK // 2) as i:
                for s in range(2):
                    sp.wait_ge(sem("ut_done"), i * 8 + (4 * s - 4))
                    sp.dma_start(uN[s], u_v[:, ds(i * 2 + s, 1), :].rearrange("a b d -> a (b d)")).then_inc(
                        sem(f"u_in{s}"), 16)
            sp.wait_ge(sem("d_done"), PK)
            for half in range(2):
                cs = slice(half * 1024, half * 1024 + 1024)
                first = 0
                if half == 0:
                    for s in range(4):
                        sp.dma_start(vR[s].rearrange("p (a b) -> p a b", a=2), v_v[:, 2 * s:2 * s + 2, cs]).then_inc(
                            sem(f"v_in{s}"), 16)
                    first = 1
                with sp.Fori(first, 16) as i:
                    for s in range(4):
                        sp.wait_ge(sem("v_done"), i * 4 + (64 * half + s - 3))
                        sp.dma_start(vR[s].rearrange("p (a b) -> p a b", a=2), v_v[:, ds(i * 8 + 2 * s, 2), cs]).then_inc(
                            sem(f"v_in{s}"), 16)

        def pe_peer(pe):
            pe.wait_ge(sem("key_in"), 16)
            for g in range(2):
                for j in range(4):
                    h = 4 * g + j
                    m = pe.transpose(ps[4 + g][:, j * P:(j + 1) * P], keyn[:, 2 * h:2 * h + 2, :].rearrange("p a b -> p (a b)"),
                                     ident[:])
                m.then_inc(sem("key_done"), 1)
            pe.wait_ge(sem("key_copied"), 2)
            pe.wait_ge(sem("mm_freed"), WQ_END)
            for i, (t0, n) in enumerate(TOK):
                for g in range(2):
                    if i:
                        pe.wait_ge(sem("scr_copied"), 4 * (i - 1) + 2 * g + 2)
                    for j in range(4):
                        for c in range(2):
                            m = pe.matmul(ps[2 * g + c][0:n, j * P:(j + 1) * P],
                                          qpT[64 * c:64 * c + 64, 4 * g + j, t0:t0 + n],
                                          keyT[64 * c:64 * c + 64, 4 * g + j, :], start=True, stop=True)
                            if j == 3:
                                m.then_inc(sem("scr_done"), 1)
            for i, (t0, n) in enumerate(TOK):
                pe.wait_ge(sem("tok3_ready"), i + 1)
                for q in range(3):
                    m = pe.transpose(ps[4 + q][:, t0:t0 + n], tok3[0:n, i, q, :], ident[0:n, 0:n])
            m.then_inc(sem("ex3_done"), 1)

            def spread(i, s, first):
                pe.wait_ge(sem("oh_ready"), i * 2 + (s + 1))
                if not first:
                    pe.wait_ge(sem("g_copied"), i * 2 + (s - 1))
                for j in range(4):
                    m = pe.matmul(ps[s][:, j * P:(j + 1) * P], ohA[s][:, j, :], ohB[s][:, j, :], start=True, stop=True)
                m.then_inc(sem("g_done"), 1)

            pe.wait_ge(sem("scr_copied"), 12)
            for s in range(2):
                spread(0, s, True)
            with pe.Fori(1, NP_) as i:
                for s in range(2):
                    spread(i, s, False)
            pe.wait_ge(sem("g_copied"), 2 * NP_)

            def turn(n2, s, off, first):
                pe.wait_ge(sem(f"u_in{s}"), n2 * 16 + 16)
                for q in range(4):
                    if not first:
                        pe.wait_ge(sem(f"ut_copied{q % 2}"), n2 * 4 + (2 * s - 2 + q // 2 + 1))
                    for j in range(4):
                        k = 4 * q + j
                        m = pe.transpose(ps[q][:, j * P:(j + 1) * P], uN[s][:, k * P:(k + 1) * P], ident[:])
                    m.then_inc(sem("ut_done"), 1)

            def dots(n2, s, first):
                for q in range(2):
                    pe.wait_ge(sem(f"ut_copied{q}"), n2 * 4 + (2 * s + 2))
                if not first:
                    pe.wait_ge(sem("gelu_done"), n2 * 2 + (s - 1))
                for k in range(KD):
                    m = pe.matmul(ps[4 + s][:, 0:T], uX[s][:, k * P:(k + 1) * P], nT[:, k, :],
                                  start=(k == 0), stop=(k == KD - 1))
                m.then_inc(sem("d_done"), 1)

            turn(0, 0, 0, True)
            turn(0, 1, 0, False)
            dots(0, 0, True)
            turn(1, 0, 0, False)
            dots(0, 1, True)
            with pe.Fori(1, PK // 2 - 1) as i:
                turn(i, 1, 0, False)
                dots(i, 0, False)
                turn(i + 1, 0, 0, False)
                dots(i, 1, False)
            e = PK // 2 - 1
            turn(e, 1, 0, False)
            dots(e, 0, False)
            dots(e, 1, False)

            pe.wait_ge(sem("act_ready"), PK)
            pe.wait_ge(sem("gelu_done"), PK)
            for half in range(2):
                if half:
                    pe.wait_ge(sem("pv_added"), 8)

                def four(i, kind):
                    for s in range(4):
                        pe.wait_ge(sem(f"v_in{s}"), i * 16 + (256 * half + 16))
                        for b in range(2):
                            for c in range(8):
                                m = pe.matmul(ps[c][:, 0:T], vR[s][:, b * 1024 + c * P:b * 1024 + (c + 1) * P],
                                              work[:, ds(i * (8 * T) + (2 * s + b) * T, T)],
                                              start=(kind == 0 and s == 0 and b == 0),
                                              stop=(kind == 2 and s == 3 and b == 1))
                        m.then_inc(sem("v_done"), 1)
                four(0, 0)
                with pe.Fori(1, 15) as i:
                    four(i, 1)
                four(15, 2)

        def act_peer(act, o):
            base, nb, _k = STREAM["wq"]
            with act.Fori(0, nb // 2) as i:
                o.loop(i, {"mm_freed": 4})
                for b in range(4):
                    act.wait_ge(sem("mm_done"), i * 4 + (2 * base + b + 1))
                    o.do(act.copy(qpT[:, ds(i * 4 + b, 1), :], ps[b][:, 0:T].unsqueeze(1)), sem("mm_freed"))
                o.leave(nb // 2)
            for g in range(2):
                act.wait_ge(sem("key_done"), g + 1)
                o.do(act.copy(keyT[:, 4 * g:4 * g + 4, :], ps[4 + g][:, 0:512].rearrange("p (a b) -> p a b", b=P)),
                     sem("key_copied"))
            for i, (t0, n) in enumerate(TOK):
                for b in range(4):
                    act.wait_ge(sem("scr_done"), 4 * i + b + 1)
                    dst = scr[0:n, i, :].rearrange("p (h c k) -> p h c k", c=2, k=PK)[:, 4 * (b // 2):4 * (b // 2) + 4, b % 2, :]
                    o.do(act.copy(dst, ps[b][0:n, 0:512].rearrange("p (h k) -> p h k", k=PK)), sem("scr_copied"))
            for i in range(3):
                act.wait_ge(sem("vdiff_ready"), i + 1)
                n = TOK[i][1]
                g = tok3[0:n, i, 2, :]
                o.do(act.activation(g, g, ACT.Exp), sem("vexp_ready"))
            act.wait_ge(sem("ex3_done"), 1)
            for q in range(3):
                o.do(act.copy(ex3[:, q, :], ps[4 + q][:, 0:T]), sem("ex3_copied"))

            with act.Fori(0, NP_) as i:
                o.loop(i, {"g_copied": 2})
                for s in range(2):
                    act.wait_ge(sem("g_done"), i * 2 + (s + 1))
                    o.do(act.copy(dense[:, :, ds(i * 8 + 4 * s, 4)], ps[s][:, 0:512].rearrange("p (t k) -> p k t", k=P)),
                         sem("g_copied"))
                o.leave(NP_)

            def turned(i, s, first):
                if not first:
                    act.wait_ge(sem("d_done"), i * 2 + (s - 1))
                for q in (0, 2):
                    act.wait_ge(sem("ut_done"), i * 8 + (4 * s + q + 1))
                    o.do(act.copy(uX[s][:, 512 * q:512 * q + 512], ps[q][:, 0:512]), sem("ut_copied0"))

            def gelu(i, s, first):
                act.wait_ge(sem("d_done"), i * 2 + (s + 1))
                if not first:
                    act.wait_ge(sem("act_ready"), i * 2 + (s - 1))
                o.do(act.activation(gel[:, s, :], ps[4 + s][:, 0:T], ACT.Gelu_apprx_tanh), sem("gelu_done"))

            turned(0, 0, True)
            turned(0, 1, True)
            gelu(0, 0, True)
            turned(1, 0, False)
            gelu(0, 1, True)
            with act.Fori(1, PK // 2 - 1) as i:
                o.loop(i, {"ut_copied0": 4, "gelu_done": 2})
                turned(i, 1, False)
                gelu(i, 0, False)
                turned(i + 1, 0, False)
                gelu(i, 1, False)
                o.leave(PK // 2 - 2)
            e = PK // 2 - 1
            turned(e, 1, False)
            gelu(e, 0, False)
            gelu(e, 1, False)
            o.open = {}

        def dve_peer(v, o):
            hr = "p (h r) -> p h r"
            for i, (t0, n) in enumerate(TOK):
                v.wait_ge(sem("scr_copied"), 4 * i + 4)
                s3 = scr[0:n, i, :].rearrange("p (a k) -> p a k", k=PK)
                o.settle()

                def best16(src, m, val, idx):
                    for half in range(2):
                        for a in range(m):
                            o.do(v.max(val[0:n, a, 8 * half:8 * half + 8], src[:, a, :]))
                        o.settle()
                        for a in range(m):
                            o.do(v.max_index(idx[0:n, a, 8 * half:8 * half + 8], val[0:n, a, 8 * half:8 * half + 8],
                                             src[:, a, :]))
                            if half == 0:
                                o.do(v.match_replace(src[:, a, :], val[0:n, a, 0:8], src[:, a, :], -3.0e38))
                        o.settle()

                best16(s3, 16, tv, ti)
                o.do(v.tensor_copy(tf[0:n], ti[0:n]))
                t4 = tv[0:n].rearrange("p (h c) r -> p h c r", c=2)
                o.do(v.tensor_tensor(cand[0:n], bc(t4[:, :, 0, :], TK), t4[:, :, 1:2, :].to_broadcast([n, PH, TK, TK]),
                                     ALU.add))
                o.settle()
                best16(cand[0:n].rearrange("p h a b -> p h (a b)"), PH, vs, ic.rearrange(hr, r=TK))
                g = tok3[0:n, i, 2, :].rearrange(hr, r=TK)
                o.do(v.tensor_tensor(g, vs[0:n], vs[0:n, :, 0:1].to_broadcast([n, PH, TK]), ALU.subtract), sem("vdiff_ready"))
                f4 = tf[0:n].rearrange("p (h c) r -> p h c r", c=2)
                for c, (op, k) in enumerate(((ALU.logical_shift_right, 4), (ALU.bitwise_and, 15))):
                    o.do(v.tensor_scalar(ia[0:n], ic[0:n], k, None, op))
                    o.settle()
                    o.do(v.tensor_copy(iF[c][0:n], ia[0:n]))
                    o.settle()
                    e3 = eq[0:n].rearrange("p h r q -> p (h r) q")
                    o.do(v.tensor_tensor(e3, bc(iF[c][0:n], TK), iota[0:n, 0:TK].unsqueeze(1).to_broadcast([n, P, TK]),
                                         ALU.is_equal))
                    o.settle()
                    o.do(v.tensor_tensor(eq[0:n], eq[0:n], f4[:, :, c:c + 1, :].to_broadcast([n, PH, TK, TK]), ALU.mult))
                    o.settle()
                    o.do(v.tensor_reduce(tok3[0:n, i, c, :], e3, AX.X, ALU.add))
                v.wait_ge(sem("vexp_ready"), i + 1)
                o.do(v.tensor_reduce(gsum[0:n, 0, :], g, AX.X, ALU.add))
                o.settle()
                o.do(v.reciprocal(gsum[0:n, 1, :], gsum[0:n, 0, :]))
                o.settle()
                o.do(v.tensor_tensor(g, g, bc(gsum[0:n, 1, :], TK), ALU.mult), sem("tok3_ready"))
            v.wait_ge(sem("ex3_copied"), 3)

            def onehots(i, s, first):
                if not first:
                    v.wait_ge(sem("g_done"), i * 2 + (s - 1))
                for j in range(4):
                    t = i * 8 + 4 * s + j
                    o.do(v.tensor_scalar(ohA[s][:, j, :], iota[:], ex3[:, 0, ds(t, 1)], ex3[:, 2, ds(t, 1)],
                                         ALU.is_equal, ALU.mult))
                    o.do(v.tensor_scalar(ohB[s][:, j, :], iota[:], ex3[:, 1, ds(t, 1)], None, ALU.is_equal),
                         sem("oh_ready") if j == 3 else None)

            for s in range(2):
                onehots(0, s, True)
            with v.Fori(1, NP_) as i:
                o.loop(i, {"oh_ready": 2, "dve_own": 14})
                for s in range(2):
                    onehots(i, s, False)
                o.leave(NP_ - 1)
            o.open = {}
            v.wait_ge(sem("g_copied"), 2 * NP_)

            def turned(i, s, first):
                if not first:
                    v.wait_ge(sem("d_done"), i * 2 + (s - 1))
                for q in (1, 3):
                    v.wait_ge(sem("ut_done"), i * 8 + (4 * s + q + 1))
                    o.do(v.tensor_copy(uX[s][:, 512 * q:512 * q + 512], ps[q][:, 0:512]), sem("ut_copied1"))

            def gate(i, s):
                v.wait_ge(sem("gelu_done"), i * 2 + (s + 1))
                a = work[:, ds(i * (2 * T) + s * T, T)]
                o.do(v.tensor_tensor(a, a, gel[:, s, :], ALU.mult), sem("act_ready"))

            turned(0, 0, True)
            turned(0, 1, True)
            gate(0, 0)
            turned(1, 0, False)
            gate(0, 1)
            with v.Fori(1, PK // 2 - 1) as i:
                o.loop(i, {"ut_copied1": 4, "act_ready": 2})
                turned(i, 1, False)
                gate(i, 0)
                turned(i + 1, 0, False)
                gate(i, 1)
                o.leave(PK // 2 - 2)
            e = PK // 2 - 1
            turned(e, 1, False)
            gate(e, 0)
            gate(e, 1)
            o.open = {}
            for half in range(2):
                v.wait_ge(sem("v_done"), 64 * (half + 1))
                for c in range(8):
                    h = hT[:, 8 * half + c, :]
                    o.do(v.tensor_tensor(h, h, ps[c][:, 0:T], ALU.add), sem("pv_added"))
            o.settle()

        proj = wk(0, 2, D)
        pN = wk(4096, 3, PLE)
        pT = wk(4864, 2, T)
        yout = wk(8192, 3, D)

        def sp_tail(sp):
            w = ins["w_ple_gate"][0].rearrange("(k p) n -> p k n", p=P)
            sp.wait_ge(sem("v_done"), 128)
            for i, (t0, n) in enumerate(TOK):
                src = ins["p_prompt"][0, 0, t0:t0 + n, :] if i < 2 else ins["p_sample"][0].rearrange("b s d -> (b s) d")
                sp.dma_start(pN[0:n, i, :], src).then_inc(sem("p_in"), 16)
            for s in range(2):
                sp.dma_start(ring[:, s, :].rearrange("p (k n) -> p k n", n=WB), w[:, :, s * WB:(s + 1) * WB]).then_inc(
                    sem(f"pw_in{s}"), 16)
            sp.dma_start(proj, ins["w_ple_proj"][0].rearrange("(k p) n -> p k n", p=P)).then_inc(sem("proj_in"), 16)
            with sp.Fori(1, 4) as i:
                for s in range(2):
                    sp.wait_ge(sem("gate_mm"), i * 4 + (2 * s - 2))
                    sp.dma_start(ring[:, s, :].rearrange("p (k n) -> p k n", n=WB),
                                 w[:, :, ds(i * (2 * WB) + s * WB, WB)]).then_inc(sem(f"pw_in{s}"), 16)
            for i, (t0, n) in enumerate(TOK):
                dst = outs[0][0, t0:t0 + n, :] if i < 2 else outs[1].rearrange("b s d -> (b s) d")
                for q in range(2):
                    sp.wait_ge(sem(f"y_out{q}"), 2 * (i + 1))
                sp.dma_start(dst, yout[0:n, i, :]).then_inc(sem("y_stored"), 16)
            sp.wait_ge(sem("y_stored"), 48)

        def pe_tail(pe):
            pe.wait_ge(sem("p_in"), 48)
            pe.wait_ge(sem("pv_added"), 16)
            for i, (t0, n) in enumerate(TOK):
                for c in range(2):
                    m = pe.transpose(ps[c][:, t0:t0 + n], pN[0:n, i, c * P:(c + 1) * P], ident[0:n, 0:n])
            m.then_inc(sem("pt_done"), 1)
            pe_norm(pe, 2)
            pe.wait_ge(sem("pt_copied"), 1)
            pe.wait_ge(sem("n_ready"), 3 * KD)
            pe.wait_ge(sem("proj_in"), 16)

            def pair(i, first):
                for s in range(2):
                    pe.wait_ge(sem(f"pw_in{s}"), i * 16 + 16)
                    for c in range(2):
                        if not first:
                            pe.wait_ge(sem("sig_done"), i * 4 + (2 * s + c - 3))
                        for k in range(KD):
                            m = pe.matmul(ps[2 * s + c][:, 0:T], ring[:, s, k * WB + c * P:k * WB + (c + 1) * P],
                                          nT[:, k, :], start=(k == 0), stop=(k == KD - 1))
                        m.then_inc(sem("gate_mm"), 1)

            def embed(c8):
                for c in range(2 * c8, 2 * c8 + 2):
                    if c >= 2:
                        pe.wait_ge(sem("e_copied"), c - 1)
                    for k in range(2):
                        m = pe.matmul(ps[4 + c % 2][:, 0:T], proj[:, k, c * P:(c + 1) * P], pT[:, k, :],
                                      start=(k == 0), stop=(k == 1))
                    m.then_inc(sem("e_done"), 1)

            for c8 in range(8):
                embed(c8)
            pair(0, True)
            with pe.Fori(1, 4) as i:
                pair(i, False)
            pe_norm(pe, 3)
            pe.wait_ge(sem("n_ready"), 4 * KD)
            for g in range(12):
                i, q = divmod(g, 4)
                t0, n = TOK[i]
                if g >= 4:
                    pe.wait_ge(sem(f"y_out{g % 2}"), (g - 4) // 2 + 1)
                for j in range(4):
                    m = pe.transpose(ps[g % 4][0:n, j * P:(j + 1) * P], nT[:, 4 * q + j, t0:t0 + n], ident[:])
                m.then_inc(sem("yt_done"), 1)

        eT = wk(14336, KD, T)

        def act_tail(act, o):
            act.wait_ge(sem("pt_done"), 1)
            for c in range(2):
                o.do(act.copy(pT[:, c, :], ps[c][:, 0:T]), sem("pt_copied") if c else None)
            act.wait_ge(sem("pv_added"), 16)
            act_norm(act, 2)
            for c in range(KD):
                act.wait_ge(sem("e_done"), c + 1)
                o.do(act.copy(eT[:, c, :], ps[4 + c % 2][:, 0:T]), sem("e_copied"))

            def sig(i, first):
                for b in range(4):
                    act.wait_ge(sem("gate_mm"), i * 4 + (b + 1))
                    if not (first and b < 2):
                        act.wait_ge(sem("gate_used"), i * 4 + (b - 1))
                    o.do(act.activation(gel[:, b % 2, :], ps[b][:, 0:T], ACT.Sigmoid), sem("sig_done"))

            o.open = {}
            sig(0, True)
            with act.Fori(1, 4) as i:
                o.loop(i, {"sig_done": 4})
                sig(i, False)
                o.leave(3)
            act.wait_ge(sem("h_added"), KD)
            act_norm(act, 3)
            for g in range(0, 12, 2):
                i, q = divmod(g, 4)
                n = TOK[i][1]
                act.wait_ge(sem("yt_done"), g + 1)
                o.do(act.copy(yout[0:n, i, 512 * q:512 * q + 512], ps[g % 4][0:n, 0:512]), sem("y_out0"))

        def dve_tail(v, o):
            dve_norm(v, o, 2)
            v.wait_ge(sem("e_copied"), KD)
            with v.Fori(0, 4) as i:
                o.loop(i, {"gate_used": 4, "h_added": 4})
                for b in range(4):
                    v.wait_ge(sem("sig_done"), i * 4 + (b + 1))
                    e = eT[:, ds(i * 4 + b, 1), :]
                    h = hT[:, ds(i * 4 + b, 1), :]
                    o.do(v.tensor_tensor(e, e, gel[:, b % 2:b % 2 + 1, :], ALU.mult), sem("gate_used"))
                    o.settle()
                    o.do(v.tensor_tensor(h, h, e, ALU.add), sem("h_added"))
                o.leave(4)
            dve_norm(v, o, 3)
            for g in range(1, 12, 2):
                i, q = divmod(g, 4)
                n = TOK[i][1]
                v.wait_ge(sem("yt_done"), g + 1)
                o.do(v.tensor_copy(yout[0:n, i, 512 * q:512 * q + 512], ps[g % 4][0:n, 0:512]), sem("y_out1"))

        block = ctx.enter_context(nc.Block())

        @block.sync
        def _(sp):
            for i, (t0, n) in enumerate(TOK):
                src = ins["x_prompt"][0, t0:t0 + n, :] if i < 2 else ins["x_sample"].rearrange("b s d -> (b s) d")
                sp.dma_start(xin[0:n, i, :], src).then_inc(sem(f"x_in{i}"), 16)
            v = sem("vec_in")
            at = 0
            for name, rows in (("norm_mix", 16), ("norm_ffn", 16), ("norm_ple", 16), ("norm_final", 16),
                               ("mlstm_norm", 8), ("b_glu", 8)):
                a = ins[name] if name == "norm_final" else ins[name][0]
                sp.dma_start(vrow[at:at + rows, :], a.rearrange("(r p) -> r p", p=P)).then_inc(v, 16)
                at += rows
            sp.dma_start(vrow[80:88, :], ins["ssm_D"][0].rearrange("(u r) c -> u (r c)", r=8)).then_inc(v, 16)
            sp.dma_start(gb8[0:4], ins["b_igate"].rearrange("a h -> h a")).then_inc(v, 16)
            sp.dma_start(gb8[4:8], ins["b_fgate"].rearrange("a h -> h a")).then_inc(v, 16)

            def weights(name, src, c0):
                base, nb, kt = STREAM[name]
                w = src.rearrange("(k p) n -> p k n", p=P)
                first = 0
                if base == 0:
                    for s in range(2):
                        sp.dma_start(ring[:, s, 0:kt * WB].rearrange("p (k n) -> p k n", n=WB),
                                     w[:, :, c0 + s * WB:c0 + (s + 1) * WB]).then_inc(sem(f"w_in{s}"), 16)
                    first = 1
                with sp.Fori(first, nb // 2) as i:
                    for s in range(2):
                        sp.wait_ge(sem("mm_done"), i * 4 + 2 * (base + s) - 2)
                        sp.dma_start(ring[:, s, 0:kt * WB].rearrange("p (k n) -> p k n", n=WB),
                                     w[:, :, ds(i * (2 * WB) + (c0 + s * WB), WB)]).then_inc(sem(f"w_in{s}"), 16)

            w_in = ins["w_in"][0]
            s5 = sem("s5_in")
            for q, name in enumerate(AB):
                sp.dma_start(r32[0:NJ, q, :], ins[name][0].rearrange("(j g) p -> j (g p)", g=2)).then_inc(s5, 16)
            sp.dma_start(dtr[0:NJ, :], ins["ssm_log_dt"][0].rearrange("(j g) -> j g", g=2)).then_inc(s5, 16)
            for q, name in enumerate(("re", "im")):
                sp.dma_start(Bn[q], ins[f"ssm_B_{name}"][0].rearrange("(j g) p c -> (g p) j c", g=2)).then_inc(s5, 16)
                sp.dma_start(Cn[q], ins[f"ssm_C_{name}"][0].rearrange("(u r) c p -> (r c) u p", r=8)).then_inc(s5, 16)
                sp.dma_start(s0r[:, :, q, :], ins[f"state_ssm_{name}"][0]
                             .rearrange("b (j g) p -> (b j) (g p)", g=2)
                             .rearrange("(t r) q -> r t q", t=2)).then_inc(s5, 16)
            sp.dma_start(gw, w_in[:, 4 * MW:4 * MW + 8].rearrange("(k p) n -> p k n", p=P)).then_inc(sem("gw_in"), 16)
            weights("u", w_in, 4 * MW + 8)
            weights("z", w_in, 0)
            weights("glu", ins["w_glu"][0], 0)
            sp_mlstm(sp)
            weights("out", ins["w_out"][0], 0)
            weights("wq", ins["peer_w_q"][0], 0)
            sp_peer(sp)
            sp_tail(sp)

        @block.gpsimd
        def _(pool):
            o = Own(pool, sem("pool_own"))
            o.do(pool.memset(ident[:], 0.0))
            o.do(pool.memset(ones[:], 1.0))
            o.do(pool.memset(par[:, 0:4], 1.0))
            o.do(pool.memset(bmask, 1.0))
            o.settle()
            o.do(pool.affine_select(out=ident[:], in_=ident[:], compare_op=ALU.not_equal, fill=1.0, base=0,
                                    pattern=[[-1, P]], channel_multiplier=1))
            o.do(pool.iota(iota[:], [[1, P]], base=0, channel_multiplier=0, allow_small_or_imprecise_dtypes=True))
            o.do(pool.affine_select(out=tri, in_=ones[:], compare_op=ALU.is_ge, fill=0.0, base=0,
                                    pattern=[[1, P]], channel_multiplier=-1))
            o.do(pool.affine_select(out=trs, in_=ones[0:TS, 0:TS], compare_op=ALU.is_ge, fill=0.0, base=0,
                                    pattern=[[1, TS]], channel_multiplier=-1))
            o.settle()
            tv = trs.rearrange("p (b s) -> p b s", s=NS)
            o.do(pool.affine_select(out=tv, in_=tv, compare_op=ALU.is_ge, fill=0.0, base=0,
                                    pattern=[[-NS, NB], [0, NS]], channel_multiplier=1))
            o.do(pool.affine_select(out=bmask, in_=bmask, compare_op=ALU.is_ge, fill=0.0, base=0,
                                    pattern=[[-NS, NB]], channel_multiplier=1))
            o.do(pool.affine_select(out=par[:, 0:4], in_=par[:, 0:4], compare_op=ALU.is_ge, fill=0.0, base=0,
                                    pattern=[[-32, 4]], channel_multiplier=1))
            o.settle()
            o.do(pool.affine_select(out=bmask, in_=bmask, compare_op=ALU.is_ge, fill=0.0, base=NS - 1,
                                    pattern=[[NS, NB]], channel_multiplier=-1))
            o.do(pool.affine_select(out=par[:, 0:4], in_=par[:, 0:4], compare_op=ALU.is_ge, fill=0.0, base=15,
                                    pattern=[[32, 4]], channel_multiplier=-1))
            o.settle()
            o.do(pool.memset(par[:, 7:8], 0.0), sem("const_ready"))

        @block.tensor
        def _(pe):
            pe.wait_ge(sem("const_ready"), 1)
            for g in range(12):
                i, q = divmod(g, 4)
                n = TOK[i][1]
                if q == 0:
                    pe.wait_ge(sem(f"x_in{i}"), 16)
                if g >= 4:
                    pe.wait_ge(sem(f"xt_copied{g % 2}"), (g - 4) // 2 + 1)
                for j in range(4):
                    m = pe.transpose(ps[g % 4][:, j * n:(j + 1) * n],
                                     xin[0:n, i, (4 * q + j) * P:(4 * q + j + 1) * P], ident[0:n, 0:n])
                m.then_inc(sem("xt_done"), 1)
            pe.wait_ge(sem("vec_in"), 16 * 9)
            pe.transpose(ps[4][:, 0:88], vrow[0:88, :], ident[0:88, 0:88]).then_inc(sem("vec_done"), 1)
            pe_norm(pe, 0)
            pe.wait_ge(sem("n_ready"), KD)
            pe.wait_ge(sem("xt_copied0"), 6)
            pe.wait_ge(sem("xt_copied1"), 6)
            pe_linear(pe, "u", nT)
            pe.wait_ge(sem("gw_in"), 16)
            for k in range(KD):
                m = pe.matmul(ps[5][0:8, 0:T], gw[:, k, :], nT[:, k, :], start=(k == 0), stop=(k == KD - 1))
            m.then_inc(sem("gate_done"), 1)
            pe.wait_ge(sem("abf_rows"), 1)
            for q in range(4):
                m = pe.transpose(ps[4][:, q * NJ:(q + 1) * NJ], r32[0:NJ, 10 + q, :], ident[0:NJ, 0:NJ])
            m.then_inc(sem("abf_done"), 1)
            pe.wait_ge(sem("s5_in"), 16 * 9)
            for q in range(2):
                for t in range(2):
                    m = pe.transpose(ps[6][:, (2 * q + t) * P:(2 * q + t + 1) * P], s0r[:, t, q, :], ident[:])
            m.then_inc(sem("s0_done"), 1)
            pe.wait_ge(sem("gate_copied"), 1)
            pe.wait_ge(sem("abf_copied"), 1)
            pe.wait_ge(sem("s0_copied"), 1)
            for g in range(8):
                src, q, half = [Bbd, Cbd][g // 4], (g // 2) % 2, g % 2
                pe.wait_ge(sem("bd_ready"), g // 4 + 1)
                if g >= 4:
                    pe.wait_ge(sem("bct_copied"), g - 3)
                for j in range(4):
                    u = 4 * half + j
                    if g < 4:
                        a = Bbd[q][:, 4 * u:4 * u + 4, :, :].rearrange("p a b c -> p (a b c)")
                    else:
                        a = Cbd[q][:, u, :, :].rearrange("p b c -> p (b c)")
                    m = pe.transpose(ps[4 + g % 4][:, j * P:(j + 1) * P], a, ident[:])
                m.then_inc(sem("bct_done"), 1)
            pe.wait_ge(sem("bct_copied"), 8)
            pe.wait_ge(sem("mm_freed"), 8)
            for j in range(NJ):
                u, r = divmod(j, 4)
                if j >= 2:
                    pe.wait_ge(sem("bu_copied0"), j - 1)
                    pe.wait_ge(sem("bu_copied1"), j - 1)
                for q in range(2):
                    pe.matmul(ps[4 + 2 * (j % 2) + q][:, 0:T], BT[q][32 * r:32 * r + 32, u, :],
                              uT[32 * r:32 * r + 32, u, :], start=True, stop=True).then_inc(sem("bu_done"), 1)
            pe_linear(pe, "z", nT)
            pe.wait_ge(sem("s5_ready"), 1)
            pe.wait_ge(sem("bu_copied0"), NJ)
            pe.wait_ge(sem("bu_copied1"), NJ)
            for u in range(8):
                if u >= 2:
                    pe.wait_ge(sem("y_sum"), u - 1)
                for r in range(4):
                    for q in range(2):
                        m = pe.matmul(ps[4 + u % 2][32 * r:32 * r + 32, 0:T], CT[q][:, u, 32 * r:32 * r + 32],
                                      st[q][:, 4 * u + r, :], start=(q == 0), stop=(q == 1))
                m.then_inc(sem("y_done"), 1)
            pe.wait_ge(sem("send_ready"), 1)
            for q in range(2):
                pe.transpose(ps[6][0:NJ, q * P:(q + 1) * P], send[:, q, 0, :], ident[:])
                for t in range(2):
                    m = pe.transpose(ps[7][:, (2 * q + t) * P:(2 * q + t + 1) * P],
                                     send[:, q, 1 + 4 * t:5 + 4 * t, :].rearrange("p a b -> p (a b)"), ident[:])
            m.then_inc(sem("send_done"), 1)
            pe.wait_ge(sem("yg_ready"), 8)
            pe_linear(pe, "glu", uT)
            pe_mlstm(pe)
            pe.wait_ge(sem("glu_ready"), 8)
            pe.wait_ge(sem("hm_ready"), 2 * H)
            pe_linear(pe, "out", mix)
            pe_norm(pe, 1)
            pe.wait_ge(sem("n_ready"), 2 * KD)
            pe_linear(pe, "wq", nT)
            pe_peer(pe)
            pe_tail(pe)

        @block.scalar
        def _(act):
            o_act.eng = act
            o = o_act
            for g in range(0, 12, 2):
                i, q = divmod(g, 4)
                t0, n = TOK[i]
                act.wait_ge(sem("xt_done"), g + 1)
                o.do(act.copy(hT[:, 4 * q:4 * q + 4, t0:t0 + n],
                              ps[g % 4][:, 0:4 * n].rearrange("p (a b) -> p a b", b=n)), sem("xt_copied0"))
            act.wait_ge(sem("vec_done"), 1)
            o.do(act.copy(gv[:], ps[4][:, 0:88]), sem("vec_copied"))
            act.wait_ge(sem("xt_copied1"), 6)
            o.settle()
            act_norm(act, 0)
            act.wait_ge(sem("s5_in"), 16 * 9)
            o.do(act.activation(dtr[0:NJ, :], dtr[0:NJ, :], ACT.Exp), sem("dt_ready"))

            def copy_tiles(name, dst, fn=None):
                base, nb, kt = STREAM[name]

                def one(i, b, peeled=False):
                    act.wait_ge(sem("mm_done"), i * 4 + (2 * base + b + 1))
                    src = ps[b][:, 0:T]
                    d = dst[:, b, :] if peeled else dst[:, ds(i * 4 + b, 1), :]
                    if not peeled:
                        src = src.unsqueeze(1)
                    o.do(act.copy(d, src), sem("mm_freed"))
                with act.Fori(0, nb // 2) as i:
                    o.loop(i, {"mm_freed": 4})
                    for b in range(4):
                        one(i, b)
                    o.leave(nb // 2)

            copy_tiles("u", uT)
            act.wait_ge(sem("theta_ready"), 1)
            o.do(act.activation(r32[0:NJ, 4, :], r32[0:NJ, 2, :], ACT.Exp))
            o.do(act.activation(r32[0:NJ, 5, :], r32[0:NJ, 3, :], ACT.Sin))
            o.do(act.activation(r32[0:NJ, 6, :], r32[0:NJ, 3, :], ACT.Sin, scale=0.5), sem("trig_ready"))
            o.settle()
            act.wait_ge(sem("s0_done"), 1)
            o.do(act.copy(s0T, ps[6][:, 0:512].rearrange("p (a b) -> p a b", a=2)), sem("s0_copied"))
            for g in range(8):
                dst = [BT, CT][g // 4][(g // 2) % 2]
                half = g % 2
                act.wait_ge(sem("bct_done"), g + 1)
                o.do(act.copy(dst[:, 4 * half:4 * half + 4, :],
                              ps[4 + g % 4][:, 0:512].rearrange("p (a b) -> p a b", b=P)), sem("bct_copied"))
            for j in range(NJ):
                act.wait_ge(sem("bu_done"), 2 * j + 1)
                o.do(act.copy(st[0][:, j, :], ps[4 + 2 * (j % 2)][:, 0:T]), sem("bu_copied0"))
            copy_tiles("z", zT)
            for u in range(8):
                act.wait_ge(sem("y_sum"), u + 1)
                o.do(act.activation(uT[:, u, :], uT[:, u, :], ACT.Gelu_apprx_tanh), sem("yg_ready"))
            o.settle()
            act.wait_ge(sem("send_done"), 1)
            o.do(act.copy(sout[0:NJ, 0:2, :], ps[6][0:NJ, 0:2 * P].rearrange("p (a b) -> p a b", b=P)))
            o.do(act.copy(sout[:, 2:6, :], ps[7][:, 0:512].rearrange("p (a b) -> p a b", b=P)), sem("sout_ready"))
            o.do(act.activation(zT[:, 24:32, :], zT[:, 24:32, :], ACT.Sigmoid), sem("og_ready"))
            base = STREAM["glu"][0]
            for c in range(8):
                act.wait_ge(sem("mm_done"), 2 * base + c + 1)
                if c >= 2:
                    act.wait_ge(sem("glu_ready"), c - 1)
                o.do(act.activation(gel[:, c % 2, :], ps[c % 4][:, 0:T], ACT.Sigmoid, bias=gv[:, 72 + c:73 + c]),
                     sem("mm_freed"))
            act_mlstm(act, o)
            act.wait_ge(sem("mm_freed"), 2 * (STREAM["out"][0] + STREAM["out"][1]))
            act_norm(act, 1)
            act_peer(act, o)
            act_tail(act, o)

        @block.vector
        def _(v):
            o = Own(v, sem("dve_own"))
            v.wait_ge(sem("const_ready"), 1)
            for g in range(1, 12, 2):
                i, q = divmod(g, 4)
                t0, n = TOK[i]
                v.wait_ge(sem("xt_done"), g + 1)
                o.do(v.tensor_copy(hT[:, 4 * q:4 * q + 4, t0:t0 + n],
                                   ps[g % 4][:, 0:4 * n].rearrange("p (a b) -> p a b", b=n)), sem("xt_copied1"))
            v.wait_ge(sem("vec_copied"), 1)
            v.wait_ge(sem("xt_copied0"), 6)
            dve_norm(v, o, 0)
            dve_s5_setup(v, o)
            for j in range(NJ):
                v.wait_ge(sem("bu_done"), 2 * j + 2)
                o.do(v.tensor_copy(st[1][:, j, :], ps[5 + 2 * (j % 2)][:, 0:T]), sem("bu_copied1"))
            v.wait_ge(sem("bu_copied0"), NJ)
            dve_s5_scan(v, o)
            for u in range(8):
                v.wait_ge(sem("y_done"), u + 1)
                o.do(v.scalar_tensor_tensor(uT[:, u, :], uT[:, u, :], gv[:, 80 + u:81 + u], ps[4 + u % 2][:, 0:T],
                                            ALU.mult, ALU.add), sem("y_sum"))
            base = STREAM["glu"][0]
            for c in range(8):
                v.wait_ge(sem("mm_freed"), 2 * base + c + 1)
                o.do(v.tensor_tensor(mix[:, 8 + c, :], uT[:, c, :], gel[:, c % 2, :], ALU.mult), sem("glu_ready"))
            dve_mlstm(v, o)
            base, nb, _k = STREAM["out"]
            with v.Fori(0, nb // 2) as i:
                o.loop(i, {"mm_freed": 4})
                for b in range(4):
                    v.wait_ge(sem("mm_done"), i * 4 + (2 * base + b + 1))
                    h = hT[:, ds(i * 4 + b, 1), :]
                    o.do(v.tensor_tensor(h, h, ps[b][:, 0:T].unsqueeze(1), ALU.add), sem("mm_freed"))
                o.leave(nb // 2)
            o.settle()
            dve_norm(v, o, 1)
            dve_peer(v, o)
            dve_tail(v, o)


_INS = ["x_prompt", "x_sample", "state_mlstm_C", "state_mlstm_n", "state_mlstm_m", "state_ssm_re", "state_ssm_im",
        "p_prompt", "p_sample", "norm_mix", "w_in", "b_igate", "b_fgate", "mlstm_norm", "ssm_A_re", "ssm_A_im",
        "ssm_B_re", "ssm_B_im", "ssm_C_re", "ssm_C_im", "ssm_D", "ssm_log_dt", "w_glu", "b_glu", "w_out", "norm_ffn",
        "peer_w_q", "peer_keys", "peer_u", "peer_v", "norm_ple", "w_ple_gate", "w_ple_proj", "norm_final"]
_OUTS = [(1, TP, D), (NB, NS, D),
         (1, 1, H, DH, DH), (1, 1, H, DH), (1, 1, H), (1, 1, G, SP_), (1, 1, G, SP_),
         (1, NB, H, DH, DH), (1, NB, H, DH), (1, NB, H), (1, NB, G, SP_), (1, NB, G, SP_)]


def kernel(**inputs):
    import numpy as np
    import concourse.bacc as bacc
    from concourse.bass_utils import run_bass_kernel_spmd

    nc = bacc.Bacc("TRN2", target_bir_lowering=False, num_devices=1, dynamic_dma_scratch_size=1024)
    arrays, ins = {}, {}
    for name in _INS:
        a = np.ascontiguousarray(inputs[name])
        arrays[f"in_{name}"] = a
        ins[name] = nc.dram_tensor(f"in_{name}", a.shape, mybir.dt.from_np(a.dtype), kind="ExternalInput").ap()
    outs = [nc.dram_tensor(f"out_{i}", shape, F32, kind="ExternalOutput").ap() for i, shape in enumerate(_OUTS)]
    build(nc, ins, outs)
    r = run_bass_kernel_spmd(nc, [arrays], core_ids=[0])
    return tuple(r.results[0][f"out_{i}"] for i in range(len(_OUTS)))
```

```python
from contextlib import ExitStack
import math

import concourse.bass as bass
from concourse import mybir

F32 = mybir.dt.float32
F32R = mybir.dt.float32r
U32 = mybir.dt.uint32
ALU = mybir.AluOpType
ACT = mybir.ActivationFunctionType
AX = mybir.AxisListType

P = 128
D = 2048
KD = D // P
TP, NB, NS = 256, 8, 4
TS = NB * NS
T = TP + TS
TOK = [(0, 128), (128, 128), (256, TS)]
H, DH = 4, 256
MW = H * DH
G, SP_, GC = 64, 64, 16
NJ = G * SP_ // P
CH = 16
NCH = TP // CH
PH, PK, TK = 8, 128, 16
PLE = 256
EPS = 1e-6
WB = 256
COLS_IN = 4 * MW + 2 * H + G * GC
NEG = -1.0e38

O_RE, O_IM = 0, NJ * T
O_Z = 2 * NJ * T
O_U = O_Z + 32 * T
O_MIX = O_U + 8 * T
O_EX = O_MIX + 16 * T
WORK = P * T
assert O_EX + 8 * T == WORK

STREAM, _n = {}, 0
for _name, _blocks, _kt in (("u", 4, KD), ("z", 16, KD), ("glu", 4, 8)):
    STREAM[_name] = (_n, _blocks, _kt)
    _n += _blocks


TRIPLE, _n = {}, 0
for _name, _tiles in (("out", KD), ("wq", 8), ("U", PK), ("gate", KD)):
    TRIPLE[_name] = (_n, _tiles)
    _n += _tiles


class Own:

    def __init__(self, eng, chain):
        self.eng, self.chain, self.n, self.open, self.per = eng, chain, {}, {}, None

    def do(self, ins, sem=None):
        s = self.chain if sem is None else sem
        ins.then_inc(s, 1)
        self.n[s.name] = self.n.get(s.name, 0) + 1
        self.open[s.name] = s

    def settle(self):
        for name, s in self.open.items():
            n = self.n[name]
            if self.per is not None:
                i, per = self.per
                self.eng.wait_ge(s, i * per.get(name, 0) + n)
            else:
                self.eng.wait_ge(s, n)
        self.open = {}

    def loop(self, i, per):
        self.per, self.at = (i, per), dict(self.n)

    def leave(self, trips):
        per = self.per[1]
        for name, n in self.n.items():
            assert n - self.at.get(name, 0) == per.get(name, 0), (name, n - self.at.get(name, 0))
            self.n[name] = self.at.get(name, 0) + trips * per.get(name, 0)
        self.per = None


def build(nc, ins, outs):
    ctx = ExitStack()
    with ctx:
        def sb(name, shape, dt=F32):
            base = nc.sbuf_base
            t = ctx.enter_context(nc.sbuf_tensor(name, shape, dt))
            sb_at[name] = -(-base // 32) * 32
            return t

        sb_at = {}
        sems = {}

        def sem(name):
            if name not in sems:
                sems[name] = ctx.enter_context(nc.semaphore(name))
            return sems[name]

        low = sb("low", [P, 2 * KD * T])
        ring = sb("ring", [P, 2, 4096])
        work = sb("work", [P, WORK])
        ident = sb("ident", [P, P])
        ones = sb("ones", [P, P])
        iota = sb("iota", [P, P])
        gv = sb("gv", [P, 88])
        rstd = sb("rstd", [P, T])
        rs = sb("rs", [P, T])
        gel = sb("gel", [P, 2, T])
        ex3 = sb("ex3", [P, 3, T])
        tri = ex3[:, 0, 0:P]
        trs = ex3[0:TS, 0, P:P + TS]
        cols = ex3[:, 0, 160:192]
        bmask = ex3[0:TS, 0, 192:192 + NB]
        par = ex3[:, 0, 200:208]
        gb8 = ex3[0:8, 0, 208:209]
        rows8 = ex3[0:8, 1, :]
        ps = [ctx.enter_context(nc.psum_tensor(f"ps{i}", [P, 512], F32)) for i in range(8)]

        low_at, ring_at, work_at = sb_at["low"], sb_at["ring"], sb_at["work"]

        def alias(name, at, *shape, dt=F32R):
            return nc.alloc_sbuf_tensor_at(name, [P, *shape], dt, offset=at)[:]

        hT = low[:, 0:KD * T].rearrange("p (k t) -> p k t", t=T)
        nT = low[:, KD * T:2 * KD * T].rearrange("p (k t) -> p k t", t=T)
        mix_h = alias("mix_h", work_at + 4 * (O_Z + 8 * T), KD, T)
        mix_l = alias("mix_l", work_at + 4 * O_MIX, KD, T)
        ffn_h = alias("ffn_h", low_at + 4 * KD * T, KD, T)
        ffn_l = alias("ffn_l", low_at, KD, T)
        ple_h = alias("ple_h", work_at + 4 * 24000, KD, T)
        ple_l = alias("ple_l", work_at + 4 * (24000 + KD * T), KD, T)
        natural = [ring[:, 0, 2048 * s:2048 * s + 2048] for s in range(2)]
        part_h = alias("part_h", ring_at + 16384, 4, 512)
        part_l = alias("part_l", ring_at + 16384 + 8192, 4, 512)
        act_h = alias("act_h", low_at + 4 * KD * T, 2, T)
        act_l = alias("act_l", low_at + 4 * KD * T + 8 * T, 2, T)
        spill = nc.dram_tensor("spill", [P, KD * T], F32).ap()

        def wk(off, *shape):
            n = math.prod(shape)
            ap = work[:, off:off + n]
            if len(shape) == 2:
                ap = ap.rearrange("p (a b) -> p a b", b=shape[1])
            elif len(shape) == 3:
                ap = ap.rearrange("p (a b c) -> p a b c", b=shape[1], c=shape[2])
            return ap

        def bc(ap, n):
            return ap.unsqueeze(len(ap.shape)).to_broadcast([*ap.shape, n])

        st = [wk(O_RE, NJ, T), wk(O_IM, NJ, T)]
        zT = wk(O_Z, 32, T)
        uT = wk(O_U, 8, T)
        mix = wk(O_MIX, 16, T)
        xin = wk(O_Z, 3, D)
        Bn = [wk(0, NJ, GC), wk(512, NJ, GC)]
        Bbd = [wk(1024, NJ, 2, GC), wk(2048, NJ, 2, GC)]
        Cn = [wk(3072, 8, SP_), wk(3584, 8, SP_)]
        Cbd = [wk(4096, 8, 2, SP_), wk(5120, 8, 2, SP_)]
        tB = [wk(6144 + 512 * i, NJ, GC) for i in range(4)]
        r32 = wk(8192, 16, P)
        s0r = wk(10240, 2, 2, P)
        vrow = wk(10752, 1, P)[:, 0, :]
        dtr = wk(10880, 1, 2)[:, 0, :]
        gw = wk(11008, KD, 8)
        BT = [wk(O_MIX, 8, P), wk(O_MIX + 1024, 8, P)]
        CT = [wk(O_MIX + 2048, 8, P), wk(O_MIX + 3072, 8, P)]
        abT = wk(O_MIX + 4096, 4, NJ)
        a16 = wk(O_MIX + 4224, 4, NJ)
        s0T = gel[:, :, 0:NB * NJ]
        tS = [wk(O_EX + 512 * i, NJ, 16) for i in range(4)]

        ds = bass.ds
        AB = ["ssm_A_re", "ssm_A_im"]

        send = wk(O_EX, 2, 1 + NB, NJ)
        sout = wk(O_EX + 576, 6, P)

        def pe_norm(pe, n):
            for q in range(4):
                pe.wait_ge(sem("sq_done"), 4 * n + q + 1)
                for k in range(4 * q, 4 * q + 4):
                    m = pe.matmul(ps[7][:, 0:T], ones[:], nT[:, k, :], start=(k == 0), stop=(k == KD - 1))
            m.then_inc(sem("ss_done"), 1)

        def pe_linear(pe, name, rhs):
            base, nb, kt = STREAM[name]

            def blk(i, s, first):
                pe.wait_ge(sem(f"w_in{s}"), 16 * (base // 2 + 1) + i * 16)
                for c in range(2):
                    if not first:
                        pe.wait_ge(sem("mm_freed"), i * 4 + (2 * base + 2 * s + c - 3))
                    for k in range(kt):
                        m = pe.matmul(ps[2 * s + c][:, 0:T],
                                      ring[:, s, k * WB + c * P:k * WB + (c + 1) * P], rhs[:, k, :],
                                      start=(k == 0), stop=(k == kt - 1))
                    m.then_inc(sem("mm_done"), 1)

            i0 = 0
            if base == 0:
                blk(0, 0, True)
                blk(0, 1, True)
                i0 = 1
            with pe.Fori(i0, nb // 2) as i:
                blk(i, 0, False)
                blk(i, 1, False)

        def act_norm(act, n):
            for q in range(4):
                o_act.do(act.activation(nT[:, 4 * q:4 * q + 4, :], hT[:, 4 * q:4 * q + 4, :], ACT.Square),
                         sem("sq_done"))
            act.wait_ge(sem("ms_ready"), n + 1)
            o_act.do(act.activation(rstd[:], rs[:], ACT.Sqrt), sem("sd_ready"))

        def dve_norm(v, o, n, high=None, lo=None):
            v.wait_ge(sem("ss_done"), n + 1)
            o.do(v.tensor_scalar(rs[:], ps[7][:, 0:T], 1.0 / D, EPS, ALU.mult, ALU.add), sem("ms_ready"))
            v.wait_ge(sem("sd_ready"), n + 1)
            newton(v, o, rstd[:], rs[:], gel[:, 0, :])
            if high is not None and n == 1:
                v.wait_ge(sem("h_spilled"), 16)

            def lower(k):
                v.wait_ge(sem("n_high"), (n - 1) * KD + k + 1)
                o.do(v.tensor_tensor(lo[:, k, :], gel[:, k % 2, :], high[:, k, :].bitcast(F32), ALU.subtract),
                     sem("n_ready"))

            for k in range(KD):
                to = nT[:, k, :] if high is None else gel[:, k % 2, :]
                if high is not None and k >= 2:
                    v.wait_ge(sem("n_ready"), n * KD + k - 1)
                o.do(v.scalar_tensor_tensor(to, hT[:, k, :], gv[:, 16 * n + k:16 * n + k + 1], rstd[:],
                                            ALU.mult, ALU.mult), sem("n_ready" if high is None else "n_full"))
                if high is not None and k:
                    lower(k - 1)
            if high is not None:
                lower(KD - 1)

        def act_norm_high(act, o, n, high):
            for k in range(KD):
                act.wait_ge(sem("n_full"), (n - 1) * KD + k + 1)
                o.do(act.copy(high[:, k, :], gel[:, k % 2, :]), sem("n_high"))

        def newton(v, o, r, x, t):
            o.settle()
            o.do(v.reciprocal(r, r))
            o.settle()
            o.do(v.tensor_tensor(t, r, r, ALU.mult))
            o.settle()
            o.do(v.scalar_tensor_tensor(t, t, -0.5, x, ALU.mult, ALU.mult))
            o.settle()
            o.do(v.scalar_tensor_tensor(r, t, 1.5, r, ALU.add, ALU.mult))
            o.settle()

        def in_pairs(eng, name, quarter, evac, per=None, o=None):
            base, n = TRIPLE[name]
            ev = evac or (lambda i, c, s: None)
            lead = 1 if base == 0 else 0
            quarter(0, 0, 0, 0 if base == 0 else 9)
            if lead:
                quarter(0, 1, 1, 1)
                ev(0, 0, 0)
                quarter(0, 2, 0, 9)
                ev(0, 1, 1)
            with eng.Fori(lead, n // 2 - 1) as i:
                if o is not None:
                    o.loop(i, per)
                quarter(i, 1, 1, 9)
                ev(i, 0, 0)
                quarter(i, 2, 0, 9)
                ev(i, 1, 1)
                if o is not None:
                    o.leave(n // 2 - 1 - lead)
            e = n // 2 - 1
            quarter(e, 1, 1, 9)
            ev(e, 0, 0)
            ev(e, 1, 1)

        def tiles(sp, name, src):
            base, n = TRIPLE[name]
            lead = 0
            if base == 0:
                sp.wait_ge(sem("mm_done"), 2 * (STREAM["glu"][0] + STREAM["glu"][1]))
                for s in range(2):
                    sp.dma_start(natural[s].rearrange("p (k n) -> p k n", n=P), src(0, s)).then_inc(sem(f"nat_in{s}"), 16)
                lead = 1
            with sp.Fori(lead, n // 2) as i:
                for s in range(2):
                    sp.wait_ge(sem("low_done"), i * 8 + 4 * (base + s - 1))
                    sp.dma_start(natural[s].rearrange("p (k n) -> p k n", n=P), src(i, s)).then_inc(sem(f"nat_in{s}"), 16)

        def three(pe, bank, slot, k, rhs_h, rhs_l, start, stop):
            j = (k % 4) * P
            w_h, w_l = part_h[:, slot, j:j + P], part_l[:, slot, j:j + P]
            pe.matmul(bank, w_h, rhs_h, start=start, stop=False)
            pe.matmul(bank, w_h, rhs_l, start=False, stop=False)
            return pe.matmul(bank, w_l, rhs_h, start=False, stop=stop)

        def pe_quarter(pe, name, i, c, s, q, head, rhs_h, rhs_l):
            base, _ = TRIPLE[name]
            pe.wait_ge(sem("low_done"), i * 8 + (4 * (base + c) + q + 1))
            if q == 0 and head > 1:
                pe.wait_ge(sem("tile_freed"), i * 2 + (base + c - 1))
            for k in range(4 * q, 4 * q + 4):
                m = three(pe, ps[4 + s][:, 0:T], q, k, rhs_h[:, k, :], rhs_l[:, k, :], k == 0, k == KD - 1)
            m.then_inc(sem("q_used"), 1)

        def pe_triple(pe, name, rhs_h, rhs_l):
            def quarter(i, c, s, head):
                for q in range(4):
                    pe_quarter(pe, name, i, c, s, q, head, rhs_h, rhs_l)
            in_pairs(pe, name, quarter, None)

        def high_parts(act, o, name, evac, per):
            base, _ = TRIPLE[name]

            def quarter(i, c, s, head):
                act.wait_ge(sem(f"nat_in{s}"), i * 16 + 16 * ((base + c) // 2 + 1))
                for q in range(4):
                    if head > 0:
                        act.wait_ge(sem("q_used"), i * 8 + (4 * (base + c) + q - 3))
                    o.do(act.copy(part_h[:, q, :], natural[s][:, 512 * q:512 * q + 512]), sem("high_done"))
            in_pairs(act, name, quarter, evac, {"high_done": 8, **per}, o)
            o.open = {}

        def low_parts(v, o, name, bank, evac, per):
            base, _ = TRIPLE[name]

            def quarter(i, c, s, head):
                for q in range(4):
                    v.wait_ge(sem("high_done"), i * 8 + (4 * (base + c) + q + 1))
                    src = natural[s][:, 512 * q:512 * q + 512] if bank is None else bank(q)
                    o.do(v.tensor_tensor(part_l[:, q, :], src, part_h[:, q, :].bitcast(F32), ALU.subtract),
                         sem("low_done"))
            in_pairs(v, name, quarter, evac, {"low_done": 8, **per}, o)
            o.open = {}

        o_act = Own(None, sem("act_own"))

        def dve_s5_setup(v, o):
            R = [r32[0:NJ, q, :] for q in range(16)]
            Ar, Ai, dre, th, mag, sn, sh, k, c, t, are, aim, fre, fim = R[:14]
            v.wait_ge(sem("s5_in"), 16 * 9)
            v.wait_ge(sem("dt_ready"), 1)
            for src, dst in ((Ar, dre), (Ai, th)):
                for g in range(2):
                    o.do(v.tensor_scalar(dst[:, g * SP_:(g + 1) * SP_], src[:, g * SP_:(g + 1) * SP_],
                                         dtr[0:NJ, g:g + 1], None, ALU.mult))
            o.settle()
            MAGIC = 1.5 * 2.0 ** 23
            o.do(v.tensor_scalar(k, th, 1.0 / (2 * math.pi), MAGIC, ALU.mult, ALU.add))
            o.settle()
            o.do(v.tensor_scalar(k, k, MAGIC, None, ALU.subtract))
            c1 = 6.28125
            c2 = 0.0019350051879882812
            c3 = 2 * math.pi - c1 - c2
            for cc in (c1, c2, c3):
                o.settle()
                o.do(v.scalar_tensor_tensor(th, k, -cc, th, ALU.mult, ALU.add))
            o.settle()
            o.do(v.tensor_scalar(th, th, 3.1415925, -3.1415925, ALU.min, ALU.max), sem("theta_ready"))
            o.do(v.tensor_reduce(par[:, 4:5], par[:, 0:4], AX.X, ALU.max))
            o.settle()
            o.do(v.tensor_scalar(par[:, 5:6], par[:, 4:5], -1.0, 1.0, ALU.mult, ALU.add))
            o.do(v.tensor_scalar(par[:, 6:7], par[:, 4:5], -1.0, None, ALU.mult))
            o.settle()
            o.do(v.tensor_scalar(par[:, 7:8], par[:, 5:6], -1.0, None, ALU.mult))
            o.settle()
            for q in range(2):
                for g in range(2):
                    o.do(v.tensor_scalar(Cbd[q][:, :, g, :], Cn[q], par[:, 4 + g + 2 * q:5 + g + 2 * q], None, ALU.mult))
                o.do(v.memset(Bbd[q], 0.0))
            v.wait_ge(sem("trig_ready"), 1)
            o.do(v.tensor_tensor(c, sh, sh, ALU.mult))
            o.do(v.tensor_tensor(aim, mag, sn, ALU.mult))
            o.do(v.tensor_tensor(fre, Ar, Ar, ALU.mult))
            o.do(v.tensor_tensor(fim, Ai, Ai, ALU.mult))
            o.settle()
            o.do(v.tensor_scalar(c, c, -2.0, 1.0, ALU.mult, ALU.add))
            o.do(v.tensor_tensor(t, fre, fim, ALU.add))
            o.settle()
            o.do(v.tensor_tensor(are, mag, c, ALU.mult))
            o.do(v.reciprocal(t, t))
            o.settle()
            o.do(v.tensor_scalar(k, are, 1.0, None, ALU.subtract))
            o.do(v.tensor_tensor(fre, aim, Ai, ALU.mult))
            o.do(v.tensor_tensor(fim, aim, Ar, ALU.mult))
            o.settle()
            o.do(v.tensor_tensor(c, k, Ar, ALU.mult))
            o.do(v.tensor_tensor(k, k, Ai, ALU.mult))
            o.settle()
            o.do(v.tensor_tensor(fre, fre, c, ALU.add))
            o.do(v.tensor_tensor(fim, fim, k, ALU.subtract))
            o.settle()
            o.do(v.tensor_tensor(fre, fre, t, ALU.mult))
            o.do(v.tensor_tensor(fim, fim, t, ALU.mult), sem("abf_rows"))
            v.wait_ge(sem("gate_done"), 1)
            v.wait_ge(sem("vec_in"), 16 * 9)
            o.do(v.tensor_scalar(rows8, ps[5][0:8, 0:T], gb8[:, 0:1], None, ALU.add), sem("gate_copied"))
            v.wait_ge(sem("abf_done"), 1)
            o.do(v.tensor_copy(abT, ps[4][:, 0:4 * NJ].rearrange("p (a b) -> p a b", a=4)), sem("abf_copied"))
            o.settle()
            fr, fi = bc(abT[:, 2, :], GC), bc(abT[:, 3, :], GC)
            o.do(v.tensor_tensor(tB[0], Bn[0], fr, ALU.mult))
            o.do(v.tensor_tensor(tB[1], Bn[1], fi, ALU.mult))
            o.do(v.tensor_tensor(tB[2], Bn[1], fr, ALU.mult))
            o.do(v.tensor_tensor(tB[3], Bn[0], fi, ALU.mult))
            o.settle()
            for q, op in ((0, ALU.subtract), (1, ALU.add)):
                for g in range(2):
                    sl = slice(g * SP_, (g + 1) * SP_)
                    o.do(v.tensor_tensor(Bbd[q][sl, :, g, :], tB[2 * q][sl], tB[2 * q + 1][sl], op))
            o.settle()
            o.do(v.tensor_copy(par[:, 0:1], par[:, 0:1]), sem("bd_ready"))
            o.do(v.tensor_copy(par[:, 1:2], par[:, 1:2]), sem("bd_ready"))

        def cmul_add(v, o, dst, a, src, tmp):
            o.do(v.tensor_tensor(tmp[0], a[0], src[0], ALU.mult))
            o.do(v.tensor_tensor(tmp[1], a[1], src[1], ALU.mult))
            o.do(v.tensor_tensor(tmp[2], a[0], src[1], ALU.mult))
            o.do(v.tensor_tensor(tmp[3], a[1], src[0], ALU.mult))
            o.settle()
            o.do(v.tensor_tensor(dst[0], dst[0], tmp[0], ALU.add))
            o.do(v.tensor_tensor(dst[1], dst[1], tmp[2], ALU.add))
            o.settle()
            o.do(v.tensor_tensor(dst[0], dst[0], tmp[1], ALU.subtract))
            o.do(v.tensor_tensor(dst[1], dst[1], tmp[3], ALU.add))
            o.settle()

        def cmul(v, o, dst, a, src, tmp):
            o.do(v.tensor_tensor(tmp[0], a[0], src[0], ALU.mult))
            o.do(v.tensor_tensor(tmp[1], a[1], src[1], ALU.mult))
            o.do(v.tensor_tensor(tmp[2], a[0], src[1], ALU.mult))
            o.do(v.tensor_tensor(tmp[3], a[1], src[0], ALU.mult))
            o.settle()
            o.do(v.tensor_tensor(dst[0], tmp[0], tmp[1], ALU.subtract))
            o.do(v.tensor_tensor(dst[1], tmp[2], tmp[3], ALU.add))
            o.settle()

        CMUL = 8

        def dve_s5_scan(v, o):
            o.settle()
            v.wait_ge(sem("s0_copied"), 1)
            a = [abT[:, 0, :], abT[:, 1, :]]
            pw = [a16[:, 0, :], a16[:, 1, :]]
            g2 = [a16[:, 2, :], a16[:, 3, :]]
            ts = [t[:, :, 0] for t in tS]
            cmul(v, o, pw, a, a, ts)
            for _ in range(3):
                cmul(v, o, pw, pw, pw, ts)
            smp = [s[:, :, TP:T].rearrange("p j (b s) -> p s j b", s=NS) for s in st]
            s0 = [s0T[:, q, :].rearrange("p (b j) -> p j b", j=NJ) for q in range(2)]
            aB = [bc(x, NB) for x in a]
            for s in range(NS):
                src = s0 if s == 0 else [x[:, s - 1] for x in smp]
                cmul_add(v, o, [x[:, s] for x in smp], aB, src, [t[:, :, 0:NB] for t in tS])
            chk = [s[:, :, 0:TP].rearrange("p j (k t) -> p t j k", t=CH) for s in st]
            aC = [bc(x, NCH).unsqueeze(1) for x in a]
            tC = [t.unsqueeze(1) for t in tS]
            with v.Fori(0, CH - 1) as i:
                o.loop(i, {"dve_own": CMUL})
                cmul_add(v, o, [x[:, ds(i + 1, 1)] for x in chk], aC, [x[:, ds(i, 1)] for x in chk], tC)
                o.leave(CH - 1)
            end = [s[:, :, CH - 1:TP:CH] for s in st]
            with v.Fori(0, NCH - 1) as i:
                o.loop(i, {"dve_own": CMUL})
                cmul_add(v, o, [x[:, :, ds(i + 1, 1)] for x in end], [x.unsqueeze(2) for x in pw],
                         [x[:, :, ds(i, 1)] for x in end], [t[:, :, 0:1] for t in tS])
                o.leave(NCH - 1)
            for q in range(2):
                o.do(v.tensor_copy(g2[q], a[q]))
            o.settle()
            n = NCH - 1
            prev = [x[:, :, 0:n].unsqueeze(1) for x in end]
            with v.Fori(0, CH - 1) as i:
                o.loop(i, {"dve_own": CMUL + 6})
                cmul_add(v, o, [x[:, ds(i, 1), :, 1:NCH] for x in chk], [bc(x, n).unsqueeze(1) for x in g2], prev,
                         [t[:, :, 0:n].unsqueeze(1) for t in tS])
                cmul(v, o, g2, g2, a, ts)
                o.leave(CH - 1)
            for q in range(2):
                o.do(v.tensor_copy(send[:, q, 0, :], st[q][:, :, TP - 1]))
                o.do(v.tensor_copy(send[:, q, 1:1 + NB, :],
                                   st[q][:, :, TP + NS - 1:T:NS].rearrange("p j b -> p b j")))
            o.settle()
            o.do(v.tensor_copy(g2[0], g2[0]), sem("s5_ready"))
            o.do(v.tensor_copy(g2[1], g2[1]), sem("send_ready"))

        CR = [wk(4096 * i, NB, 2, DH) for i in range(2)]
        ktok = wk(8192, 3, MW)
        vtok = wk(11264, 3, MW)
        kwm = wk(14336, NB, DH)
        S_ = [wk(16384 + 416 * i, 1, 416)[:, 0, :] for i in range(2)]
        n0r = wk(17216, 1, P)[:, 0, :]
        n0T = wk(17344, NB, H, 2)
        ncol = wk(17408, 9, H, 2)
        nrow = wk(17480, 1, P)[:, 0, :]
        m0b = wk(17608, NB, H)
        qn = wk(17640, 4, 2, TS)
        w0 = wk(17896, H, TS)
        ntmp = wk(18024, NB, 2)
        exf = wk(O_EX, 8, T)
        rI, rF = exf[:, 0:4, :], exf[:, 4:8, :]
        r2, r3 = uT[:, 0:4, :], uT[:, 4:8, :]
        r4, r5, r6, r7 = (nT[:, 4 * i:4 * i + 4, :] for i in range(4))
        hb, hsq = r4[:, 0:2, :], r4[:, 2:4, :]
        pC = zT[:, 0:8, 0:DH]
        mrow = rows8

        def flat(x):
            return x.rearrange("p a t -> p (a t)")

        def smp4(x):
            return x[:, :, TP:T].rearrange("p h (b s) -> p h b s", s=NS)

        def sp_mlstm(sp):
            sp.wait_ge(sem("sout_ready"), 1)
            for q, (a, b) in enumerate(((5, 10), (6, 11))):
                sp.dma_start(outs[a][0, 0].rearrange("(j g) p -> j (g p)", g=2), sout[0:NJ, q, :]).then_inc(
                    sem("s5_stored"), 16)
                sp.dma_start(outs[b][0].rearrange("b (j g) p -> (b j) (g p)", g=2).rearrange("(t r) q -> r t q", t=2),
                             sout[:, 2 + 2 * q:4 + 2 * q, :]).then_inc(sem("s5_stored"), 16)
            sp.wait_ge(sem("y_sum"), 8)
            mi = sem("ml_in")
            sp.dma_start(n0r[0:64, :], ins["state_mlstm_n"][0].rearrange("b h (c p) -> (b h c) p", p=P)).then_inc(mi, 16)
            sp.dma_start(m0b, ins["state_mlstm_m"][0].partition_broadcast(P)).then_inc(mi, 16)

            def c_load(h):
                if h >= 2:
                    sp.wait_ge(sem(f"c_out{h % 2}"), 16 * NB * (h // 2))
                for b in range(NB):
                    sp.dma_start(CR[h % 2][:, b], ins["state_mlstm_C"][0, b, h].rearrange("(c p) e -> p c e", p=P)
                                 ).then_inc(sem(f"c_in{h % 2}"), 16)

            def c_store(h):
                sp.wait_ge(sem("cn_read"), NB * (h + 1))
                for b in range(NB):
                    sp.dma_start(outs[7][0, b, h].rearrange("(c p) e -> p c e", p=P), CR[h % 2][:, b]).then_inc(
                        sem(f"c_out{h % 2}"), 16)

            c_load(0)
            c_load(1)
            for h in range(H):
                c_store(h)
                if h + 2 < H:
                    c_load(h + 2)
            for h in range(H):
                sp.wait_ge(sem("pc_copied"), h + 1)
                sp.dma_start(outs[2][0, 0, h].rearrange("(c p) e -> p c e", p=P), pC[:, 2 * h:2 * h + 2, :]).then_inc(
                    sem("ml_stored"), 16)
            sp.wait_ge(sem("nrow_copied"), 1)
            sp.dma_start(outs[3][0, 0].rearrange("h (c p) -> (h c) p", p=P), nrow[0:8, :]).then_inc(sem("ml_stored"), 16)
            sp.dma_start(outs[8][0].rearrange("b h (c p) -> (b h c) p", p=P), nrow[8:72, :]).then_inc(sem("ml_stored"), 16)
            sp.wait_ge(sem("mrow_ready"), 1)
            sp.dma_start(outs[4][0], mrow[0:1, 0:4]).then_inc(sem("ml_stored"), 16)
            sp.dma_start(outs[9].rearrange("a b h -> a (b h)"), mrow[0:1, 4:36]).then_inc(sem("ml_stored"), 16)
            sp.wait_ge(sem("s5_stored"), 64)
            sp.wait_ge(sem("ml_stored"), 16 * 8)
            for s in range(2):
                sp.wait_ge(sem(f"c_out{s}"), 16 * NB * 2)

        def pe_mlstm(pe):
            for r in range(8):
                if r == 0:
                    pe.wait_ge(sem("sout_ready"), 1)
                if r >= 4:
                    pe.wait_ge(sem("bc_copied"), r - 3)
                pe.matmul(ps[4 + r % 4][:, 0:T], ident[0:8, r:r + 1].to_broadcast([8, P]), rows8,
                          start=True, stop=True).then_inc(sem("bc_done"), 1)
            pe.wait_ge(sem("ml_in"), 32)
            pe.wait_ge(sem("bc_copied"), 5)
            pe.transpose(ps[4][:, 0:64], n0r[0:64, :], ident[0:64, 0:64]).then_inc(sem("n0_done"), 1)
            pe.wait_ge(sem("mm_freed"), 2 * (STREAM["glu"][0] + 4))
            for g in range(12):
                arr, rest = divmod(g, 6)
                i, half = divmod(rest, 2)
                t0, n = TOK[i]
                if g >= 4:
                    pe.wait_ge(sem("tok_copied"), g - 3)
                for j in range(4):
                    m = pe.transpose(ps[g % 4][0:n, j * P:(j + 1) * P],
                                     zT[:, 8 + 8 * arr + 4 * half + j, t0:t0 + n], ident[:])
                m.then_inc(sem("tok_done"), 1)
            pe.wait_ge(sem("wk_ready"), 1)
            pe.wait_ge(sem("bc_copied"), 8)
            for q, row in enumerate((rI, r7)):
                for i, (t0, n) in enumerate(TOK):
                    for h in range(H):
                        c = 12 * q + 4 * i + h
                        m = pe.matmul(ps[5][0:n, c:c + 1], row[0:1, h, t0:t0 + n], ones[0:1, 0:1], start=True, stop=True)
            m.then_inc(sem("col_done"), 1)
            pe.wait_ge(sem("col_copied"), 1)
            pe.wait_ge(sem("n0_copied"), 1)
            pe.wait_ge(sem("tok_copied"), 12)
            for h in range(H):
                qs = [zT[:, 2 * h + c, :] for c in range(2)]
                ks = [zT[:, 8 + 2 * h + c, :] for c in range(2)]
                if h >= 1:
                    pe.wait_ge(sem("sw_ready"), h)
                for c in range(2):
                    pe.matmul(ps[0][:, 0:256], ks[c][:, 0:128], qs[c][:, 0:256], start=(c == 0), stop=(c == 1))
                for c in range(2):
                    pe.matmul(ps[0][:, 256:384], ks[c][:, 128:256], qs[c][:, 128:256], start=(c == 0), stop=(c == 1))
                for c in range(2):
                    m = pe.matmul(ps[0][0:TS, 384:384 + TS], ks[c][:, TP:T], qs[c][:, TP:T], start=(c == 0), stop=(c == 1))
                m.then_inc(sem("sc_done"), 1)
                S, C, hs = S_[h % 2], CR[h % 2], h % 2
                pe.wait_ge(sem("sw_ready"), h + 1)
                pe.wait_ge(sem("qn_ready"), h + 1)
                pe.wait_ge(sem(f"c_in{h % 2}"), 16 * NB * (h // 2 + 1))
                if h >= 1:
                    pe.wait_ge(sem("hms_ready"), h)
                    pe.wait_ge(sem("hb_ready"), 2 * h)

                def both(bank, lhs, before):
                    pe.matmul(bank[:, 0:128], lhs(0), S[:, 0:128], start=True, stop=True)
                    pe.matmul(bank[:, 128:256], lhs(0), S[:, 128:256], start=True, stop=False)
                    pe.matmul(bank[:, 128:256], lhs(1), S[:, 256:384], start=False, stop=True)
                    before(bank)
                    return pe.matmul(bank[:, TP:T], lhs(2), S[0:TS, 384:416], start=False, stop=True)

                def den_before(bank):
                    for c in range(2):
                        pe.matmul(bank[:, TP:T], ones[:], qn[:, 2 + c, hs, :], start=(c == 0), stop=False)

                both(ps[1], lambda i: ones[0:TOK[i][1], :], den_before).then_inc(sem("den_done"), 1)
                for e in range(2):
                    c0 = h * DH + e * P

                    def num_before(bank):
                        for b in range(NB):
                            for c in range(2):
                                pe.matmul(bank[:, TP + NS * b:TP + NS * (b + 1)], C[:, b, c, e * P:(e + 1) * P],
                                          qn[:, c, hs, NS * b:NS * (b + 1)], start=(b == 0 and c == 0), stop=False)

                    both(ps[2 + e], lambda i: vtok[0:TOK[i][1], i, c0:c0 + P], num_before).then_inc(sem("num_done"), 1)
                pe.wait_ge(sem("kw_ready"), 1)
                if h >= 1:
                    pe.wait_ge(sem("pc_copied"), h)
                    pe.wait_ge(sem("nc_read"), h)
                for c in range(2):
                    for i in range(2):
                        pe.matmul(ps[4][:, c * DH:(c + 1) * DH], ktok[:, i, h * DH + c * P:h * DH + (c + 1) * P],
                                  vtok[:, i, h * DH:(h + 1) * DH], start=(i == 0), stop=(i == 1))
                for c in range(2):
                    for i in range(2):
                        m = pe.matmul(ps[5][:, c:c + 1], ktok[:, i, h * DH + c * P:h * DH + (c + 1) * P],
                                      ones[:, 0:1], start=(i == 0), stop=(i == 1))
                m.then_inc(sem("pc_done"), 1)
                pe.wait_ge(sem("kwm_ready"), h + 1)
                for b in range(NB):
                    at = NB * h + b
                    if at >= 2:
                        pe.wait_ge(sem("cn_read"), at - 1)
                    bank = ps[6 + at % 2]
                    for c in range(2):
                        pe.matmul(bank[:, c * DH:(c + 1) * DH], kwm[0:TS, b, c * P:(c + 1) * P],
                                  vtok[0:TS, 2, h * DH:(h + 1) * DH], start=True, stop=True)
                    for c in range(2):
                        m = pe.matmul(ps[5][:, 2 + 2 * b + c:3 + 2 * b + c], kwm[0:TS, b, c * P:(c + 1) * P],
                                      ones[0:TS, 0:1], start=True, stop=True)
                    m.then_inc(sem("cn_done"), 1)
                pe.wait_ge(sem("hsq_done"), h + 1)
                for e in range(2):
                    m = pe.matmul(ps[1][:, 0:T], ones[:], hsq[:, e, :], start=(e == 0), stop=(e == 1))
                m.then_inc(sem("hss_done"), 1)
            pe.wait_ge(sem("nc_read"), H)
            pe.transpose(ps[5][0:72, 0:P], ncol.rearrange("p a b c -> p (a b c)"), ident[:]).then_inc(sem("nrow_done"), 1)

        def act_mlstm(act, o):
            act.wait_ge(sem("s5_stored"), 64)
            for r in range(8):
                act.wait_ge(sem("bc_done"), r + 1)
                o.do(act.copy(exf[:, r, :], ps[4 + r % 4][:, 0:T]), sem("bc_copied"))
            o.settle()
            act.wait_ge(sem("glu_ready"), 8)
            o.do(act.activation(r2, rF, ACT.Abs))
            o.settle()
            o.do(act.activation(r2, r2, ACT.Exp, scale=-1.0))
            o.settle()
            o.do(act.activation(r2, r2, ACT.Ln, bias=1.0), sem("ln_ready"))
            act.wait_ge(sem("n0_done"), 1)
            o.do(act.copy(n0T.rearrange("p a b c -> p (a b c)"), ps[4][:, 0:64]), sem("n0_copied"))
            for g in range(12):
                arr, rest = divmod(g, 6)
                i, half = divmod(rest, 2)
                n = TOK[i][1]
                act.wait_ge(sem("tok_done"), g + 1)
                dst = [ktok, vtok][arr]
                o.do(act.copy(dst[0:n, i, 512 * half:512 * half + 512], ps[g % 4][0:n, 0:512]), sem("tok_copied"))
            act.wait_ge(sem("m_ready"), 1)
            o.settle()
            o.do(act.activation(r2, r6, ACT.Exp, scale=-1.0))
            o.do(act.activation(w0, w0, ACT.Exp))
            o.do(act.activation(r7, r7, ACT.Exp), sem("wk_ready"))
            for h in range(H):
                S = S_[h % 2]
                act.wait_ge(sem("sarg_ready"), h + 1)
                o.do(act.activation(S[:, 0:384], S[:, 0:384], ACT.Exp, scale=-1.0))
                o.do(act.activation(S[0:TS, 384:416], S[0:TS, 384:416], ACT.Exp, scale=-1.0), sem("sexp_ready"))
                act.wait_ge(sem("pc_done"), h + 1)
                o.do(act.copy(pC[:, 2 * h:2 * h + 2, :], ps[4][:, 0:512].rearrange("p (a b) -> p a b", a=2)),
                     sem("pc_copied"))
                act.wait_ge(sem("hb_ready"), 2 * h + 2)
                if h >= 1:
                    act.wait_ge(sem("hss_done"), h)
                o.do(act.activation(hsq, hb, ACT.Square), sem("hsq_done"))
                act.wait_ge(sem("hms_ready"), h + 1)
                o.do(act.activation(rstd[:], rs[:], ACT.Sqrt), sem("hsd_ready"))
            act.wait_ge(sem("nrow_done"), 1)
            o.do(act.copy(nrow[0:72, :], ps[5][0:72, 0:P]), sem("nrow_copied"))

        def split_mix(v, o, c0, n, name):
            o.settle()
            for c in range(c0, c0 + n):
                o.do(v.tensor_copy(mix_h[:, c, :], mix[:, c, :]))
            o.settle()
            for c in range(c0, c0 + n):
                o.do(v.tensor_tensor(mix_l[:, c, :], mix[:, c, :], mix_h[:, c, :].bitcast(F32), ALU.subtract), sem(name))

        def dve_mlstm(v, o):
            v.wait_ge(sem("mm_done"), 2 * (STREAM["z"][0] + STREAM["z"][1]))
            v.wait_ge(sem("ln_ready"), 1)
            v.wait_ge(sem("ml_in"), 32)
            o.settle()
            o.do(v.memset(r7, 1.0))
            o.do(v.scalar_tensor_tensor(flat(rF), flat(rF), 0.0, flat(r2), ALU.min, ALU.subtract))
            o.settle()
            o.do(v.memset(r7[:, :, 0:1], 0.0))
            o.do(v.memset(r7[:, :, TP:T:NS], 0.0))
            o.settle()
            o.do(v.tensor_tensor_scan(flat(r3), flat(r7), flat(rF), 0.0, ALU.mult, ALU.add))
            o.settle()
            o.do(v.tensor_tensor(flat(rI), flat(rI), flat(r3), ALU.subtract))
            o.do(v.tensor_scalar(flat(r7), flat(r7), 1.0, -NEG, ALU.subtract, ALU.mult))
            o.settle()
            o.do(v.tensor_copy(flat(r4), flat(rI)))
            o.settle()
            o.do(v.tensor_scalar(r4[:, :, 0:1], r4[:, :, 0:1], 0.0, None, ALU.max))
            first = r4[:, :, TP:T:NS]
            o.do(v.tensor_tensor(first, first, m0b.rearrange("p b h -> p h b"), ALU.max))
            o.settle()
            o.do(v.tensor_tensor_scan(flat(r5), flat(r7), flat(r4), 0.0, ALU.add, ALU.max))
            o.settle()
            o.do(v.tensor_tensor(flat(r6), flat(r3), flat(r5), ALU.add))
            w4 = w0.rearrange("p h (b s) -> p h b s", s=NS)
            o.do(v.tensor_tensor(w4, bc(m0b.rearrange("p b h -> p h b"), NS), smp4(r5), ALU.subtract))
            o.do(v.tensor_tensor(r7[:, :, 0:TP], rI[:, :, 0:TP], r5[:, :, TP - 1:TP].to_broadcast([P, H, TP]),
                                 ALU.subtract))
            o.do(v.tensor_tensor(smp4(r7), smp4(rI), smp4(r5)[:, :, :, NS - 1:NS].to_broadcast([P, H, NB, NS]),
                                 ALU.subtract))
            o.settle()
            o.do(v.tensor_copy(mrow[0:1, 0:4], r6[0:1, :, TP - 1]), sem("m_ready"))
            v.wait_ge(sem("bc_done"), 8)
            o.do(v.tensor_copy(mrow[0:1, 4:36].rearrange("p (b h) -> p b h", h=H),
                               r6[0:1, :, TP + NS - 1:T:NS].rearrange("p h b -> p b h")), sem("mrow_ready"))
            v.wait_ge(sem("col_done"), 1)
            for q in range(2):
                o.do(v.tensor_copy(cols[:, 12 * q:12 * q + 8], ps[5][:, 12 * q:12 * q + 8]))
                o.do(v.tensor_copy(cols[0:TS, 12 * q + 8:12 * q + 12], ps[5][0:TS, 12 * q + 8:12 * q + 12]))
            o.settle()
            v.wait_ge(sem("tok_copied"), 12)
            for i in range(3):
                for h in range(H):
                    n = TOK[i][1]
                    a = ktok[0:n, i, h * DH:(h + 1) * DH]
                    s = sem("col_copied") if (i, h) == (0, 0) else sem("kw_ready") if (i, h) == (2, H - 1) else None
                    o.do(v.tensor_scalar(a, a, cols[0:n, 12 + 4 * i + h:13 + 4 * i + h], DH ** -0.5, ALU.mult, ALU.mult), s)
            o.settle()
            split_mix(v, o, 8, 8, "ys_split")
            v.wait_ge(sem("n0_copied"), 1)
            for h in range(H):
                S, hs = S_[h % 2], h % 2
                if h >= 2:
                    v.wait_ge(sem("num_done"), 2 * (h - 1))
                for i, (lo, hi, t0) in enumerate(((0, 256, 0), (256, 384, 128), (384, 416, TP))):
                    n = TOK[i][1]
                    o.do(v.tensor_scalar(S[0:n, lo:hi], r5[0:n, h, t0:t0 + hi - lo], cols[0:n, 4 * i + h:4 * i + h + 1],
                                         0.0, ALU.subtract, ALU.max), sem("sarg_ready") if i == 2 else None)
                qs = zT[:, 2 * h:2 * h + 2, TP:T]
                o.do(v.tensor_tensor(qn[:, 0:2, hs, :], qs, w0[:, h:h + 1, :].to_broadcast([P, 2, TS]), ALU.mult))
                o.settle()
                for c in range(2):
                    o.do(v.tensor_tensor(qn[:, 2 + c, hs, :].rearrange("p (b s) -> p b s", s=NS),
                                         qn[:, c, hs, :].rearrange("p (b s) -> p b s", s=NS), bc(n0T[:, :, h, c], NS),
                                         ALU.mult), sem("qn_ready") if c == 1 else None)
                if h >= 1:
                    v.wait_ge(sem("cn_done"), NB * h)
                o.do(v.tensor_tensor(kwm[0:TS], ktok[0:TS, 2:3, h * DH:(h + 1) * DH].to_broadcast([TS, NB, DH]),
                                     bc(bmask, DH), ALU.mult), sem("kwm_ready"))
                v.wait_ge(sem("sexp_ready"), h + 1)
                v.wait_ge(sem("sc_done"), h + 1)
                o.do(v.scalar_tensor_tensor(S[:, 0:384], ps[0][:, 0:384], DH ** -0.5, S[:, 0:384], ALU.mult, ALU.mult))
                o.do(v.scalar_tensor_tensor(S[0:TS, 384:416], ps[0][0:TS, 384:416], DH ** -0.5, S[0:TS, 384:416],
                                            ALU.mult, ALU.mult))
                o.settle()
                o.do(v.tensor_tensor(S[:, 0:128], S[:, 0:128], tri, ALU.mult))
                o.do(v.tensor_tensor(S[:, 256:384], S[:, 256:384], tri, ALU.mult))
                o.do(v.tensor_tensor(S[0:TS, 384:416], S[0:TS, 384:416], trs, ALU.mult), sem("sw_ready"))
                v.wait_ge(sem("den_done"), h + 1)
                o.do(v.tensor_tensor(rs[:], ps[1][:, 0:T], r2[:, h, :], ALU.max))
                o.settle()
                o.do(v.scalar_tensor_tensor(rs[:], ps[1][:, 0:T], -1.0, rs[:], ALU.mult, ALU.max))
                o.settle()
                o.do(v.reciprocal(rs[:], rs[:]))
                o.settle()
                for e in range(2):
                    v.wait_ge(sem("num_done"), 2 * h + e + 1)
                    o.do(v.tensor_tensor(hb[:, e, :], ps[2 + e][:, 0:T], rs[:], ALU.mult), sem("hb_ready"))
                for b in range(NB):
                    v.wait_ge(sem("cn_done"), NB * h + b + 1)
                    cs = CR[h % 2][:, b].rearrange("p a b -> p (a b)")
                    o.do(v.scalar_tensor_tensor(cs, cs, w0[:, h, NS * b + NS - 1:NS * b + NS],
                                                ps[6 + b % 2][:, 0:512], ALU.mult, ALU.add), sem("cn_read"))
                o.do(v.tensor_copy(ncol[:, 0, h, :], ps[5][:, 0:2]))
                o.do(v.tensor_tensor(ntmp, n0T[:, :, h, :], bc(w0[:, h, NS - 1:TS:NS], 2), ALU.mult))
                o.settle()
                o.do(v.tensor_tensor(ncol[:, 1:9, h, :], ntmp, ps[5][:, 2:18].rearrange("p (a b) -> p a b", b=2),
                                     ALU.add), sem("nc_read"))
                v.wait_ge(sem("hss_done"), h + 1)
                o.do(v.tensor_scalar(rs[:], ps[1][:, 0:T], 1.0 / DH, EPS, ALU.mult, ALU.add), sem("hms_ready"))
                v.wait_ge(sem("hsd_ready"), h + 1)
                newton(v, o, rstd[:], rs[:], r7[:, 0, :])
                for e in range(2):
                    o.do(v.scalar_tensor_tensor(hb[:, e, :], hb[:, e, :], gv[:, 64 + 2 * h + e:65 + 2 * h + e], rstd[:],
                                                ALU.mult, ALU.mult))
                o.settle()
                v.wait_ge(sem("og_ready"), 1)
                for e in range(2):
                    o.do(v.tensor_tensor(mix[:, 2 * h + e, :], hb[:, e, :], zT[:, 24 + 2 * h + e, :], ALU.mult))
                split_mix(v, o, 2 * h, 2, "hm_ready")

        qpT = wk(0, 8, T)
        keyn = wk(2304, 16, 64)
        keyT = wk(3328, PH, PK)
        scr = wk(4352, 3, 16 * PK)
        tv = wk(10496, 16, TK)
        ti = work[:, 10752:11008].bitcast(U32).rearrange("p (a b) -> p a b", b=TK)
        tf = wk(11008, 16, TK)
        cand = wk(11264, PH, TK, TK)
        vs = wk(13312, PH, TK)
        ic = work[:, 13440:13568].bitcast(U32)
        ia = work[:, 13568:13696].bitcast(U32)
        iF = [wk(13696, 1, P)[:, 0, :], wk(13824, 1, P)[:, 0, :]]
        eq = wk(13952, PH, TK, TK)
        tok3 = wk(16000, 3, 3, P)
        gsum = wk(17152, 2, PH)
        dense = wk(0, P, T)
        ohA = [ring[:, 1, 512 * s:512 * s + 512].rearrange("p (a b) -> p a b", b=P) for s in range(2)]
        ohB = [ring[:, 1, 1024 + 512 * s:1536 + 512 * s].rearrange("p (a b) -> p a b", b=P) for s in range(2)]
        u_v = ins["peer_u"][0].rearrange("(a b) d -> a b d", b=PK)
        v_v = ins["peer_v"][0].rearrange("(a b) d -> a b d", b=PK)
        WQ_END = sum(TRIPLE["wq"])
        UB = TRIPLE["U"][0]
        vh = alias("v_high", ring_at + 16384, 2, 1024)
        vl = alias("v_low", ring_at + 16384 + 8192, 2, 1024)
        NP_ = 36

        def sp_peer(sp):
            sp.wait_ge(sem("q_used"), 4 * KD)
            sp.dma_start(keyn, ins["peer_keys"][0].rearrange("h c k d -> k (h c) d")).then_inc(sem("key_in"), 16)
            sp.wait_ge(sem("low_done"), 4 * WQ_END)
            for s in range(2):
                sp.dma_start(natural[s], u_v[:, s, :]).then_inc(sem(f"nat_in{s}"), 16)
            with sp.Fori(1, PK // 2) as i:
                for s in range(2):
                    sp.wait_ge(sem("turned"), i * 8 + (4 * s - 4))
                    sp.dma_start(natural[s], u_v[:, ds(i * 2 + s, 1), :].rearrange("a b d -> a (b d)")).then_inc(
                        sem(f"nat_in{s}"), 16)
            sp.wait_ge(sem("turned"), 4 * PK)
            for half in range(2):
                cs = slice(half * 1024, half * 1024 + 1024)
                first = 0
                if half == 0:
                    for s in range(2):
                        sp.dma_start(natural[s].rearrange("p (a b) -> p a b", a=2), v_v[:, 2 * s:2 * s + 2, cs]).then_inc(
                            sem(f"v_in{s}"), 16)
                    sp.wait_ge(sem("q_used"), 4 * (UB + PK))
                    sp.dma_start(low[:, 0:KD * T], spill).then_inc(sem("h_back"), 16)
                    first = 1
                with sp.Fori(first, 32) as i:
                    for s in range(2):
                        sp.wait_ge(sem("vl_done"), i * 4 + (128 * half + 2 * s - 2))
                        sp.dma_start(natural[s].rearrange("p (a b) -> p a b", a=2), v_v[:, ds(i * 4 + 2 * s, 2), cs]).then_inc(
                            sem(f"v_in{s}"), 16)

        def pe_peer(pe):
            pe.wait_ge(sem("key_in"), 16)
            for g in range(2):
                for j in range(4):
                    h = 4 * g + j
                    m = pe.transpose(ps[g][:, j * P:(j + 1) * P], keyn[:, 2 * h:2 * h + 2, :].rearrange("p a b -> p (a b)"),
                                     ident[:])
                m.then_inc(sem("key_done"), 1)
            pe.wait_ge(sem("key_copied"), 2)
            pe.wait_ge(sem("tile_freed"), WQ_END)
            for i, (t0, n) in enumerate(TOK):
                for g in range(2):
                    if i:
                        pe.wait_ge(sem("scr_copied"), 4 * (i - 1) + 2 * g + 2)
                    for j in range(4):
                        for c in range(2):
                            m = pe.matmul(ps[2 * g + c][0:n, j * P:(j + 1) * P],
                                          qpT[64 * c:64 * c + 64, 4 * g + j, t0:t0 + n],
                                          keyT[64 * c:64 * c + 64, 4 * g + j, :], start=True, stop=True)
                            if j == 3:
                                m.then_inc(sem("scr_done"), 1)
            for i, (t0, n) in enumerate(TOK):
                pe.wait_ge(sem("tok3_ready"), i + 1)
                for q in range(3):
                    m = pe.transpose(ps[4 + q][:, t0:t0 + n], tok3[0:n, i, q, :], ident[0:n, 0:n])
            m.then_inc(sem("ex3_done"), 1)

            def spread(i, s, first):
                pe.wait_ge(sem("oh_ready"), i * 2 + (s + 1))
                if not first:
                    pe.wait_ge(sem("g_copied"), i * 2 + (s - 1))
                for j in range(4):
                    m = pe.matmul(ps[s][:, j * P:(j + 1) * P], ohA[s][:, j, :], ohB[s][:, j, :], start=True, stop=True)
                m.then_inc(sem("g_done"), 1)

            pe.wait_ge(sem("scr_copied"), 12)
            for s in range(2):
                spread(0, s, True)
            with pe.Fori(1, NP_) as i:
                for s in range(2):
                    spread(i, s, False)
            pe.wait_ge(sem("g_copied"), 2 * NP_)

            def turn(i, c, s, q, first=False):
                if q == 0:
                    pe.wait_ge(sem(f"nat_in{s}"), i * 16 + 16 * ((UB + c) // 2 + 1))
                if not first:
                    pe.wait_ge(sem("low_done"), i * 8 + (4 * (UB + c) + q - 3))
                for j in range(4):
                    k = 4 * q + j
                    m = pe.transpose(ps[q][:, j * P:(j + 1) * P], natural[s][:, k * P:(k + 1) * P], ident[:])
                m.then_inc(sem("turned"), 1)

            def dots(i, c, s, last=False):
                for q in range(4):
                    if q < 2:
                        turn(i, c, s, q + 2)
                    elif not last:
                        turn(i, c + 1, 1 - s, q - 2)
                    pe_quarter(pe, "U", i, c, s, q, 9, ffn_h, ffn_l)

            turn(0, 0, 0, 0, True)
            turn(0, 0, 0, 1, True)
            with pe.Fori(0, PK // 2 - 1) as i:
                dots(i, 0, 0)
                dots(i, 1, 1)
            dots(PK // 2 - 1, 0, 0)
            dots(PK // 2 - 1, 1, 1, True)

            pe.wait_ge(sem("tile_freed"), UB + PK)
            for half in range(2):
                if half:
                    pe.wait_ge(sem("pv_added"), 8)

                def pair(i, kind):
                    for s in range(2):
                        pe.wait_ge(sem("vl_done"), i * 2 + (128 * half + s + 1))
                        pe.wait_ge(sem("al_done"), i * 2 + (128 * half + s + 1))
                        st_, sp_ = kind == 0 and s == 0, kind == 2 and s == 1
                        for c in range(8):
                            w_h, w_l = vh[:, s, c * P:(c + 1) * P], vl[:, s, c * P:(c + 1) * P]
                            pe.matmul(ps[c][:, 0:T], w_h, act_h[:, s, :], start=st_, stop=False)
                            pe.matmul(ps[c][:, 0:T], w_h, act_l[:, s, :], start=False, stop=False)
                            m = pe.matmul(ps[c][:, 0:T], w_l, act_h[:, s, :], start=False, stop=sp_)
                        m.then_inc(sem("v_done"), 1)
                pair(0, 0)
                with pe.Fori(1, PK // 2 - 1) as i:
                    pair(i, 1)
                pair(PK // 2 - 1, 2)

        def act_peer(act, o):
            def copy_q(i, c, s):
                act.wait_ge(sem("q_used"), i * 8 + 4 * (TRIPLE["wq"][0] + c + 1))
                o.do(act.copy(work[:, ds(i * (2 * T) + c * T, T)], ps[4 + s][:, 0:T]), sem("tile_freed"))

            high_parts(act, o, "wq", copy_q, {"tile_freed": 2})
            for g in range(2):
                act.wait_ge(sem("key_done"), g + 1)
                o.do(act.copy(keyT[:, 4 * g:4 * g + 4, :], ps[g][:, 0:512].rearrange("p (a b) -> p a b", b=P)),
                     sem("key_copied"))
            for i, (t0, n) in enumerate(TOK):
                for b in range(4):
                    act.wait_ge(sem("scr_done"), 4 * i + b + 1)
                    dst = scr[0:n, i, :].rearrange("p (h c k) -> p h c k", c=2, k=PK)[:, 4 * (b // 2):4 * (b // 2) + 4, b % 2, :]
                    o.do(act.copy(dst, ps[b][0:n, 0:512].rearrange("p (h k) -> p h k", k=PK)), sem("scr_copied"))
            for i in range(3):
                act.wait_ge(sem("vdiff_ready"), i + 1)
                n = TOK[i][1]
                g = tok3[0:n, i, 2, :]
                o.do(act.activation(g, g, ACT.Exp), sem("vexp_ready"))
            act.wait_ge(sem("ex3_done"), 1)
            for q in range(3):
                o.do(act.copy(ex3[:, q, :], ps[4 + q][:, 0:T]), sem("ex3_copied"))

            with act.Fori(0, NP_) as i:
                o.loop(i, {"g_copied": 2})
                for s in range(2):
                    act.wait_ge(sem("g_done"), i * 2 + (s + 1))
                    o.do(act.copy(dense[:, :, ds(i * 8 + 4 * s, 4)], ps[s][:, 0:512].rearrange("p (t k) -> p k t", k=P)),
                         sem("g_copied"))
                o.leave(NP_)

            def high(i, c, s, head):
                for q in range(4):
                    act.wait_ge(sem("turned"), i * 8 + (4 * c + q + 1))
                    act.wait_ge(sem("q_used"), i * 8 + (4 * (UB + c) + q - 3))
                    o.do(act.copy(part_h[:, q, :], ps[q][:, 0:512]), sem("high_done"))

            def gelu(i, c, s):
                act.wait_ge(sem("q_used"), i * 8 + 4 * (UB + c + 1))
                act.wait_ge(sem("tile_freed"), i * 2 + (UB + c - 1))
                o.do(act.activation(gel[:, s, :], ps[4 + s][:, 0:T], ACT.Gelu_apprx_tanh), sem("gelu_done"))

            in_pairs(act, "U", high, gelu, {"high_done": 8, "gelu_done": 2}, o)
            o.open = {}
            act.wait_ge(sem("q_used"), 4 * (UB + PK))
            act.wait_ge(sem("tile_freed"), UB + PK)
            for half in range(2):
                def four(i, head):
                    for s in range(4):
                        if s % 2 == 0:
                            act.wait_ge(sem(f"v_in{s // 2}"), i * 16 + (16 * 32 * half + 16))
                        if not (head and s < 2):
                            act.wait_ge(sem("v_done"), i * 4 + (128 * half + s - 1))
                        o.do(act.copy(vh[:, s % 2, :], natural[s // 2][:, 1024 * (s % 2):1024 * (s % 2) + 1024]),
                             sem("vh_done"))
                        o.do(act.copy(act_h[:, s % 2, :], work[:, ds(i * (4 * T) + s * T, T)]), sem("ah_done"))
                if half == 0:
                    four(0, True)
                with act.Fori(1 - half, 32) as i:
                    o.loop(i, {"vh_done": 4, "ah_done": 4})
                    four(i, False)
                    o.leave(31 + half)
                o.open = {}

        def dve_peer(v, o):
            hr = "p (h r) -> p h r"
            low_parts(v, o, "wq", None, None, {})
            for i, (t0, n) in enumerate(TOK):
                v.wait_ge(sem("scr_copied"), 4 * i + 4)
                s3 = scr[0:n, i, :].rearrange("p (a k) -> p a k", k=PK)
                o.settle()

                def best16(src, m, val, idx):
                    for half in range(2):
                        for a in range(m):
                            o.do(v.max(val[0:n, a, 8 * half:8 * half + 8], src[:, a, :]))
                        o.settle()
                        for a in range(m):
                            o.do(v.max_index(idx[0:n, a, 8 * half:8 * half + 8], val[0:n, a, 8 * half:8 * half + 8],
                                             src[:, a, :]))
                            if half == 0:
                                o.do(v.match_replace(src[:, a, :], val[0:n, a, 0:8], src[:, a, :], -3.0e38))
                        o.settle()

                best16(s3, 16, tv, ti)
                o.do(v.tensor_copy(tf[0:n], ti[0:n]))
                t4 = tv[0:n].rearrange("p (h c) r -> p h c r", c=2)
                o.do(v.tensor_tensor(cand[0:n], bc(t4[:, :, 0, :], TK), t4[:, :, 1:2, :].to_broadcast([n, PH, TK, TK]),
                                     ALU.add))
                o.settle()
                best16(cand[0:n].rearrange("p h a b -> p h (a b)"), PH, vs, ic.rearrange(hr, r=TK))
                g = tok3[0:n, i, 2, :].rearrange(hr, r=TK)
                o.do(v.tensor_tensor(g, vs[0:n], vs[0:n, :, 0:1].to_broadcast([n, PH, TK]), ALU.subtract), sem("vdiff_ready"))
                f4 = tf[0:n].rearrange("p (h c) r -> p h c r", c=2)
                for c, (op, k) in enumerate(((ALU.logical_shift_right, 4), (ALU.bitwise_and, 15))):
                    o.do(v.tensor_scalar(ia[0:n], ic[0:n], k, None, op))
                    o.settle()
                    o.do(v.tensor_copy(iF[c][0:n], ia[0:n]))
                    o.settle()
                    e3 = eq[0:n].rearrange("p h r q -> p (h r) q")
                    o.do(v.tensor_tensor(e3, bc(iF[c][0:n], TK), iota[0:n, 0:TK].unsqueeze(1).to_broadcast([n, P, TK]),
                                         ALU.is_equal))
                    o.settle()
                    o.do(v.tensor_tensor(eq[0:n], eq[0:n], f4[:, :, c:c + 1, :].to_broadcast([n, PH, TK, TK]), ALU.mult))
                    o.settle()
                    o.do(v.tensor_reduce(tok3[0:n, i, c, :], e3, AX.X, ALU.add))
                v.wait_ge(sem("vexp_ready"), i + 1)
                o.do(v.tensor_reduce(gsum[0:n, 0, :], g, AX.X, ALU.add))
                o.settle()
                o.do(v.reciprocal(gsum[0:n, 1, :], gsum[0:n, 0, :]))
                o.settle()
                o.do(v.tensor_tensor(g, g, bc(gsum[0:n, 1, :], TK), ALU.mult), sem("tok3_ready"))
            v.wait_ge(sem("ex3_copied"), 3)

            def onehots(i, s, first):
                if not first:
                    v.wait_ge(sem("g_done"), i * 2 + (s - 1))
                for j in range(4):
                    t = i * 8 + 4 * s + j
                    o.do(v.tensor_scalar(ohA[s][:, j, :], iota[:], ex3[:, 0, ds(t, 1)], ex3[:, 2, ds(t, 1)],
                                         ALU.is_equal, ALU.mult))
                    o.do(v.tensor_scalar(ohB[s][:, j, :], iota[:], ex3[:, 1, ds(t, 1)], None, ALU.is_equal),
                         sem("oh_ready") if j == 3 else None)

            for s in range(2):
                onehots(0, s, True)
            with v.Fori(1, NP_) as i:
                o.loop(i, {"oh_ready": 2, "dve_own": 14})
                for s in range(2):
                    onehots(i, s, False)
                o.leave(NP_ - 1)
            o.open = {}
            v.wait_ge(sem("g_copied"), 2 * NP_)

            def gate(i, c, s):
                v.wait_ge(sem("gelu_done"), i * 2 + (c + 1))
                a = work[:, ds(i * (2 * T) + c * T, T)]
                o.do(v.tensor_tensor(a, a, gel[:, s, :], ALU.mult), sem("tile_freed"))

            low_parts(v, o, "U", lambda q: ps[q][:, 0:512], gate, {"tile_freed": 2})
            for half in range(2):
                def four(i):
                    for s in range(4):
                        v.wait_ge(sem("vh_done"), i * 4 + (128 * half + s + 1))
                        o.do(v.tensor_tensor(vl[:, s % 2, :], natural[s // 2][:, 1024 * (s % 2):1024 * (s % 2) + 1024],
                                             vh[:, s % 2, :].bitcast(F32), ALU.subtract), sem("vl_done"))
                        v.wait_ge(sem("ah_done"), i * 4 + (128 * half + s + 1))
                        o.do(v.tensor_tensor(act_l[:, s % 2, :], work[:, ds(i * (4 * T) + s * T, T)],
                                             act_h[:, s % 2, :].bitcast(F32), ALU.subtract), sem("al_done"))
                with v.Fori(0, 32) as i:
                    o.loop(i, {"vl_done": 4, "al_done": 4})
                    four(i)
                    o.leave(32)
                o.open = {}
                v.wait_ge(sem("v_done"), 128 * (half + 1))
                if half == 0:
                    v.wait_ge(sem("h_back"), 16)
                for c in range(8):
                    h = hT[:, 8 * half + c, :]
                    o.do(v.tensor_tensor(h, h, ps[c][:, 0:T], ALU.add), sem("pv_added"))
            o.settle()

        proj = wk(0, 2, D)
        pN = wk(4096, 3, PLE)
        pT = wk(4864, 2, T)
        yout = wk(8192, 3, D)

        def sp_tail(sp):
            w = ins["w_ple_gate"][0].rearrange("(k p) n -> p k n", p=P)
            sp.wait_ge(sem("v_done"), 256)
            for i, (t0, n) in enumerate(TOK):
                src = ins["p_prompt"][0, 0, t0:t0 + n, :] if i < 2 else ins["p_sample"][0].rearrange("b s d -> (b s) d")
                sp.dma_start(pN[0:n, i, :], src).then_inc(sem("p_in"), 16)
            for s in range(2):
                sp.dma_start(natural[s].rearrange("p (k n) -> p k n", n=P), w[:, :, s * P:(s + 1) * P]).then_inc(
                    sem(f"nat_in{s}"), 16)
            sp.dma_start(proj, ins["w_ple_proj"][0].rearrange("(k p) n -> p k n", p=P)).then_inc(sem("proj_in"), 16)
            with sp.Fori(1, KD // 2) as i:
                for s in range(2):
                    sp.wait_ge(sem("low_done"), i * 8 + 4 * (TRIPLE["gate"][0] + s - 1))
                    sp.dma_start(natural[s].rearrange("p (k n) -> p k n", n=P), w[:, :, ds(i * 256 + s * P, P)]).then_inc(
                        sem(f"nat_in{s}"), 16)
            for i, (t0, n) in enumerate(TOK):
                dst = outs[0][0, t0:t0 + n, :] if i < 2 else outs[1].rearrange("b s d -> (b s) d")
                for q in range(2):
                    sp.wait_ge(sem(f"y_out{q}"), 2 * (i + 1))
                sp.dma_start(dst, yout[0:n, i, :]).then_inc(sem("y_stored"), 16)
            sp.wait_ge(sem("y_stored"), 48)

        def pe_tail(pe):
            pe.wait_ge(sem("p_in"), 48)
            pe.wait_ge(sem("pv_added"), 16)
            for i, (t0, n) in enumerate(TOK):
                for c in range(2):
                    m = pe.transpose(ps[c][:, t0:t0 + n], pN[0:n, i, c * P:(c + 1) * P], ident[0:n, 0:n])
            m.then_inc(sem("pt_done"), 1)
            pe_norm(pe, 2)
            pe.wait_ge(sem("pt_copied"), 1)
            pe.wait_ge(sem("n_ready"), 3 * KD)
            pe.wait_ge(sem("proj_in"), 16)

            def embed(c8):
                for c in range(2 * c8, 2 * c8 + 2):
                    if c >= 2:
                        pe.wait_ge(sem("e_copied"), c - 1)
                    for k in range(2):
                        m = pe.matmul(ps[4 + c % 2][:, 0:T], proj[:, k, c * P:(c + 1) * P], pT[:, k, :],
                                      start=(k == 0), stop=(k == 1))
                    m.then_inc(sem("e_done"), 1)

            for c8 in range(8):
                embed(c8)
            pe.wait_ge(sem("e_copied"), KD)
            pe_triple(pe, "gate", ple_h, ple_l)
            pe_norm(pe, 3)
            pe.wait_ge(sem("n_ready"), 4 * KD)
            for g in range(12):
                i, q = divmod(g, 4)
                t0, n = TOK[i]
                if g >= 4:
                    pe.wait_ge(sem(f"y_out{g % 2}"), (g - 4) // 2 + 1)
                for j in range(4):
                    m = pe.transpose(ps[g % 4][0:n, j * P:(j + 1) * P], nT[:, 4 * q + j, t0:t0 + n], ident[:])
                m.then_inc(sem("yt_done"), 1)

        eT = wk(14336, KD, T)
        sg = wk(19000, 2, T)

        def act_tail(act, o):
            act.wait_ge(sem("pt_done"), 1)
            for c in range(2):
                o.do(act.copy(pT[:, c, :], ps[c][:, 0:T]), sem("pt_copied") if c else None)
            act.wait_ge(sem("pv_added"), 16)
            act_norm(act, 2)
            act_norm_high(act, o, 2, ple_h)
            for c in range(KD):
                act.wait_ge(sem("e_done"), c + 1)
                o.do(act.copy(eT[:, c, :], ps[4 + c % 2][:, 0:T]), sem("e_copied"))

            def sig(i, c, s):
                b = TRIPLE["gate"][0]
                act.wait_ge(sem("q_used"), i * 8 + 4 * (b + c + 1))
                o.do(act.activation(sg[:, s, :], ps[4 + s][:, 0:T], ACT.Sigmoid), sem("sig_done"))

            o.open = {}
            high_parts(act, o, "gate", sig, {"sig_done": 2})
            act.wait_ge(sem("h_added"), KD)
            act_norm(act, 3)
            for g in range(0, 12, 2):
                i, q = divmod(g, 4)
                n = TOK[i][1]
                act.wait_ge(sem("yt_done"), g + 1)
                o.do(act.copy(yout[0:n, i, 512 * q:512 * q + 512], ps[g % 4][0:n, 0:512]), sem("y_out0"))

        def dve_tail(v, o):
            dve_norm(v, o, 2, ple_h, ple_l)
            v.wait_ge(sem("e_copied"), KD)

            def gated(i, c, s):
                v.wait_ge(sem("sig_done"), i * 2 + (c + 1))
                e = work[:, ds(i * (2 * T) + (14336 + c * T), T)]
                h = low[:, ds(i * (2 * T) + c * T, T)]
                o.do(v.tensor_tensor(e, e, sg[:, s, :], ALU.mult), sem("tile_freed"))
                v.wait_ge(sem("tile_freed"), i * 2 + (TRIPLE["gate"][0] + c + 1))
                o.do(v.tensor_tensor(h, h, e, ALU.add), sem("h_added"))

            low_parts(v, o, "gate", None, gated, {"tile_freed": 2, "h_added": 2})
            o.open = {}
            v.wait_ge(sem("h_added"), KD)
            dve_norm(v, o, 3)
            for g in range(1, 12, 2):
                i, q = divmod(g, 4)
                n = TOK[i][1]
                v.wait_ge(sem("yt_done"), g + 1)
                o.do(v.tensor_copy(yout[0:n, i, 512 * q:512 * q + 512], ps[g % 4][0:n, 0:512]), sem("y_out1"))

        block = ctx.enter_context(nc.Block())

        @block.sync
        def _(sp):
            for i, (t0, n) in enumerate(TOK):
                src = ins["x_prompt"][0, t0:t0 + n, :] if i < 2 else ins["x_sample"].rearrange("b s d -> (b s) d")
                sp.dma_start(xin[0:n, i, :], src).then_inc(sem(f"x_in{i}"), 16)
            v = sem("vec_in")
            at = 0
            for name, rows in (("norm_mix", 16), ("norm_ffn", 16), ("norm_ple", 16), ("norm_final", 16),
                               ("mlstm_norm", 8), ("b_glu", 8)):
                a = ins[name] if name == "norm_final" else ins[name][0]
                sp.dma_start(vrow[at:at + rows, :], a.rearrange("(r p) -> r p", p=P)).then_inc(v, 16)
                at += rows
            sp.dma_start(vrow[80:88, :], ins["ssm_D"][0].rearrange("(u r) c -> u (r c)", r=8)).then_inc(v, 16)
            sp.dma_start(gb8[0:4], ins["b_igate"].rearrange("a h -> h a")).then_inc(v, 16)
            sp.dma_start(gb8[4:8], ins["b_fgate"].rearrange("a h -> h a")).then_inc(v, 16)

            def weights(name, src, c0):
                base, nb, kt = STREAM[name]
                w = src.rearrange("(k p) n -> p k n", p=P)
                first = 0
                if base == 0:
                    for s in range(2):
                        sp.dma_start(ring[:, s, 0:kt * WB].rearrange("p (k n) -> p k n", n=WB),
                                     w[:, :, c0 + s * WB:c0 + (s + 1) * WB]).then_inc(sem(f"w_in{s}"), 16)
                    first = 1
                with sp.Fori(first, nb // 2) as i:
                    for s in range(2):
                        sp.wait_ge(sem("mm_done"), i * 4 + 2 * (base + s) - 2)
                        sp.dma_start(ring[:, s, 0:kt * WB].rearrange("p (k n) -> p k n", n=WB),
                                     w[:, :, ds(i * (2 * WB) + (c0 + s * WB), WB)]).then_inc(sem(f"w_in{s}"), 16)

            w_in = ins["w_in"][0]
            s5 = sem("s5_in")
            for q, name in enumerate(AB):
                sp.dma_start(r32[0:NJ, q, :], ins[name][0].rearrange("(j g) p -> j (g p)", g=2)).then_inc(s5, 16)
            sp.dma_start(dtr[0:NJ, :], ins["ssm_log_dt"][0].rearrange("(j g) -> j g", g=2)).then_inc(s5, 16)
            for q, name in enumerate(("re", "im")):
                sp.dma_start(Bn[q], ins[f"ssm_B_{name}"][0].rearrange("(j g) p c -> (g p) j c", g=2)).then_inc(s5, 16)
                sp.dma_start(Cn[q], ins[f"ssm_C_{name}"][0].rearrange("(u r) c p -> (r c) u p", r=8)).then_inc(s5, 16)
                sp.dma_start(s0r[:, :, q, :], ins[f"state_ssm_{name}"][0]
                             .rearrange("b (j g) p -> (b j) (g p)", g=2)
                             .rearrange("(t r) q -> r t q", t=2)).then_inc(s5, 16)
            sp.dma_start(gw, w_in[:, 4 * MW:4 * MW + 8].rearrange("(k p) n -> p k n", p=P)).then_inc(sem("gw_in"), 16)
            weights("u", w_in, 4 * MW + 8)
            weights("z", w_in, 0)
            weights("glu", ins["w_glu"][0], 0)
            sp_mlstm(sp)
            tiles(sp, "out", lambda i, c: ins["w_out"][0].rearrange("(k p) n -> p k n", p=P)[:, :, ds(i * 256 + c * P, P)])
            sp.wait_ge(sem("tile_freed"), KD)
            sp.dma_start(spill, low[:, 0:KD * T]).then_inc(sem("h_spilled"), 16)
            tiles(sp, "wq", lambda i, c: ins["peer_w_q"][0].rearrange("(k p) n -> p k n", p=P)[:, :, ds(i * 256 + c * P, P)])
            sp_peer(sp)
            sp_tail(sp)

        @block.gpsimd
        def _(pool):
            o = Own(pool, sem("pool_own"))
            o.do(pool.memset(ident[:], 0.0))
            o.do(pool.memset(ones[:], 1.0))
            o.do(pool.memset(par[:, 0:4], 1.0))
            o.do(pool.memset(bmask, 1.0))
            o.settle()
            o.do(pool.affine_select(out=ident[:], in_=ident[:], compare_op=ALU.not_equal, fill=1.0, base=0,
                                    pattern=[[-1, P]], channel_multiplier=1))
            o.do(pool.iota(iota[:], [[1, P]], base=0, channel_multiplier=0, allow_small_or_imprecise_dtypes=True))
            o.do(pool.affine_select(out=tri, in_=ones[:], compare_op=ALU.is_ge, fill=0.0, base=0,
                                    pattern=[[1, P]], channel_multiplier=-1))
            o.do(pool.affine_select(out=trs, in_=ones[0:TS, 0:TS], compare_op=ALU.is_ge, fill=0.0, base=0,
                                    pattern=[[1, TS]], channel_multiplier=-1))
            o.settle()
            tv = trs.rearrange("p (b s) -> p b s", s=NS)
            o.do(pool.affine_select(out=tv, in_=tv, compare_op=ALU.is_ge, fill=0.0, base=0,
                                    pattern=[[-NS, NB], [0, NS]], channel_multiplier=1))
            o.do(pool.affine_select(out=bmask, in_=bmask, compare_op=ALU.is_ge, fill=0.0, base=0,
                                    pattern=[[-NS, NB]], channel_multiplier=1))
            o.do(pool.affine_select(out=par[:, 0:4], in_=par[:, 0:4], compare_op=ALU.is_ge, fill=0.0, base=0,
                                    pattern=[[-32, 4]], channel_multiplier=1))
            o.settle()
            o.do(pool.affine_select(out=bmask, in_=bmask, compare_op=ALU.is_ge, fill=0.0, base=NS - 1,
                                    pattern=[[NS, NB]], channel_multiplier=-1))
            o.do(pool.affine_select(out=par[:, 0:4], in_=par[:, 0:4], compare_op=ALU.is_ge, fill=0.0, base=15,
                                    pattern=[[32, 4]], channel_multiplier=-1))
            o.settle()
            o.do(pool.memset(par[:, 7:8], 0.0), sem("const_ready"))

        @block.tensor
        def _(pe):
            pe.wait_ge(sem("const_ready"), 1)
            for g in range(12):
                i, q = divmod(g, 4)
                n = TOK[i][1]
                if q == 0:
                    pe.wait_ge(sem(f"x_in{i}"), 16)
                if g >= 4:
                    pe.wait_ge(sem(f"xt_copied{g % 2}"), (g - 4) // 2 + 1)
                for j in range(4):
                    m = pe.transpose(ps[g % 4][:, j * n:(j + 1) * n],
                                     xin[0:n, i, (4 * q + j) * P:(4 * q + j + 1) * P], ident[0:n, 0:n])
                m.then_inc(sem("xt_done"), 1)
            pe.wait_ge(sem("vec_in"), 16 * 9)
            pe.transpose(ps[4][:, 0:88], vrow[0:88, :], ident[0:88, 0:88]).then_inc(sem("vec_done"), 1)
            pe_norm(pe, 0)
            pe.wait_ge(sem("n_ready"), KD)
            pe.wait_ge(sem("xt_copied0"), 6)
            pe.wait_ge(sem("xt_copied1"), 6)
            pe_linear(pe, "u", nT)
            pe.wait_ge(sem("gw_in"), 16)
            for k in range(KD):
                m = pe.matmul(ps[5][0:8, 0:T], gw[:, k, :], nT[:, k, :], start=(k == 0), stop=(k == KD - 1))
            m.then_inc(sem("gate_done"), 1)
            pe.wait_ge(sem("abf_rows"), 1)
            for q in range(4):
                m = pe.transpose(ps[4][:, q * NJ:(q + 1) * NJ], r32[0:NJ, 10 + q, :], ident[0:NJ, 0:NJ])
            m.then_inc(sem("abf_done"), 1)
            pe.wait_ge(sem("s5_in"), 16 * 9)
            for q in range(2):
                for t in range(2):
                    m = pe.transpose(ps[6][:, (2 * q + t) * P:(2 * q + t + 1) * P], s0r[:, t, q, :], ident[:])
            m.then_inc(sem("s0_done"), 1)
            pe.wait_ge(sem("gate_copied"), 1)
            pe.wait_ge(sem("abf_copied"), 1)
            pe.wait_ge(sem("s0_copied"), 1)
            for g in range(8):
                src, q, half = [Bbd, Cbd][g // 4], (g // 2) % 2, g % 2
                pe.wait_ge(sem("bd_ready"), g // 4 + 1)
                if g >= 4:
                    pe.wait_ge(sem("bct_copied"), g - 3)
                for j in range(4):
                    u = 4 * half + j
                    if g < 4:
                        a = Bbd[q][:, 4 * u:4 * u + 4, :, :].rearrange("p a b c -> p (a b c)")
                    else:
                        a = Cbd[q][:, u, :, :].rearrange("p b c -> p (b c)")
                    m = pe.transpose(ps[4 + g % 4][:, j * P:(j + 1) * P], a, ident[:])
                m.then_inc(sem("bct_done"), 1)
            pe.wait_ge(sem("bct_copied"), 8)
            pe.wait_ge(sem("mm_freed"), 8)
            for j in range(NJ):
                u, r = divmod(j, 4)
                if j >= 2:
                    pe.wait_ge(sem("bu_copied0"), j - 1)
                    pe.wait_ge(sem("bu_copied1"), j - 1)
                for q in range(2):
                    pe.matmul(ps[4 + 2 * (j % 2) + q][:, 0:T], BT[q][32 * r:32 * r + 32, u, :],
                              uT[32 * r:32 * r + 32, u, :], start=True, stop=True).then_inc(sem("bu_done"), 1)
            pe_linear(pe, "z", nT)
            pe.wait_ge(sem("s5_ready"), 1)
            pe.wait_ge(sem("bu_copied0"), NJ)
            pe.wait_ge(sem("bu_copied1"), NJ)
            for u in range(8):
                if u >= 2:
                    pe.wait_ge(sem("y_sum"), u - 1)
                for r in range(4):
                    for q in range(2):
                        m = pe.matmul(ps[4 + u % 2][32 * r:32 * r + 32, 0:T], CT[q][:, u, 32 * r:32 * r + 32],
                                      st[q][:, 4 * u + r, :], start=(q == 0), stop=(q == 1))
                m.then_inc(sem("y_done"), 1)
            pe.wait_ge(sem("send_ready"), 1)
            for q in range(2):
                pe.transpose(ps[6][0:NJ, q * P:(q + 1) * P], send[:, q, 0, :], ident[:])
                for t in range(2):
                    m = pe.transpose(ps[7][:, (2 * q + t) * P:(2 * q + t + 1) * P],
                                     send[:, q, 1 + 4 * t:5 + 4 * t, :].rearrange("p a b -> p (a b)"), ident[:])
            m.then_inc(sem("send_done"), 1)
            pe.wait_ge(sem("yg_ready"), 8)
            pe_linear(pe, "glu", uT)
            pe_mlstm(pe)
            pe.wait_ge(sem("glu_ready"), 8)
            pe.wait_ge(sem("hm_ready"), 2 * H)
            pe.wait_ge(sem("ys_split"), 8)
            pe_triple(pe, "out", mix_h, mix_l)
            pe_norm(pe, 1)
            pe.wait_ge(sem("n_ready"), 2 * KD)
            pe_triple(pe, "wq", ffn_h, ffn_l)
            pe_peer(pe)
            pe_tail(pe)

        @block.scalar
        def _(act):
            o_act.eng = act
            o = o_act
            for g in range(0, 12, 2):
                i, q = divmod(g, 4)
                t0, n = TOK[i]
                act.wait_ge(sem("xt_done"), g + 1)
                o.do(act.copy(hT[:, 4 * q:4 * q + 4, t0:t0 + n],
                              ps[g % 4][:, 0:4 * n].rearrange("p (a b) -> p a b", b=n)), sem("xt_copied0"))
            act.wait_ge(sem("vec_done"), 1)
            o.do(act.copy(gv[:], ps[4][:, 0:88]), sem("vec_copied"))
            act.wait_ge(sem("xt_copied1"), 6)
            o.settle()
            act_norm(act, 0)
            act.wait_ge(sem("s5_in"), 16 * 9)
            o.do(act.activation(dtr[0:NJ, :], dtr[0:NJ, :], ACT.Exp), sem("dt_ready"))

            def copy_tiles(name, dst, fn=None):
                base, nb, kt = STREAM[name]

                def one(i, b, peeled=False):
                    act.wait_ge(sem("mm_done"), i * 4 + (2 * base + b + 1))
                    src = ps[b][:, 0:T]
                    d = dst[:, b, :] if peeled else dst[:, ds(i * 4 + b, 1), :]
                    if not peeled:
                        src = src.unsqueeze(1)
                    o.do(act.copy(d, src), sem("mm_freed"))
                with act.Fori(0, nb // 2) as i:
                    o.loop(i, {"mm_freed": 4})
                    for b in range(4):
                        one(i, b)
                    o.leave(nb // 2)

            copy_tiles("u", uT)
            act.wait_ge(sem("theta_ready"), 1)
            o.do(act.activation(r32[0:NJ, 4, :], r32[0:NJ, 2, :], ACT.Exp))
            o.do(act.activation(r32[0:NJ, 5, :], r32[0:NJ, 3, :], ACT.Sin))
            o.do(act.activation(r32[0:NJ, 6, :], r32[0:NJ, 3, :], ACT.Sin, scale=0.5), sem("trig_ready"))
            o.settle()
            act.wait_ge(sem("s0_done"), 1)
            o.do(act.copy(s0T, ps[6][:, 0:512].rearrange("p (a b) -> p a b", a=2)), sem("s0_copied"))
            for g in range(8):
                dst = [BT, CT][g // 4][(g // 2) % 2]
                half = g % 2
                act.wait_ge(sem("bct_done"), g + 1)
                o.do(act.copy(dst[:, 4 * half:4 * half + 4, :],
                              ps[4 + g % 4][:, 0:512].rearrange("p (a b) -> p a b", b=P)), sem("bct_copied"))
            for j in range(NJ):
                act.wait_ge(sem("bu_done"), 2 * j + 1)
                o.do(act.copy(st[0][:, j, :], ps[4 + 2 * (j % 2)][:, 0:T]), sem("bu_copied0"))
            copy_tiles("z", zT)
            for u in range(8):
                act.wait_ge(sem("y_sum"), u + 1)
                o.do(act.activation(uT[:, u, :], uT[:, u, :], ACT.Gelu_apprx_tanh), sem("yg_ready"))
            o.settle()
            act.wait_ge(sem("send_done"), 1)
            o.do(act.copy(sout[0:NJ, 0:2, :], ps[6][0:NJ, 0:2 * P].rearrange("p (a b) -> p a b", b=P)))
            o.do(act.copy(sout[:, 2:6, :], ps[7][:, 0:512].rearrange("p (a b) -> p a b", b=P)), sem("sout_ready"))
            o.do(act.activation(zT[:, 24:32, :], zT[:, 24:32, :], ACT.Sigmoid), sem("og_ready"))
            base = STREAM["glu"][0]
            for c in range(8):
                act.wait_ge(sem("mm_done"), 2 * base + c + 1)
                if c >= 2:
                    act.wait_ge(sem("glu_ready"), c - 1)
                o.do(act.activation(gel[:, c % 2, :], ps[c % 4][:, 0:T], ACT.Sigmoid, bias=gv[:, 72 + c:73 + c]),
                     sem("mm_freed"))
            act_mlstm(act, o)
            high_parts(act, o, "out", None, {})
            act.wait_ge(sem("tile_freed"), KD)
            act_norm(act, 1)
            act_norm_high(act, o, 1, ffn_h)
            act_peer(act, o)
            act_tail(act, o)

        @block.vector
        def _(v):
            o = Own(v, sem("dve_own"))
            v.wait_ge(sem("const_ready"), 1)
            for g in range(1, 12, 2):
                i, q = divmod(g, 4)
                t0, n = TOK[i]
                v.wait_ge(sem("xt_done"), g + 1)
                o.do(v.tensor_copy(hT[:, 4 * q:4 * q + 4, t0:t0 + n],
                                   ps[g % 4][:, 0:4 * n].rearrange("p (a b) -> p a b", b=n)), sem("xt_copied1"))
            v.wait_ge(sem("vec_copied"), 1)
            v.wait_ge(sem("xt_copied0"), 6)
            dve_norm(v, o, 0)
            dve_s5_setup(v, o)
            for j in range(NJ):
                v.wait_ge(sem("bu_done"), 2 * j + 2)
                o.do(v.tensor_copy(st[1][:, j, :], ps[5 + 2 * (j % 2)][:, 0:T]), sem("bu_copied1"))
            v.wait_ge(sem("bu_copied0"), NJ)
            dve_s5_scan(v, o)
            for u in range(8):
                v.wait_ge(sem("y_done"), u + 1)
                o.do(v.scalar_tensor_tensor(uT[:, u, :], uT[:, u, :], gv[:, 80 + u:81 + u], ps[4 + u % 2][:, 0:T],
                                            ALU.mult, ALU.add), sem("y_sum"))
            base = STREAM["glu"][0]
            for c in range(8):
                v.wait_ge(sem("mm_freed"), 2 * base + c + 1)
                o.do(v.tensor_tensor(mix[:, 8 + c, :], uT[:, c, :], gel[:, c % 2, :], ALU.mult), sem("glu_ready"))
            dve_mlstm(v, o)

            def add(i, c, s):
                v.wait_ge(sem("q_used"), i * 8 + (4 * c + 4))
                h = low[:, ds(i * (2 * T) + c * T, T)]
                o.do(v.tensor_tensor(h, h, ps[4 + s][:, 0:T], ALU.add), sem("tile_freed"))

            low_parts(v, o, "out", None, add, {"tile_freed": 2})
            o.settle()
            dve_norm(v, o, 1, ffn_h, ffn_l)
            dve_peer(v, o)
            dve_tail(v, o)


_INS = ["x_prompt", "x_sample", "state_mlstm_C", "state_mlstm_n", "state_mlstm_m", "state_ssm_re", "state_ssm_im",
        "p_prompt", "p_sample", "norm_mix", "w_in", "b_igate", "b_fgate", "mlstm_norm", "ssm_A_re", "ssm_A_im",
        "ssm_B_re", "ssm_B_im", "ssm_C_re", "ssm_C_im", "ssm_D", "ssm_log_dt", "w_glu", "b_glu", "w_out", "norm_ffn",
        "peer_w_q", "peer_keys", "peer_u", "peer_v", "norm_ple", "w_ple_gate", "w_ple_proj", "norm_final"]
_OUTS = [(1, TP, D), (NB, NS, D),
         (1, 1, H, DH, DH), (1, 1, H, DH), (1, 1, H), (1, 1, G, SP_), (1, 1, G, SP_),
         (1, NB, H, DH, DH), (1, NB, H, DH), (1, NB, H), (1, NB, G, SP_), (1, NB, G, SP_)]


def kernel(**inputs):
    import numpy as np
    import concourse.bacc as bacc
    from concourse.bass_utils import run_bass_kernel_spmd

    nc = bacc.Bacc("TRN2", target_bir_lowering=False, num_devices=1, dynamic_dma_scratch_size=1024)
    arrays, ins = {}, {}
    for name in _INS:
        a = np.ascontiguousarray(inputs[name])
        arrays[f"in_{name}"] = a
        ins[name] = nc.dram_tensor(f"in_{name}", a.shape, mybir.dt.from_np(a.dtype), kind="ExternalInput").ap()
    outs = [nc.dram_tensor(f"out_{i}", shape, F32, kind="ExternalOutput").ap() for i, shape in enumerate(_OUTS)]
    build(nc, ins, outs)
    r = run_bass_kernel_spmd(nc, [arrays], core_ids=[0])
    return tuple(r.results[0][f"out_{i}"] for i in range(len(_OUTS)))
```

```python
from contextlib import ExitStack
import itertools
import math

import concourse.bass as bass
from concourse import mybir

F32 = mybir.dt.float32
F32R = mybir.dt.float32r
U32 = mybir.dt.uint32
ALU = mybir.AluOpType
ACT = mybir.ActivationFunctionType
AX = mybir.AxisListType

P = 128
D = 2048
KD = D // P
TP, NB, NS = 256, 8, 4
TS = NB * NS
T = TP + TS
TOK = [(0, 128), (128, 128), (256, TS)]
H, DH = 4, 256
MW = H * DH
G, SP_, GC = 64, 64, 16
NJ = G * SP_ // P
CH = 16
NCH = TP // CH
PH, PK, TK = 8, 128, 16
UA = 36
PLE = 256
EPS = 1e-6
WB = 256
COLS_IN = 4 * MW + 2 * H + G * GC
NEG = -1.0e38

O_RE, O_IM = 0, NJ * T
O_Z = 2 * NJ * T
O_U = O_Z + 32 * T
O_MIX = O_U + 8 * T
O_EX = O_MIX + 16 * T
WORK = P * T
assert O_EX + 8 * T == WORK

STREAM, _n = {}, 0
for _name, _blocks, _kt in (("u", 4, KD), ("z", 16, KD), ("glu", 4, 8)):
    STREAM[_name] = (_n, _blocks, _kt)
    _n += _blocks


TRIPLE, _n = {}, 0
for _name, _tiles in (("out", KD), ("wq", 8), ("Ua", UA), ("Ub", PK - UA), ("gate", KD)):
    TRIPLE[_name] = (_n, _tiles)
    _n += _tiles


class Own:

    def __init__(self, eng, chain):
        self.eng, self.chain, self.n, self.open, self.per = eng, chain, {}, {}, None

    def do(self, ins, sem=None):
        s = self.chain if sem is None else sem
        ins.then_inc(s, 1)
        self.n[s.name] = self.n.get(s.name, 0) + 1
        self.open[s.name] = s

    def settle(self):
        for name, s in self.open.items():
            n = self.n[name]
            if self.per is not None:
                i, per = self.per
                self.eng.wait_ge(s, i * per.get(name, 0) + n)
            else:
                self.eng.wait_ge(s, n)
        self.open = {}

    def loop(self, i, per):
        self.per, self.at = (i, per), dict(self.n)

    def leave(self, trips):
        per = self.per[1]
        for name, n in self.n.items():
            assert n - self.at.get(name, 0) == per.get(name, 0), (name, n - self.at.get(name, 0))
            self.n[name] = self.at.get(name, 0) + trips * per.get(name, 0)
        self.per = None


def build(nc, ins, outs):
    ctx = ExitStack()
    with ctx:
        def sb(name, shape, dt=F32):
            base = nc.sbuf_base
            t = ctx.enter_context(nc.sbuf_tensor(name, shape, dt))
            sb_at[name] = -(-base // 32) * 32
            return t

        sb_at = {}
        sems = {}

        def sem(name):
            if name not in sems:
                sems[name] = ctx.enter_context(nc.semaphore(name))
            return sems[name]

        low = sb("low", [P, 2 * KD * T])
        ring = sb("ring", [P, 2, 4096])
        work = sb("work", [P, WORK])
        ident = sb("ident", [P, P])
        ones = sb("ones", [P, P])
        iota = sb("iota", [P, P])
        gv = sb("gv", [P, 88])
        rstd = sb("rstd", [P, T])
        rs = sb("rs", [P, T])
        m0 = sb("m0", [P, NB * H])
        warm = sb("warm", [P, 1])
        gel = sb("gel", [P, 2, T])
        ex3 = sb("ex3", [P, 3, T])
        tri = ex3[:, 0, 0:P]
        trs = ex3[0:TS, 0, P:P + TS]
        cols = ex3[:, 0, 160:192]
        bmask = ex3[0:TS, 0, 192:192 + NB]
        par = ex3[:, 0, 200:208]
        gb8 = ex3[0:8, 0, 208:209]
        rows8 = ex3[0:8, 1, :]
        ps = [ctx.enter_context(nc.psum_tensor(f"ps{i}", [P, 512], F32)) for i in range(8)]

        low_at, ring_at, work_at = sb_at["low"], sb_at["ring"], sb_at["work"]

        def alias(name, at, *shape, dt=F32R):
            return nc.alloc_sbuf_tensor_at(name, [P, *shape], dt, offset=at)[:]

        hT = low[:, 0:KD * T].rearrange("p (k t) -> p k t", t=T)
        nT = low[:, KD * T:2 * KD * T].rearrange("p (k t) -> p k t", t=T)
        mix_h = alias("mix_h", work_at + 4 * (O_Z + 8 * T), KD, T)
        mix_l = alias("mix_l", work_at + 4 * O_MIX, KD, T)
        ffn_h = alias("ffn_h", low_at + 4 * KD * T, KD, T)
        ffn_l = alias("ffn_l", low_at, KD, T)
        ple_h = alias("ple_h", work_at + 4 * 24000, KD, T)
        ple_l = alias("ple_l", work_at + 4 * (24000 + KD * T), KD, T)
        natural = [ring[:, 0, 2048 * s:2048 * s + 2048] for s in range(2)]
        part_h = alias("part_h", ring_at + 16384, 4, 512)
        part_l = alias("part_l", ring_at + 16384 + 8192, 4, 512)
        act_h = alias("act_h", low_at + 4 * KD * T, 4, T)
        act_l = alias("act_l", low_at + 4 * (KD + 4) * T, 4, T)
        spill = nc.dram_tensor("spill", [P, KD * T], F32).ap()

        def wk(off, *shape):
            n = math.prod(shape)
            ap = work[:, off:off + n]
            if len(shape) == 2:
                ap = ap.rearrange("p (a b) -> p a b", b=shape[1])
            elif len(shape) == 3:
                ap = ap.rearrange("p (a b c) -> p a b c", b=shape[1], c=shape[2])
            return ap

        def bc(ap, n):
            return ap.unsqueeze(len(ap.shape)).to_broadcast([*ap.shape, n])

        st = [wk(O_RE, NJ, T), wk(O_IM, NJ, T)]
        zT = wk(O_Z, 32, T)
        uT = wk(O_U, 8, T)
        mix = wk(O_MIX, 16, T)
        xin = wk(O_Z, 3, D)
        Bn = [wk(0, NJ, GC), wk(512, NJ, GC)]
        Bbd = [wk(1024, NJ, 2, GC), wk(2048, NJ, 2, GC)]
        Cn = [wk(3072, 8, SP_), wk(3584, 8, SP_)]
        Cbd = [wk(4096, 8, 2, SP_), wk(5120, 8, 2, SP_)]
        tB = [wk(6144 + 512 * i, NJ, GC) for i in range(4)]
        r32 = wk(8192, 16, P)
        s0r = wk(10240, 2, 2, P)
        vrow = wk(10752, 1, P)[:, 0, :]
        dtr = wk(10880, 1, 2)[:, 0, :]
        gw = wk(11008, KD, 8)
        BT = [wk(O_MIX, 8, P), wk(O_MIX + 1024, 8, P)]
        CT = [wk(O_MIX + 2048, 8, P), wk(O_MIX + 3072, 8, P)]
        abT = wk(O_MIX + 4096, 4, NJ)
        a16 = wk(O_MIX + 4224, 4, NJ)
        s0T = gel[:, :, 0:NB * NJ]
        tS = [wk(O_EX + 512 * i, NJ, 16) for i in range(4)]

        ds = bass.ds
        AB = ["ssm_A_re", "ssm_A_im"]

        send = wk(O_EX, 2, 1 + NB, NJ)
        sout = wk(O_EX + 576, 6, P)

        def pe_norm(pe, n):
            for q in range(4):
                pe.wait_ge(sem("sq_done"), 2 * n + q + 1)
                for k in range(4 * q, 4 * q + 4):
                    m = pe.matmul(ps[7][:, 0:T], ones[:], nT[:, k, :], start=(k == 0), stop=(k == KD - 1))
            m.then_inc(sem("ss_done"), 1)

        def pe_norm_summed(pe, n):
            pe.wait_ge(sem("acc_done"), KD * (n // 2 + 1))
            pe.matmul(ps[7][:, 0:T], ones[:], nT[:, 0, :], start=True, stop=True).then_inc(sem("ss_done"), 1)

        def dve_squares(v, n, added):
            acc, sq, before = nT[:, 0, :], nT[:, 1, :], n // 2

            def one(i, c, s):
                h = low[:, ds(i * (2 * T) + c * T, T)]
                v.wait_ge(sem(added), i * 2 + (c + 1))
                if isinstance(i, int) and (i, c) == (0, 0):
                    v.tensor_tensor(acc, h, h, ALU.mult).then_inc(sem("acc_done"), 1)
                    return
                v.wait_ge(sem("acc_done"), i * 2 + (before * KD + c))
                v.tensor_tensor(sq, h, h, ALU.mult).then_inc(sem("acc_square"), 1)
                v.wait_ge(sem("acc_square"), i * 2 + (before * (KD - 1) + c))
                v.tensor_tensor(acc, acc, sq, ALU.add).then_inc(sem("acc_done"), 1)
            return one

        def pe_linear(pe, name, rhs):
            base, nb, kt = STREAM[name]

            def blk(i, s, first):
                pe.wait_ge(sem(f"w_in{s}"), 16 * (base // 2 + 1) + i * 16)
                for c in range(2):
                    if not first:
                        pe.wait_ge(sem("mm_freed"), i * 4 + (2 * base + 2 * s + c - 3))
                    for k in range(kt):
                        if name == "glu" and c == 0:
                            pe.wait_ge(sem("yg_ready"), k + 1)
                        if base == 0 and first and s == 0 and c == 0 and k % 4 == 0:
                            pe.wait_ge(sem("n_ready"), k + 4)
                        m = pe.matmul(ps[2 * s + c][:, 0:T],
                                      ring[:, s, k * WB + c * P:k * WB + (c + 1) * P], rhs[:, k, :],
                                      start=(k == 0), stop=(k == kt - 1))
                    m.then_inc(sem("mm_done"), 1)

            i0 = 0
            if base == 0:
                blk(0, 0, True)
                blk(0, 1, True)
                i0 = 1
            with pe.Fori(i0, nb // 2) as i:
                blk(i, 0, False)
                blk(i, 1, False)

        def act_norm(act, n, beside=lambda: None):
            for q in range(4 if n in (0, 2) else 0):
                o_act.do(act.activation(nT[:, 4 * q:4 * q + 4, :], hT[:, 4 * q:4 * q + 4, :], ACT.Square),
                         sem("sq_done"))
            beside()
            o_act.do(act.activation(warm[:], ones[:, 0:1], ACT.Sqrt))
            act.wait_ge(sem("ms_ready"), n + 1)
            o_act.do(act.activation(rstd[:], rs[:], ACT.Sqrt), sem("sd_ready"))

        def dve_norm(v, o, n, high=None, lo=None):
            v.wait_ge(sem("ss_done"), n + 1)
            o.do(v.tensor_scalar(rs[:], ps[7][:, 0:T], 1.0 / D, EPS, ALU.mult, ALU.add), sem("ms_ready"))
            v.wait_ge(sem("sd_ready"), n + 1)
            newton(v, o, rstd[:], rs[:], gel[:, 0, :])
            if high is not None and n == 1:
                v.wait_ge(sem("h_spilled"), 48)

            def lower(k):
                if n == 1 and k == 12:
                    v.wait_ge(sem("rest_spilled"), 16)
                v.wait_ge(sem("n_high"), (n - 1) * KD + k + 1)
                o.do(v.tensor_tensor(lo[:, k, :], gel[:, k % 2, :], high[:, k, :].bitcast(F32), ALU.subtract),
                     sem("n_ready"))

            for k in range(KD):
                to = nT[:, k, :] if high is None else gel[:, k % 2, :]
                if high is not None and k >= 2:
                    v.wait_ge(sem("n_ready"), n * KD + k - 1)
                o.do(v.scalar_tensor_tensor(to, hT[:, k, :], gv[:, 16 * n + k:16 * n + k + 1], rstd[:],
                                            ALU.mult, ALU.mult), sem("n_ready" if high is None else "n_full"))
                if high is not None and k:
                    lower(k - 1)
            if high is not None:
                lower(KD - 1)

        def act_norm_high(act, o, n, high, beside=None):
            for k in range(KD):
                if beside is not None:
                    beside(k)
                act.wait_ge(sem("n_full"), (n - 1) * KD + k + 1)
                o.do(act.copy(high[:, k, :], gel[:, k % 2, :]), sem("n_high"))

        def newton(v, o, r, x, t):
            o.settle()
            o.do(v.reciprocal(r, r))
            o.settle()
            o.do(v.tensor_tensor(t, r, r, ALU.mult))
            o.settle()
            o.do(v.scalar_tensor_tensor(t, t, -0.5, x, ALU.mult, ALU.mult))
            o.settle()
            o.do(v.scalar_tensor_tensor(r, t, 1.5, r, ALU.add, ALU.mult))
            o.settle()

        def in_pairs(eng, name, quarter, evac, per=None, o=None, ahead=False):
            base, n = TRIPLE[name]
            ev = evac or (lambda i, c, s: None)
            lead = 1 if name in ("out", "gate") else 0
            if not ahead:
                quarter(0, 0, 0, 0 if base == 0 else 9)
            if lead:
                quarter(0, 1, 1, 1 if base == 0 else 9)
                ev(0, 0, 0)
                quarter(0, 2, 0, 9)
                ev(0, 1, 1)
            with eng.Fori(lead, n // 2 - 1) as i:
                if o is not None:
                    o.loop(i, per)
                quarter(i, 1, 1, 9)
                ev(i, 0, 0)
                quarter(i, 2, 0, 9)
                ev(i, 1, 1)
                if o is not None:
                    o.leave(n // 2 - 1 - lead)
            e = n // 2 - 1
            quarter(e, 1, 1, 9)
            ev(e, 0, 0)
            ev(e, 1, 1)

        def tile_pair(sp, name, src, i):
            base = TRIPLE[name][0]
            for s in range(2):
                if base == 0 and isinstance(i, int) and i == 0:
                    sp.wait_ge(sem("mm_done"), 2 * (STREAM["glu"][0] + STREAM["glu"][1]))
                else:
                    sp.wait_ge(sem("low_done"), i * 8 + 4 * (base + s - 1))
                sp.dma_start(natural[s].rearrange("p (k n) -> p k n", n=P), src(i, s)).then_inc(sem(f"nat_in{s}"), 16)

        def other_tiles(sp, name, src):
            with sp.Fori(1, TRIPLE[name][1] // 2) as i:
                tile_pair(sp, name, src, i)

        def part_of(name, q):
            return (q + 2) % 4 if name == "out" else q

        def three(pe, bank, slot, k, rhs_h, rhs_l, start, stop):
            j = (k % 4) * P
            w_h, w_l = part_h[:, slot, j:j + P], part_l[:, slot, j:j + P]
            pe.matmul(bank, w_h, rhs_h, start=start, stop=False)
            pe.matmul(bank, w_h, rhs_l, start=False, stop=False)
            return pe.matmul(bank, w_l, rhs_h, start=False, stop=stop)

        def pe_quarter(pe, name, i, c, s, q, head, rhs_h, rhs_l):
            base, _ = TRIPLE[name]
            pe.wait_ge(sem("low_done"), i * 8 + (4 * (base + c) + q + 1))
            if head == 9 and isinstance(i, int) and i == 0 and c == 0 and name in NORM_OF:
                pe.wait_ge(sem("n_ready"), NORM_OF[name] * KD + 4 * (q + 1))
            if q == 0 and head > 1:
                pe.wait_ge(sem("tile_freed"), i * 2 + (base + c - 1))
            if name == "out" and isinstance(i, int) and (i, c) == (0, 0):
                if q < 2:
                    pe.wait_ge(sem("ys_split"), 4 * (q + 1))
                else:
                    pe.wait_ge(sem("hm_ready"), 4 * (q - 1))
            for j in range(4):
                k = 4 * part_of(name, q) + j
                m = three(pe, ps[4 + s][:, 0:T], q, k, rhs_h[:, k, :], rhs_l[:, k, :], (q, j) == (0, 0), (q, j) == (3, 3))
            m.then_inc(sem("q_used"), 1)

        def pe_triple(pe, name, rhs_h, rhs_l):
            def quarter(i, c, s, head):
                for q in range(4):
                    pe_quarter(pe, name, i, c, s, q, head, rhs_h, rhs_l)
            in_pairs(pe, name, quarter, None)

        def high_parts(act, o, name, evac, per, only_first=False, ahead=False):
            base, _ = TRIPLE[name]

            def quarter(i, c, s, head):
                act.wait_ge(sem(f"nat_in{s}"), i * 16 + 16 * ((base + c) // 2 + 1))
                for q in range(4):
                    if head > 0:
                        act.wait_ge(sem("q_used"), i * 8 + (4 * (base + c) + q - 3))
                    k = part_of(name, q)
                    o.do(act.copy(part_h[:, q, :], natural[s][:, 512 * k:512 * k + 512]), sem("high_done"))
            if only_first:
                quarter(0, 0, 0, 0 if base == 0 else 9)
                return
            in_pairs(act, name, quarter, evac, {"high_done": 8, **per}, o, ahead)
            o.open = {}

        def low_parts(v, o, name, bank, evac, per, only_first=False, ahead=False):
            base, _ = TRIPLE[name]

            def quarter(i, c, s, head):
                for q in range(4):
                    v.wait_ge(sem("high_done"), i * 8 + (4 * (base + c) + q + 1))
                    k = part_of(name, q)
                    src = natural[s][:, 512 * k:512 * k + 512] if bank is None else bank(q)
                    o.do(v.tensor_tensor(part_l[:, q, :], src, part_h[:, q, :].bitcast(F32), ALU.subtract),
                         sem("low_done"))
            if only_first:
                quarter(0, 0, 0, 0 if base == 0 else 9)
                return
            in_pairs(v, name, quarter, evac, {"low_done": 8, **per}, o, ahead)
            o.open = {}

        NORM_OF = {"wq": 1, "gate": 2}
        o_act = Own(None, sem("act_own"))

        def dve_s5_setup(v, o):
            R = [r32[0:NJ, q, :] for q in range(16)]
            Ar, Ai, dre, th, mag, sn, sh, k, c, t, are, aim, fre, fim = R[:14]
            v.wait_ge(sem("s5_in"), 16 * 9)
            v.wait_ge(sem("dt_ready"), 1)
            for src, dst in ((Ar, dre), (Ai, th)):
                for g in range(2):
                    o.do(v.tensor_scalar(dst[:, g * SP_:(g + 1) * SP_], src[:, g * SP_:(g + 1) * SP_],
                                         dtr[0:NJ, g:g + 1], None, ALU.mult))
            o.settle()
            MAGIC = 1.5 * 2.0 ** 23
            o.do(v.tensor_scalar(k, th, 1.0 / (2 * math.pi), MAGIC, ALU.mult, ALU.add))
            o.settle()
            o.do(v.tensor_scalar(k, k, MAGIC, None, ALU.subtract))
            c1 = 6.28125
            c2 = 0.0019350051879882812
            c3 = 2 * math.pi - c1 - c2
            for cc in (c1, c2, c3):
                o.settle()
                o.do(v.scalar_tensor_tensor(th, k, -cc, th, ALU.mult, ALU.add))
            o.settle()
            o.do(v.tensor_scalar(th, th, 3.1415925, -3.1415925, ALU.min, ALU.max), sem("theta_ready"))
            o.do(v.tensor_reduce(par[:, 4:5], par[:, 0:4], AX.X, ALU.max))
            o.settle()
            o.do(v.tensor_scalar(par[:, 5:6], par[:, 4:5], -1.0, 1.0, ALU.mult, ALU.add))
            o.do(v.tensor_scalar(par[:, 6:7], par[:, 4:5], -1.0, None, ALU.mult))
            o.settle()
            o.do(v.tensor_scalar(par[:, 7:8], par[:, 5:6], -1.0, None, ALU.mult))
            o.settle()
            for q in range(2):
                for g in range(2):
                    o.do(v.tensor_scalar(Cbd[q][:, :, g, :], Cn[q], par[:, 4 + g + 2 * q:5 + g + 2 * q], None, ALU.mult))
                o.do(v.memset(Bbd[q], 0.0))
            v.wait_ge(sem("trig_ready"), 1)
            o.do(v.tensor_tensor(c, sh, sh, ALU.mult))
            o.do(v.tensor_tensor(aim, mag, sn, ALU.mult))
            o.do(v.tensor_tensor(fre, Ar, Ar, ALU.mult))
            o.do(v.tensor_tensor(fim, Ai, Ai, ALU.mult))
            o.settle()
            o.do(v.tensor_scalar(c, c, -2.0, 1.0, ALU.mult, ALU.add))
            o.do(v.tensor_tensor(t, fre, fim, ALU.add))
            o.settle()
            o.do(v.tensor_tensor(are, mag, c, ALU.mult))
            o.do(v.reciprocal(t, t))
            o.settle()
            o.do(v.tensor_scalar(k, are, 1.0, None, ALU.subtract))
            o.do(v.tensor_tensor(fre, aim, Ai, ALU.mult))
            o.do(v.tensor_tensor(fim, aim, Ar, ALU.mult))
            o.settle()
            o.do(v.tensor_tensor(c, k, Ar, ALU.mult))
            o.do(v.tensor_tensor(k, k, Ai, ALU.mult))
            o.settle()
            o.do(v.tensor_tensor(fre, fre, c, ALU.add))
            o.do(v.tensor_tensor(fim, fim, k, ALU.subtract))
            o.settle()
            o.do(v.tensor_tensor(fre, fre, t, ALU.mult))
            o.do(v.tensor_tensor(fim, fim, t, ALU.mult), sem("abf_rows"))
            v.wait_ge(sem("gate_done"), 1)
            v.wait_ge(sem("vec_in"), 16 * 9)
            o.do(v.tensor_scalar(rows8, ps[5][0:8, 0:T], gb8[:, 0:1], None, ALU.add), sem("gate_copied"))
            v.wait_ge(sem("abf_done"), 1)
            o.do(v.tensor_copy(abT, ps[4][:, 0:4 * NJ].rearrange("p (a b) -> p a b", a=4)), sem("abf_copied"))
            o.settle()
            fr, fi = bc(abT[:, 2, :], GC), bc(abT[:, 3, :], GC)
            o.do(v.tensor_tensor(tB[0], Bn[0], fr, ALU.mult))
            o.do(v.tensor_tensor(tB[1], Bn[1], fi, ALU.mult))
            o.do(v.tensor_tensor(tB[2], Bn[1], fr, ALU.mult))
            o.do(v.tensor_tensor(tB[3], Bn[0], fi, ALU.mult))
            o.settle()
            for q, op in ((0, ALU.subtract), (1, ALU.add)):
                for g in range(2):
                    sl = slice(g * SP_, (g + 1) * SP_)
                    o.do(v.tensor_tensor(Bbd[q][sl, :, g, :], tB[2 * q][sl], tB[2 * q + 1][sl], op))
            o.settle()
            o.do(v.tensor_copy(par[:, 0:1], par[:, 0:1]), sem("bd_ready"))
            o.do(v.tensor_copy(par[:, 1:2], par[:, 1:2]), sem("bd_ready"))

        def cmul_add(v, o, dst, a, src, tmp):
            o.do(v.tensor_tensor(tmp[0], a[0], src[0], ALU.mult))
            o.do(v.tensor_tensor(tmp[1], a[1], src[1], ALU.mult))
            o.do(v.tensor_tensor(tmp[2], a[0], src[1], ALU.mult))
            o.do(v.tensor_tensor(tmp[3], a[1], src[0], ALU.mult))
            o.settle()
            o.do(v.tensor_tensor(dst[0], dst[0], tmp[0], ALU.add))
            o.do(v.tensor_tensor(dst[1], dst[1], tmp[2], ALU.add))
            o.settle()
            o.do(v.tensor_tensor(dst[0], dst[0], tmp[1], ALU.subtract))
            o.do(v.tensor_tensor(dst[1], dst[1], tmp[3], ALU.add))
            o.settle()

        def cmul(v, o, dst, a, src, tmp):
            o.do(v.tensor_tensor(tmp[0], a[0], src[0], ALU.mult))
            o.do(v.tensor_tensor(tmp[1], a[1], src[1], ALU.mult))
            o.do(v.tensor_tensor(tmp[2], a[0], src[1], ALU.mult))
            o.do(v.tensor_tensor(tmp[3], a[1], src[0], ALU.mult))
            o.settle()
            o.do(v.tensor_tensor(dst[0], tmp[0], tmp[1], ALU.subtract))
            o.do(v.tensor_tensor(dst[1], tmp[2], tmp[3], ALU.add))
            o.settle()

        CMUL = 8

        def dve_s5_scan(v, o):
            o.settle()
            v.wait_ge(sem("s0_copied"), 1)
            a = [abT[:, 0, :], abT[:, 1, :]]
            pw = [a16[:, 0, :], a16[:, 1, :]]
            g2 = [a16[:, 2, :], a16[:, 3, :]]
            ts = [t[:, :, 0] for t in tS]
            cmul(v, o, pw, a, a, ts)
            for _ in range(3):
                cmul(v, o, pw, pw, pw, ts)
            smp = [s[:, :, TP:T].rearrange("p j (b s) -> p s j b", s=NS) for s in st]
            s0 = [s0T[:, q, :].rearrange("p (b j) -> p j b", j=NJ) for q in range(2)]
            aB = [bc(x, NB) for x in a]
            for s in range(NS):
                src = s0 if s == 0 else [x[:, s - 1] for x in smp]
                cmul_add(v, o, [x[:, s] for x in smp], aB, src, [t[:, :, 0:NB] for t in tS])
            chk = [s[:, :, 0:TP].rearrange("p j (k t) -> p t j k", t=CH) for s in st]
            aC = [bc(x, NCH).unsqueeze(1) for x in a]
            tC = [t.unsqueeze(1) for t in tS]
            with v.Fori(0, CH - 1) as i:
                o.loop(i, {"dve_own": CMUL})
                cmul_add(v, o, [x[:, ds(i + 1, 1)] for x in chk], aC, [x[:, ds(i, 1)] for x in chk], tC)
                o.leave(CH - 1)
            end = [s[:, :, CH - 1:TP:CH] for s in st]
            with v.Fori(0, NCH - 1) as i:
                o.loop(i, {"dve_own": CMUL})
                cmul_add(v, o, [x[:, :, ds(i + 1, 1)] for x in end], [x.unsqueeze(2) for x in pw],
                         [x[:, :, ds(i, 1)] for x in end], [t[:, :, 0:1] for t in tS])
                o.leave(NCH - 1)
            for q in range(2):
                o.do(v.tensor_copy(g2[q], a[q]))
            o.settle()
            n = NCH - 1
            prev = [x[:, :, 0:n].unsqueeze(1) for x in end]
            with v.Fori(0, CH - 1) as i:
                o.loop(i, {"dve_own": CMUL + 6})
                cmul_add(v, o, [x[:, ds(i, 1), :, 1:NCH] for x in chk], [bc(x, n).unsqueeze(1) for x in g2], prev,
                         [t[:, :, 0:n].unsqueeze(1) for t in tS])
                cmul(v, o, g2, g2, a, ts)
                o.leave(CH - 1)
            for q in range(2):
                o.do(v.tensor_copy(send[:, q, 0, :], st[q][:, :, TP - 1]))
                o.do(v.tensor_copy(send[:, q, 1:1 + NB, :],
                                   st[q][:, :, TP + NS - 1:T:NS].rearrange("p j b -> p b j")))
            o.settle()
            o.do(v.tensor_copy(g2[0], g2[0]), sem("s5_ready"))
            o.do(v.tensor_copy(g2[1], g2[1]), sem("send_ready"))

        def flat(x):
            return x.rearrange("p a t -> p (a t)")

        CR = [wk(4096 * i, NB, 2, DH) for i in range(2)]
        ktok = wk(8192, 3, MW)
        vtok = wk(11264, 3, MW)
        kwm = wk(14336, NB, DH)
        S_ = [wk(16384 + 416 * i, 1, 416)[:, 0, :] for i in range(2)]
        n0r = wk(17216, 1, P)[:, 0, :]
        n0T = wk(17344, NB, H, 2)
        ncol = wk(17408, 9, H, 2)
        nrow = wk(17480, 1, P)[:, 0, :]
        m0b = m0[:].rearrange("p (b h) -> p b h", h=H)
        qn = wk(17640, 4, 2, TS)
        w0 = wk(17896, H, TS)
        ntmp = wk(18024, NB, 2)
        nbs = wk(18040, 1, DH)[:, 0, :]
        exf = wk(14336, 8, T)
        rI, rF = exf[:, 0:4, :], exf[:, 4:8, :]
        r2, r3 = mix[:, 4:8, :], mix[:, 0:4, :]
        r4, r5, r6, r7 = (nT[:, 4 * i:4 * i + 4, :] for i in range(4))
        hb, hsq = r4[:, 0:2, :], r4[:, 2:4, :]
        qz = flat(uT[:, 4:8, :]).rearrange("p (s c q) -> p s c q", s=2, c=2)
        pC = zT[:, 0:8, 0:DH]
        mrow = rows8

        def smp4(x):
            return x[:, :, TP:T].rearrange("p h (b s) -> p h b s", s=NS)

        def w_out(i, c):
            return ins["w_out"][0].rearrange("(k p) n -> p k n", p=P)[:, :, ds(i * 256 + c * P, P)]

        def w_q(i, c):
            return ins["peer_w_q"][0].rearrange("(k p) n -> p k n", p=P)[:, :, ds(i * 256 + c * P, P)]

        def sp_mlstm(sp):
            sp.wait_ge(sem("sout_ready"), 1)
            for q, (a, b) in enumerate(((5, 10), (6, 11))):
                sp.dma_start(outs[a][0, 0].rearrange("(j g) p -> j (g p)", g=2), sout[0:NJ, q, :]).then_inc(
                    sem("s5_stored"), 16)
                sp.dma_start(outs[b][0].rearrange("b (j g) p -> (b j) (g p)", g=2).rearrange("(t r) q -> r t q", t=2),
                             sout[:, 2 + 2 * q:4 + 2 * q, :]).then_inc(sem("s5_stored"), 16)
            sp.wait_ge(sem("y_sum"), 8)
            mi = sem("ml_in")
            sp.dma_start(n0r[0:64, :], ins["state_mlstm_n"][0].rearrange("b h (c p) -> (b h c) p", p=P)).then_inc(mi, 16)

            def c_load(h):
                if h >= 2:
                    sp.wait_ge(sem(f"c_out{h % 2}"), 16 * NB * (h // 2))
                for b in range(NB):
                    sp.dma_start(CR[h % 2][:, b], ins["state_mlstm_C"][0, b, h].rearrange("(c p) e -> p c e", p=P)
                                 ).then_inc(sem(f"c_in{h % 2}"), 16)

            def c_store(h):
                sp.wait_ge(sem("cn_read"), NB * (h + 1))
                for b in range(NB):
                    sp.dma_start(outs[7][0, b, h].rearrange("(c p) e -> p c e", p=P), CR[h % 2][:, b]).then_inc(
                        sem(f"c_out{h % 2}"), 16)

            c_load(0)
            c_load(1)
            tile_pair(sp, "out", w_out, 0)
            for h in range(H):
                c_store(h)
                if h + 2 < H:
                    c_load(h + 2)
            for h in range(H):
                sp.wait_ge(sem("pc_copied"), h + 1)
                sp.dma_start(outs[2][0, 0, h].rearrange("(c p) e -> p c e", p=P), pC[:, 2 * h:2 * h + 2, :]).then_inc(
                    sem("ml_stored"), 16)
            sp.wait_ge(sem("nrow_copied"), 1)
            sp.dma_start(outs[3][0, 0].rearrange("h (c p) -> (h c) p", p=P), nrow[0:8, :]).then_inc(sem("ml_stored"), 16)
            sp.dma_start(outs[8][0].rearrange("b h (c p) -> (b h c) p", p=P), nrow[8:72, :]).then_inc(sem("ml_stored"), 16)
            sp.wait_ge(sem("mrow_ready"), 1)
            sp.dma_start(outs[4][0], mrow[0:1, 0:4]).then_inc(sem("ml_stored"), 16)
            sp.dma_start(outs[9].rearrange("a b h -> a (b h)"), mrow[0:1, 4:36]).then_inc(sem("ml_stored"), 16)
            sp.wait_ge(sem("s5_stored"), 64)
            sp.wait_ge(sem("ml_stored"), 16 * 8)
            for s in range(2):
                sp.wait_ge(sem(f"c_out{s}"), 16 * NB * 2)

        def pe_mlstm(pe):
            pe.wait_ge(sem("ml_in"), 16)
            pe.wait_ge(sem("bc_copied"), 5)
            pe.transpose(ps[4][:, 0:64], n0r[0:64, :], ident[0:64, 0:64]).then_inc(sem("n0_done"), 1)
            pe.wait_ge(sem("mm_freed"), 2 * (STREAM["glu"][0] + 4))
            for g in range(12):
                arr, rest = divmod(g, 6)
                i, half = divmod(rest, 2)
                t0, n = TOK[i]
                if g >= 4:
                    pe.wait_ge(sem("tok_copied"), g - 3)
                for j in range(4):
                    m = pe.transpose(ps[g % 4][0:n, j * P:(j + 1) * P],
                                     zT[:, 8 + 8 * arr + 4 * half + j, t0:t0 + n], ident[:])
                m.then_inc(sem("tok_done"), 1)
            pe.wait_ge(sem("wk_ready"), 1)
            pe.wait_ge(sem("bc_copied"), 8)
            for q, row in enumerate((rI, r7)):
                for i, (t0, n) in enumerate(TOK):
                    for h in range(H):
                        c = 12 * q + 4 * i + h
                        m = pe.matmul(ps[5][0:n, c:c + 1], row[0:1, h, t0:t0 + n], ones[0:1, 0:1], start=True, stop=True)
            m.then_inc(sem("col_done"), 1)
            pe.wait_ge(sem("col_copied"), 1)
            pe.wait_ge(sem("n0_copied"), 1)
            pe.wait_ge(sem("tok_copied"), 12)
            def products_with_q(h):
                S, C, hs = S_[h % 2], CR[h % 2], h % 2
                qs = [zT[:, 2 * h + c, :] for c in range(2)]
                ks = [zT[:, 8 + 2 * h + c, :] for c in range(2)]
                if h >= 1:
                    pe.wait_ge(sem("sw_ready"), h)
                for c in range(2):
                    pe.matmul(ps[0][:, 0:256], ks[c][:, 0:128], qs[c][:, 0:256], start=(c == 0), stop=(c == 1))
                for c in range(2):
                    pe.matmul(ps[0][:, 256:384], ks[c][:, 128:256], qs[c][:, 128:256], start=(c == 0), stop=(c == 1))
                for c in range(2):
                    m = pe.matmul(ps[0][0:TS, 384:384 + TS], ks[c][:, TP:T], qs[c][:, TP:T], start=(c == 0), stop=(c == 1))
                m.then_inc(sem("sc_done"), 1)
                pe.wait_ge(sem("qn_ready"), h + 1)
                pe.wait_ge(sem(f"c_in{h % 2}"), 16 * NB * (h // 2 + 1))
                if h >= 1:
                    pe.wait_ge(sem("pc_copied"), h)
                for b in range(NB):
                    for c in range(2):
                        m = pe.matmul(ps[4][0:TS, 0:DH], qz[:, hs, c, TS * b:TS * (b + 1)], C[:, b, c, :],
                                      start=(b == 0 and c == 0), stop=(b == NB - 1 and c == 1))
                m.then_inc(sem("qc_done"), 1)

            products_with_q(0)
            for h in range(H):
                S, hs = S_[h % 2], h % 2
                pe.wait_ge(sem("sw_ready"), h + 1)
                if h >= 1:
                    pe.wait_ge(sem("hms_ready"), h)
                    pe.wait_ge(sem("hb_ready"), 2 * h)

                def both(bank, lhs, before):
                    pe.matmul(bank[:, 0:128], lhs(0), S[:, 0:128], start=True, stop=True)
                    pe.matmul(bank[:, 128:256], lhs(0), S[:, 128:256], start=True, stop=False)
                    pe.matmul(bank[:, 128:256], lhs(1), S[:, 256:384], start=False, stop=True)
                    before(bank)
                    return pe.matmul(bank[:, TP:T], lhs(2), S[0:TS, 384:416], start=False, stop=True)

                def den_before(bank):
                    for c in range(2):
                        pe.matmul(bank[:, TP:T], ones[:], qn[:, 2 + c, hs, :], start=(c == 0), stop=False)

                both(ps[1], lambda i: ones[0:TOK[i][1], :], den_before).then_inc(sem("den_done"), 1)
                for e in range(2):
                    c0 = h * DH + e * P

                    def num_before(bank):
                        pe.wait_ge(sem("qc_copied"), h + 1)
                        pe.matmul(bank[:, TP:T], nbs[0:TS, e * P:(e + 1) * P], ident[0:TS, 0:TS], start=True, stop=False)

                    both(ps[2 + e], lambda i: vtok[0:TOK[i][1], i, c0:c0 + P], num_before).then_inc(sem("num_done"), 1)
                pe.wait_ge(sem("kw_ready"), 1)
                if h >= 1:
                    pe.wait_ge(sem("nc_read"), h)
                for c in range(2):
                    for i in range(2):
                        pe.matmul(ps[4][:, c * DH:(c + 1) * DH], ktok[:, i, h * DH + c * P:h * DH + (c + 1) * P],
                                  vtok[:, i, h * DH:(h + 1) * DH], start=(i == 0), stop=(i == 1))
                for c in range(2):
                    for i in range(2):
                        m = pe.matmul(ps[5][:, c:c + 1], ktok[:, i, h * DH + c * P:h * DH + (c + 1) * P],
                                      ones[:, 0:1], start=(i == 0), stop=(i == 1))
                for c in range(2):
                    m = pe.matmul(ps[5][:, 2 + NB * c:2 + NB * (c + 1)], ktok[0:TS, 2, h * DH + c * P:h * DH + (c + 1) * P],
                              bmask, start=True, stop=True)
                m.then_inc(sem("pc_done"), 1)
                pe.wait_ge(sem("kwm_ready"), h + 1)
                for b in range(NB):
                    at = NB * h + b
                    if at >= 2:
                        pe.wait_ge(sem("cn_read"), at - 1)
                    bank = ps[6 + at % 2]
                    for c in range(2):
                        m = pe.matmul(bank[:, c * DH:(c + 1) * DH], kwm[0:TS, b, c * P:(c + 1) * P],
                                      vtok[0:TS, 2, h * DH:(h + 1) * DH], start=True, stop=True)
                    m.then_inc(sem("cn_done"), 1)
                if h + 1 < H:
                    products_with_q(h + 1)
                pe.wait_ge(sem("hsq_done"), h + 1)
                for e in range(2):
                    m = pe.matmul(ps[1][:, 0:T], ones[:], hsq[:, e, :], start=(e == 0), stop=(e == 1))
                m.then_inc(sem("hss_done"), 1)
            pe.wait_ge(sem("nc_read"), H)
            pe.transpose(ps[5][0:72, 0:P], ncol.rearrange("p a b c -> p (a b c)"), ident[:]).then_inc(sem("nrow_done"), 1)

        def act_mlstm(act, o):
            act.wait_ge(sem("n0_done"), 1)
            o.do(act.copy(n0T.rearrange("p a b c -> p (a b c)"), ps[4][:, 0:64]), sem("n0_copied"))
            for g in range(12):
                arr, rest = divmod(g, 6)
                i, half = divmod(rest, 2)
                n = TOK[i][1]
                act.wait_ge(sem("tok_done"), g + 1)
                dst = [ktok, vtok][arr]
                o.do(act.copy(dst[0:n, i, 512 * half:512 * half + 512], ps[g % 4][0:n, 0:512]), sem("tok_copied"))
            act.wait_ge(sem("m_ready"), 1)
            o.settle()
            o.do(act.activation(r2, r6, ACT.Exp, scale=-1.0))
            o.do(act.activation(w0, w0, ACT.Exp))
            o.do(act.activation(r7, r7, ACT.Exp), sem("wk_ready"))
            def weights_of(h):
                S = S_[h % 2]
                act.wait_ge(sem("sarg_ready"), h + 1)
                o.do(act.activation(S[:, 0:384], S[:, 0:384], ACT.Exp, scale=-1.0))
                o.do(act.activation(S[0:TS, 384:416], S[0:TS, 384:416], ACT.Exp, scale=-1.0), sem("sexp_ready"))
                act.wait_ge(sem("qc_done"), h + 1)
                o.do(act.copy(nbs[0:TS, :], ps[4][0:TS, 0:DH]), sem("qc_copied"))

            weights_of(0)
            for h in range(H):
                act.wait_ge(sem("pc_done"), h + 1)
                o.do(act.copy(pC[:, 2 * h:2 * h + 2, :], ps[4][:, 0:512].rearrange("p (a b) -> p a b", a=2)),
                     sem("pc_copied"))
                act.wait_ge(sem("hb_ready"), 2 * h + 2)
                if h >= 1:
                    act.wait_ge(sem("hss_done"), h)
                o.do(act.activation(hsq, hb, ACT.Square), sem("hsq_done"))
                if h + 1 < H:
                    weights_of(h + 1)
                else:
                    high_parts(act, o, "out", None, {}, only_first=True)
                act.wait_ge(sem("hms_ready"), h + 1)
                o.do(act.activation(rstd[:], rs[:], ACT.Sqrt), sem("hsd_ready"))
            act.wait_ge(sem("nrow_done"), 1)
            o.do(act.copy(nrow[0:72, :], ps[5][0:72, 0:P]), sem("nrow_copied"))

        def split_mix(v, o, c0, n, name):
            o.settle()
            for c in range(c0, c0 + n):
                o.do(v.tensor_copy(mix_h[:, c, :], mix[:, c, :]))
            o.settle()
            for c in range(c0, c0 + n):
                o.do(v.tensor_tensor(mix_l[:, c, :], mix[:, c, :], mix_h[:, c, :].bitcast(F32), ALU.subtract), sem(name))

        def dve_gate_rows(v, o):
            v.wait_ge(sem("mm_done"), 2 * (STREAM["z"][0] + STREAM["z"][1]))
            v.wait_ge(sem("ln_ready"), 1)
            v.wait_ge(sem("m0_in"), 16)
            o.settle()
            o.do(v.memset(r7, 1.0))
            o.do(v.scalar_tensor_tensor(flat(rF), flat(rF), 0.0, flat(r2), ALU.min, ALU.subtract))
            o.settle()
            o.do(v.memset(r7[:, :, 0:1], 0.0))
            o.do(v.memset(r7[:, :, TP:T:NS], 0.0))
            o.settle()
            o.do(v.tensor_tensor_scan(flat(r3), flat(r7), flat(rF), 0.0, ALU.mult, ALU.add))
            o.settle()
            o.do(v.tensor_tensor(flat(rI), flat(rI), flat(r3), ALU.subtract))
            o.do(v.tensor_scalar(flat(r7), flat(r7), 1.0, -NEG, ALU.subtract, ALU.mult))
            o.settle()
            o.do(v.tensor_copy(flat(r4), flat(rI)))
            o.settle()
            o.do(v.tensor_scalar(r4[:, :, 0:1], r4[:, :, 0:1], 0.0, None, ALU.max))
            first = r4[:, :, TP:T:NS]
            o.do(v.tensor_tensor(first, first, m0b.rearrange("p b h -> p h b"), ALU.max))
            o.settle()
            o.do(v.tensor_tensor_scan(flat(r5), flat(r7), flat(r4), 0.0, ALU.add, ALU.max))
            o.settle()
            o.do(v.tensor_tensor(flat(r6), flat(r3), flat(r5), ALU.add))
            w4 = w0.rearrange("p h (b s) -> p h b s", s=NS)
            o.do(v.tensor_tensor(w4, bc(m0b.rearrange("p b h -> p h b"), NS), smp4(r5), ALU.subtract))
            o.do(v.tensor_tensor(r7[:, :, 0:TP], rI[:, :, 0:TP], r5[:, :, TP - 1:TP].to_broadcast([P, H, TP]),
                                 ALU.subtract))
            o.do(v.tensor_tensor(smp4(r7), smp4(rI), smp4(r5)[:, :, :, NS - 1:NS].to_broadcast([P, H, NB, NS]),
                                 ALU.subtract))
            o.settle()
            o.do(v.tensor_copy(mrow[0:1, 0:4], r6[0:1, :, TP - 1]), sem("m_ready"))
            v.wait_ge(sem("bc_done"), 8)
            o.do(v.tensor_copy(mrow[0:1, 4:36].rearrange("p (b h) -> p b h", h=H),
                               r6[0:1, :, TP + NS - 1:T:NS].rearrange("p h b -> p b h")), sem("mrow_ready"))

        def dve_mlstm(v, o):
            v.wait_ge(sem("col_done"), 1)
            for q in range(2):
                o.do(v.tensor_copy(cols[:, 12 * q:12 * q + 8], ps[5][:, 12 * q:12 * q + 8]))
                o.do(v.tensor_copy(cols[0:TS, 12 * q + 8:12 * q + 12], ps[5][0:TS, 12 * q + 8:12 * q + 12]))
            o.settle()
            v.wait_ge(sem("tok_copied"), 12)
            def scale_k(i):
                n = TOK[i][1]
                for h in range(H):
                    a = ktok[0:n, i, h * DH:(h + 1) * DH]
                    s = sem("col_copied") if (i, h) == (2, 0) else sem("kw_ready") if (i, h) == (1, H - 1) else None
                    o.do(v.tensor_scalar(a, a, cols[0:n, 12 + 4 * i + h:13 + 4 * i + h], DH ** -0.5, ALU.mult, ALU.mult), s)

            scale_k(2)
            v.wait_ge(sem("n0_copied"), 1)
            o.do(v.memset(flat(uT[:, 4:8, :]), 0.0))
            o.settle()
            def weights_of(h):
                S, hs = S_[h % 2], h % 2
                if h >= 2:
                    v.wait_ge(sem("num_done"), 2 * (h - 1))
                for i, (lo, hi, t0) in enumerate(((0, 256, 0), (256, 384, 128), (384, 416, TP))):
                    n = TOK[i][1]
                    o.do(v.tensor_scalar(S[0:n, lo:hi], r5[0:n, h, t0:t0 + hi - lo], cols[0:n, 4 * i + h:4 * i + h + 1],
                                         0.0, ALU.subtract, ALU.max), sem("sarg_ready") if i == 2 else None)
                qs = zT[:, 2 * h:2 * h + 2, TP:T]
                o.do(v.tensor_tensor(qn[:, 0:2, hs, :], qs, w0[:, h:h + 1, :].to_broadcast([P, 2, TS]), ALU.mult))
                for c in range(2):
                    o.do(v.tensor_tensor(qz[:, hs, c, :].rearrange("p (b r) -> p b r", r=TS + NS)[:, :, 0:NS],
                                         qs[:, c, :].rearrange("p (b s) -> p b s", s=NS),
                                         w0[:, h, :].rearrange("p (b s) -> p b s", s=NS), ALU.mult))
                o.settle()
                for c in range(2):
                    o.do(v.tensor_tensor(qn[:, 2 + c, hs, :].rearrange("p (b s) -> p b s", s=NS),
                                         qn[:, c, hs, :].rearrange("p (b s) -> p b s", s=NS), bc(n0T[:, :, h, c], NS),
                                         ALU.mult), sem("qn_ready") if c == 1 else None)
                if h >= 1:
                    v.wait_ge(sem("cn_done"), NB * h)
                o.do(v.tensor_tensor(kwm[0:TS], ktok[0:TS, 2:3, h * DH:(h + 1) * DH].to_broadcast([TS, NB, DH]),
                                     bc(bmask, DH), ALU.mult), sem("kwm_ready"))
                v.wait_ge(sem("sexp_ready"), h + 1)
                v.wait_ge(sem("sc_done"), h + 1)
                o.do(v.scalar_tensor_tensor(S[:, 0:384], ps[0][:, 0:384], DH ** -0.5, S[:, 0:384], ALU.mult, ALU.mult))
                o.do(v.scalar_tensor_tensor(S[0:TS, 384:416], ps[0][0:TS, 384:416], DH ** -0.5, S[0:TS, 384:416],
                                            ALU.mult, ALU.mult))
                o.settle()
                o.do(v.tensor_tensor(S[:, 0:128], S[:, 0:128], tri, ALU.mult))
                o.do(v.tensor_tensor(S[:, 256:384], S[:, 256:384], tri, ALU.mult))
                o.do(v.tensor_tensor(S[0:TS, 384:416], S[0:TS, 384:416], trs, ALU.mult), sem("sw_ready"))

            weights_of(0)
            scale_k(0)
            scale_k(1)
            split_mix(v, o, 8, 8, "ys_split")
            for h in range(H):
                v.wait_ge(sem("den_done"), h + 1)
                o.do(v.tensor_tensor(rs[:], ps[1][:, 0:T], r2[:, h, :], ALU.max))
                o.settle()
                o.do(v.scalar_tensor_tensor(rs[:], ps[1][:, 0:T], -1.0, rs[:], ALU.mult, ALU.max))
                o.settle()
                o.do(v.reciprocal(rs[:], rs[:]))
                o.settle()
                for e in range(2):
                    v.wait_ge(sem("num_done"), 2 * h + e + 1)
                    o.do(v.tensor_tensor(hb[:, e, :], ps[2 + e][:, 0:T], rs[:], ALU.mult), sem("hb_ready"))
                for b in range(NB):
                    v.wait_ge(sem("cn_done"), NB * h + b + 1)
                    cs = CR[h % 2][:, b].rearrange("p a b -> p (a b)")
                    o.do(v.scalar_tensor_tensor(cs, cs, w0[:, h, NS * b + NS - 1:NS * b + NS],
                                                ps[6 + b % 2][:, 0:512], ALU.mult, ALU.add), sem("cn_read"))
                o.do(v.tensor_copy(ncol[:, 0, h, :], ps[5][:, 0:2]))
                o.do(v.tensor_tensor(ntmp, n0T[:, :, h, :], bc(w0[:, h, NS - 1:TS:NS], 2), ALU.mult))
                o.settle()
                o.do(v.tensor_tensor(ncol[:, 1:9, h, :], ntmp, ps[5][:, 2:18].rearrange("p (c b) -> p b c", c=2),
                                     ALU.add), sem("nc_read"))
                if h + 1 < H:
                    weights_of(h + 1)
                else:
                    low_parts(v, o, "out", None, None, {}, only_first=True)
                v.wait_ge(sem("hss_done"), h + 1)
                o.do(v.tensor_scalar(rs[:], ps[1][:, 0:T], 1.0 / DH, EPS, ALU.mult, ALU.add), sem("hms_ready"))
                v.wait_ge(sem("hsd_ready"), h + 1)
                newton(v, o, rstd[:], rs[:], r7[:, 0, :])
                for e in range(2):
                    o.do(v.scalar_tensor_tensor(hb[:, e, :], hb[:, e, :], gv[:, 64 + 2 * h + e:65 + 2 * h + e], rstd[:],
                                                ALU.mult, ALU.mult))
                o.settle()
                v.wait_ge(sem("og_ready"), 1)
                for e in range(2):
                    o.do(v.tensor_tensor(mix[:, 2 * h + e, :], hb[:, e, :], zT[:, 24 + 2 * h + e, :], ALU.mult))
                split_mix(v, o, 2 * h, 2, "hm_ready")

        qpT = wk(0, 8, T)
        keyn = wk(2304, 16, 64)
        keyT = wk(3328, PH, PK)
        scr = wk(4352, 3, 16 * PK)
        tv = wk(10496, 16, TK)
        ti = work[:, 10752:11008].bitcast(U32).rearrange("p (a b) -> p a b", b=TK)
        tf = wk(11008, 16, TK)
        cand = wk(11264, PH, TK, TK)
        vs = wk(13312, PH, TK)
        ic = work[:, 13440:13568].bitcast(U32)
        ia = work[:, 13568:13696].bitcast(U32)
        iF = [wk(13696, 1, P)[:, 0, :], wk(13824, 1, P)[:, 0, :]]
        eq = wk(13952, PH, TK, TK)
        tok3 = wk(16000, 3, 3, P)
        gsum = wk(17152, 2, PH)
        dense = wk(0, P, T)
        ohA = [ring[:, 1, 512 * s:512 * s + 512].rearrange("p (a b) -> p a b", b=P) for s in range(4)]
        ohB = [ring[:, 1, 2048 + 512 * s:2560 + 512 * s].rearrange("p (a b) -> p a b", b=P) for s in range(4)]
        OH_ACT = [1, 2, 1, 2]
        nkey, ngate = rs, rstd
        far = gel[:].rearrange("p a t -> p (a t)")[:, 0:512].rearrange("p (a k) -> p a k", k=P)
        u_v = ins["peer_u"][0].rearrange("(a b) d -> a b d", b=PK)
        v_v = ins["peer_v"][0].rearrange("(a b) d -> a b d", b=PK)
        WQ_END = sum(TRIPLE["wq"])
        UB = TRIPLE["Ua"][0]
        K0 = PK - UA
        vh = alias("v_high", ring_at + 16384, 2, 1024)
        vl = alias("v_low", ring_at + 16384 + 8192, 2, 1024)
        NSP = T // 16

        def sp_peer(sp):
            sp.wait_ge(sem("q_used"), 4 * KD)
            sp.dma_start(keyn, ins["peer_keys"][0].rearrange("h c k d -> k (h c) d")).then_inc(sem("key_in"), 16)
            sp.wait_ge(sem("low_done"), 4 * WQ_END)
            for s in range(2):
                sp.dma_start(natural[s], u_v[:, K0 + s, :]).then_inc(sem(f"nat_in{s}"), 16)
            for first, last, behind, key in ((1, UA // 2, 0, K0), (0, K0 // 2, UA, 0)):
                with sp.Fori(first, last) as i:
                    for s in range(2):
                        sp.wait_ge(sem("turned"), i * 8 + 4 * (behind + s - 1))
                        sp.dma_start(natural[s], u_v[:, ds(i * 2 + (key + s), 1), :].rearrange("a b d -> a (b d)")).then_inc(
                            sem(f"nat_in{s}"), 16)
            sp.wait_ge(sem("turned"), 4 * PK)
            for half in range(2):
                cs = slice(half * 1024, half * 1024 + 1024)
                first = 0
                if half == 0:
                    for s in range(2):
                        sp.dma_start(natural[s].rearrange("p (a b) -> p a b", a=2), v_v[:, 2 * s:2 * s + 2, cs]).then_inc(
                            sem(f"v_in{s}"), 16)
                    sp.wait_ge(sem("q_used"), 4 * (UB + PK))
                    sp.dma_start(low[:, 0:KD * T], spill).then_inc(sem("h_back"), 16)
                    first = 1
                with sp.Fori(first, 32) as i:
                    for s in range(2):
                        sp.wait_ge(sem("vl_done"), i * 4 + (128 * half + 2 * s - 2))
                        sp.dma_start(natural[s].rearrange("p (a b) -> p a b", a=2), v_v[:, ds(i * 4 + 2 * s, 2), cs]).then_inc(
                            sem(f"v_in{s}"), 16)

        def pe_peer(pe):
            pe.wait_ge(sem("key_in"), 16)
            for g in range(2):
                for j in range(4):
                    h = 4 * g + j
                    m = pe.transpose(ps[g][:, j * P:(j + 1) * P], keyn[:, 2 * h:2 * h + 2, :].rearrange("p a b -> p (a b)"),
                                     ident[:])
                m.then_inc(sem("key_done"), 1)
            pe.wait_ge(sem("key_copied"), 2)
            pe.wait_ge(sem("tile_freed"), WQ_END)
            for i, (t0, n) in enumerate(TOK):
                for g in range(2):
                    if i:
                        pe.wait_ge(sem("scr_copied"), 4 * (i - 1) + 2 * g + 2)
                    for j in range(4):
                        for c in range(2):
                            m = pe.matmul(ps[2 * g + c][0:n, j * P:(j + 1) * P],
                                          qpT[64 * c:64 * c + 64, 4 * g + j, t0:t0 + n],
                                          keyT[64 * c:64 * c + 64, 4 * g + j, :], start=True, stop=True)
                            if j == 3:
                                m.then_inc(sem("scr_done"), 1)
            def turn(base, i, c, s, q, first=False):
                if q == 0:
                    pe.wait_ge(sem(f"nat_in{s}"), i * 16 + 16 * ((base + c) // 2 + 1))
                if not first:
                    pe.wait_ge(sem("low_done"), i * 8 + (4 * (base + c) + q - 3))
                for j in range(4):
                    k = 4 * q + j
                    m = pe.transpose(ps[q][:, j * P:(j + 1) * P], natural[s][:, k * P:(k + 1) * P], ident[:])
                m.then_inc(sem("turned"), 1)

            def dots(name, i, c, s, last=False):
                base = TRIPLE[name][0]
                for q in range(4):
                    if q < 2:
                        turn(base, i, c, s, q + 2)
                    elif not last:
                        turn(base, i, c + 1, 1 - s, q - 2)
                    pe_quarter(pe, name, i, c, s, q, 9, ffn_h, ffn_l)

            def experts(name):
                base, n = TRIPLE[name]
                turn(base, 0, 0, 0, 0, True)
                turn(base, 0, 0, 0, 1, True)
                with pe.Fori(0, n // 2 - 1) as i:
                    dots(name, i, 0, 0)
                    dots(name, i, 1, 1)
                dots(name, n // 2 - 1, 0, 0)
                dots(name, n // 2 - 1, 1, 1, True)

            pe.wait_ge(sem("scr_copied"), 12)
            experts("Ua")
            pe.wait_ge(sem("tile_freed"), UB + UA)
            for i, (t0, n) in enumerate(TOK):
                pe.wait_ge(sem("tok3_ready"), i + 1)
                for q in range(3):
                    m = pe.transpose(ps[4 + q][:, t0:t0 + n], tok3[0:n, i, q, :], ident[0:n, 0:n])
            m.then_inc(sem("ex3_done"), 1)

            def spread(i, s, first):
                pe.wait_ge(sem("oh_ready"), i * 4 + (s + 1))
                pe.wait_ge(sem("oh_act"), i * sum(OH_ACT) + sum(OH_ACT[:s + 1]))
                if not first:
                    pe.wait_ge(sem("g_scaled"), i * 4 + (s - 3))
                for j in range(4):
                    m = pe.matmul(ps[s][:, j * P:(j + 1) * P], ohA[s][:, j, :], ohB[s][:, j, :], start=True, stop=True)
                m.then_inc(sem("g_done"), 1)

            for s in range(4):
                spread(0, s, True)
            with pe.Fori(1, NSP) as i:
                for s in range(4):
                    spread(i, s, False)
            pe.wait_ge(sem("g_scaled"), 4 * NSP)
            experts("Ub")

            pe.wait_ge(sem("tile_freed"), UB + PK)
            for half in range(2):
                if half:
                    pe.wait_ge(sem("pv_added"), 8)

                def keys(i, kind):
                    for j in range(8):
                        s = j % 2
                        a_h, a_l = act_h[:, j % 4, :], act_l[:, j % 4, :]
                        pe.wait_ge(sem("vh_done"), i * 8 + (128 * half + j + 1))
                        pe.wait_ge(sem("al_done"), i * 8 + (128 * half + j + 1))
                        st_, sp_ = kind == 0 and j == 0, kind == 2 and j == 7
                        for c in range(8):
                            w_h = vh[:, s, c * P:(c + 1) * P]
                            pe.matmul(ps[c][:, 0:T], w_h, a_h, start=st_, stop=False)
                            pe.matmul(ps[c][:, 0:T], w_h, a_l, start=False, stop=False)
                        pe.wait_ge(sem("vl_done"), i * 8 + (128 * half + j + 1))
                        for c in range(8):
                            m = pe.matmul(ps[c][:, 0:T], vl[:, s, c * P:(c + 1) * P], a_h, start=False, stop=sp_)
                        m.then_inc(sem("v_done"), 1)
                keys(0, 0)
                with pe.Fori(1, PK // 8 - 1) as i:
                    keys(i, 1)
                keys(PK // 8 - 1, 2)

        def act_peer(act, o):
            def copy_q(i, c, s):
                act.wait_ge(sem("q_used"), i * 8 + 4 * (TRIPLE["wq"][0] + c + 1))
                o.do(act.copy(work[:, ds(i * (2 * T) + c * T, T)], ps[4 + s][:, 0:T]), sem("tile_freed"))

            high_parts(act, o, "wq", copy_q, {"tile_freed": 2}, ahead=True)
            for g in range(2):
                act.wait_ge(sem("key_done"), g + 1)
                o.do(act.copy(keyT[:, 4 * g:4 * g + 4, :], ps[g][:, 0:512].rearrange("p (a b) -> p a b", b=P)),
                     sem("key_copied"))
            for i, (t0, n) in enumerate(TOK):
                for b in range(4):
                    act.wait_ge(sem("scr_done"), 4 * i + b + 1)
                    dst = scr[0:n, i, :].rearrange("p (h c k) -> p h c k", c=2, k=PK)[:, 4 * (b // 2):4 * (b // 2) + 4, b % 2, :]
                    o.do(act.copy(dst, ps[b][0:n, 0:512].rearrange("p (h k) -> p h k", k=PK)), sem("scr_copied"))
            def high(name):
                base = TRIPLE[name][0]

                def quarters(i, c, s, head):
                    for q in range(4):
                        act.wait_ge(sem("turned"), i * 8 + (4 * (base - UB + c) + q + 1))
                        act.wait_ge(sem("q_used"), i * 8 + (4 * (base + c) + q - 3))
                        o.do(act.copy(part_h[:, q, :], ps[q][:, 0:512]), sem("high_done"))
                return quarters

            def gelu_first(i, c, s):
                act.wait_ge(sem("q_used"), i * 8 + 4 * (UB + c + 1))
                o.do(act.activation(work[:, ds(i * (2 * T) + (K0 + c) * T, T)], ps[4 + s][:, 0:T], ACT.Gelu_apprx_tanh),
                     sem("tile_freed"))

            def gelu(i, c, s):
                b = TRIPLE["Ub"][0]
                act.wait_ge(sem("q_used"), i * 8 + 4 * (b + c + 1))
                act.wait_ge(sem("tile_freed"), i * 2 + (b + c - 1))
                o.do(act.activation(gel[:, s, :], ps[4 + s][:, 0:T], ACT.Gelu_apprx_tanh), sem("gelu_done"))

            in_pairs(act, "Ua", high("Ua"), gelu_first, {"high_done": 8, "tile_freed": 2}, o)
            o.open = {}
            for i in range(3):
                act.wait_ge(sem("vdiff_ready"), i + 1)
                n = TOK[i][1]
                g = tok3[0:n, i, 2, :]
                o.do(act.activation(g, g, ACT.Exp), sem("vexp_ready"))
            act.wait_ge(sem("ex3_done"), 1)
            for q in range(3):
                o.do(act.copy(ex3[:, q, :], ps[4 + q][:, 0:T]), sem("ex3_copied"))
            o.do(act.mul(nkey[:], ps[4][:, 0:T], -1.0))
            o.do(act.mul(ngate[:], ps[6][:, 0:T], -1.0))
            act.wait_ge(sem("spread_free"), 1)
            o.settle()

            def distances(i, s):
                for j in range(OH_ACT[s]):
                    t = i * 16 + (4 * s + j)
                    o.do(act.activation(far[:, 2 * (s % 2) + j, :], iota[:], ACT.Abs, bias=nkey[:, ds(t, 1)]), sem("act_far"))

            def rows(i, s):
                act.wait_ge(sem("act_far"), i * sum(OH_ACT) + sum(OH_ACT[:s + 1]))
                for j in range(OH_ACT[s]):
                    t = i * 16 + (4 * s + j)
                    o.do(act.activation(ohA[s][:, j, :], far[:, 2 * (s % 2) + j, :], ACT.Relu, scale=ngate[:, ds(t, 1)],
                                        bias=ex3[:, 2, ds(t, 1)]), sem("oh_act"))

            def copy_gates(i, s):
                act.wait_ge(sem("g_done"), i * 4 + (s + 1))
                o.do(act.copy(dense[:, 0:K0, ds(i * 16 + 4 * s, 4)],
                              ps[s][:, 0:512].rearrange("p (t k) -> p k t", k=P)[:, 0:K0, :]), sem("g_copied"))

            for s in range(4):
                if s >= 2:
                    act.wait_ge(sem("oh_act"), sum(OH_ACT[:s - 1]))
                distances(0, s)
                rows(0, s)
            with act.Fori(0, NSP - 1) as i:
                for s in range(4):
                    act.wait_ge(sem("oh_act"), i * sum(OH_ACT) + (sum(OH_ACT) + sum(OH_ACT[:s]) - OH_ACT[s - 1]))
                    distances(i + 1, s)
                    copy_gates(i, s)
                    rows(i + 1, s)
            for s in range(4):
                copy_gates(NSP - 1, s)
            o.open = {}
            in_pairs(act, "Ub", high("Ub"), gelu, {"high_done": 8, "gelu_done": 2}, o)
            o.open = {}
            act.wait_ge(sem("q_used"), 4 * (UB + PK))
            act.wait_ge(sem("tile_freed"), UB + PK)
            for half in range(2):
                def four(i, head):
                    for s in range(4):
                        if s % 2 == 0:
                            act.wait_ge(sem(f"v_in{s // 2}"), i * 16 + (16 * 32 * half + 16))
                        o.do(act.copy(act_h[:, s, :], work[:, ds(i * (4 * T) + s * T, T)]), sem("ah_done"))
                        if not (head and s < 2):
                            act.wait_ge(sem("v_done"), i * 4 + (128 * half + s - 1))
                        o.do(act.copy(vh[:, s % 2, :], natural[s // 2][:, 1024 * (s % 2):1024 * (s % 2) + 1024]),
                             sem("vh_done"))
                if half == 0:
                    four(0, True)
                with act.Fori(1 - half, 32) as i:
                    o.loop(i, {"vh_done": 4, "ah_done": 4})
                    four(i, False)
                    o.leave(31 + half)
                o.open = {}

        def dve_peer(v, o):
            hr = "p (h r) -> p h r"
            low_parts(v, o, "wq", None, None, {}, ahead=True)
            rest = iter([(t, q) for t in range(UA) for q in range(4)])

            def beside(n=1):
                for t, q in itertools.islice(rest, n):
                    v.wait_ge(sem("high_done"), 4 * (UB + t) + q + 1)
                    o.do(v.tensor_tensor(part_l[:, q, :], ps[q][:, 0:512], part_h[:, q, :].bitcast(F32), ALU.subtract),
                         sem("low_done"))

            for i, (t0, n) in enumerate(TOK):
                v.wait_ge(sem("scr_copied"), 4 * i + 4)
                s3 = scr[0:n, i, :].rearrange("p (a k) -> p a k", k=PK)
                o.settle()

                def best16(src, m, val, idx, every, every_idx):
                    for half in range(2):
                        for a in range(m):
                            o.do(v.max(val[0:n, a, 8 * half:8 * half + 8], src[:, a, :]))
                            if a % every == every - 1:
                                beside()
                        o.settle()
                        for a in range(m):
                            o.do(v.max_index(idx[0:n, a, 8 * half:8 * half + 8], val[0:n, a, 8 * half:8 * half + 8],
                                             src[:, a, :]))
                            if half == 0:
                                o.do(v.match_replace(src[:, a, :], val[0:n, a, 0:8], src[:, a, :], -3.0e38))
                            if a % every_idx == 0:
                                beside()
                        o.settle()

                best16(s3, 16, tv, ti, 3, 3)
                o.do(v.tensor_copy(tf[0:n], ti[0:n]))
                t4 = tv[0:n].rearrange("p (h c) r -> p h c r", c=2)
                o.do(v.tensor_tensor(cand[0:n], bc(t4[:, :, 0, :], TK), t4[:, :, 1:2, :].to_broadcast([n, PH, TK, TK]),
                                     ALU.add))
                o.settle()
                best16(cand[0:n].rearrange("p h a b -> p h (a b)"), PH, vs, ic.rearrange(hr, r=TK), 3, 2)
                g = tok3[0:n, i, 2, :].rearrange(hr, r=TK)
                o.do(v.tensor_tensor(g, vs[0:n], vs[0:n, :, 0:1].to_broadcast([n, PH, TK]), ALU.subtract), sem("vdiff_ready"))
                f4 = tf[0:n].rearrange("p (h c) r -> p h c r", c=2)
                for c, (op, k) in enumerate(((ALU.logical_shift_right, 4), (ALU.bitwise_and, 15))):
                    o.do(v.tensor_scalar(ia[0:n], ic[0:n], k, None, op))
                    o.settle()
                    o.do(v.tensor_copy(iF[c][0:n], ia[0:n]))
                    o.settle()
                    e3 = eq[0:n].rearrange("p h r q -> p (h r) q")
                    o.do(v.tensor_tensor(e3, bc(iF[c][0:n], TK), iota[0:n, 0:TK].unsqueeze(1).to_broadcast([n, P, TK]),
                                         ALU.is_equal))
                    o.settle()
                    beside(2)
                    o.do(v.tensor_tensor(eq[0:n], eq[0:n], f4[:, :, c:c + 1, :].to_broadcast([n, PH, TK, TK]), ALU.mult))
                    o.settle()
                    beside(2)
                    o.do(v.tensor_reduce(tok3[0:n, i, c, :], e3, AX.X, ALU.add))
                    beside(2)
            beside(4 * UA)
            for i, (t0, n) in enumerate(TOK):
                g = tok3[0:n, i, 2, :].rearrange(hr, r=TK)
                v.wait_ge(sem("vexp_ready"), i + 1)
                o.do(v.tensor_reduce(gsum[0:n, 0, :], g, AX.X, ALU.add))
                o.settle()
                o.do(v.reciprocal(gsum[0:n, 1, :], gsum[0:n, 0, :]))
                o.settle()
                o.do(v.tensor_tensor(g, g, bc(gsum[0:n, 1, :], TK), ALU.mult), sem("tok3_ready"))
            v.wait_ge(sem("ex3_copied"), 3)

            v.wait_ge(sem("q_used"), 4 * (UB + UA))
            v.wait_ge(sem("tile_freed"), UB + UA)
            v.sem_inc(sem("spread_free"), 1)

            def onehots(i, s):
                o.do(v.tensor_tensor(ohB[s], iota[:].unsqueeze(1).to_broadcast([P, 4, P]),
                                     bc(ex3[:, 1, ds(i * 16 + 4 * s, 4)], P), ALU.is_equal))
                for j in range(OH_ACT[s], 4):
                    t = i * 16 + (4 * s + j)
                    o.do(v.tensor_scalar(ohA[s][:, j, :], iota[:], ex3[:, 0, ds(t, 1)], ex3[:, 2, ds(t, 1)],
                                         ALU.is_equal, ALU.mult), sem("oh_ready") if j == 3 else None)

            def scale(i, s):
                v.wait_ge(sem("g_copied"), i * 4 + (s + 1))
                d = dense[:, K0:PK, ds(i * 16 + 4 * s, 4)]
                o.do(v.tensor_tensor(d, d, ps[s][:, 0:512].rearrange("p (t k) -> p k t", k=P)[:, K0:PK, :], ALU.mult),
                     sem("g_scaled"))

            for s in range(4):
                onehots(0, s)
            with v.Fori(0, NSP - 1) as i:
                o.loop(i, {"oh_ready": 4, "g_scaled": 4, "dve_own": 16 - sum(OH_ACT)})
                for s in range(4):
                    scale(i, s)
                    onehots(i + 1, s)
                o.leave(NSP - 1)
            o.open = {}
            for s in range(4):
                scale(NSP - 1, s)

            def gate(i, c, s):
                v.wait_ge(sem("gelu_done"), i * 2 + (c + 1))
                a = work[:, ds(i * (2 * T) + c * T, T)]
                o.do(v.tensor_tensor(a, a, gel[:, s, :], ALU.mult), sem("tile_freed"))

            low_parts(v, o, "Ub", lambda q: ps[q][:, 0:512], gate, {"tile_freed": 2})
            for half in range(2):
                def four(i):
                    for s in range(4):
                        v.wait_ge(sem("ah_done"), i * 4 + (128 * half + s + 1))
                        o.do(v.tensor_tensor(act_l[:, s, :], work[:, ds(i * (4 * T) + s * T, T)],
                                             act_h[:, s, :].bitcast(F32), ALU.subtract), sem("al_done"))
                        v.wait_ge(sem("vh_done"), i * 4 + (128 * half + s + 1))
                        o.do(v.tensor_tensor(vl[:, s % 2, :], natural[s // 2][:, 1024 * (s % 2):1024 * (s % 2) + 1024],
                                             vh[:, s % 2, :].bitcast(F32), ALU.subtract), sem("vl_done"))
                with v.Fori(0, 32) as i:
                    o.loop(i, {"vl_done": 4, "al_done": 4})
                    four(i)
                    o.leave(32)
                o.open = {}
                v.wait_ge(sem("v_done"), 128 * (half + 1))
                if half == 0:
                    v.wait_ge(sem("h_back"), 16)
                for c in range(8):
                    h = hT[:, 8 * half + c, :]
                    o.do(v.tensor_tensor(h, h, ps[c][:, 0:T], ALU.add), sem("pv_added"))
            o.settle()

        proj = wk(0, 2, D)
        pN = wk(4096, 3, PLE)
        pT = wk(4864, 2, T)
        yout = wk(8192, 3, D)

        def sp_tail(sp):
            w = ins["w_ple_gate"][0].rearrange("(k p) n -> p k n", p=P)
            sp.wait_ge(sem("v_done"), 256)
            for i, (t0, n) in enumerate(TOK):
                src = ins["p_prompt"][0, 0, t0:t0 + n, :] if i < 2 else ins["p_sample"][0].rearrange("b s d -> (b s) d")
                sp.dma_start(pN[0:n, i, :], src).then_inc(sem("p_in"), 16)
            for s in range(2):
                sp.dma_start(natural[s].rearrange("p (k n) -> p k n", n=P), w[:, :, s * P:(s + 1) * P]).then_inc(
                    sem(f"nat_in{s}"), 16)
            sp.dma_start(proj, ins["w_ple_proj"][0].rearrange("(k p) n -> p k n", p=P)).then_inc(sem("proj_in"), 16)
            with sp.Fori(1, KD // 2) as i:
                for s in range(2):
                    sp.wait_ge(sem("low_done"), i * 8 + 4 * (TRIPLE["gate"][0] + s - 1))
                    sp.dma_start(natural[s].rearrange("p (k n) -> p k n", n=P), w[:, :, ds(i * 256 + s * P, P)]).then_inc(
                        sem(f"nat_in{s}"), 16)
            for i, (t0, n) in enumerate(TOK):
                dst = outs[0][0, t0:t0 + n, :] if i < 2 else outs[1].rearrange("b s d -> (b s) d")
                for q in range(2):
                    sp.wait_ge(sem(f"y_out{q}"), 2 * (i + 1))
                sp.dma_start(dst, yout[0:n, i, :]).then_inc(sem("y_stored"), 16)
            sp.wait_ge(sem("y_stored"), 48)

        def pe_tail(pe):
            pe.wait_ge(sem("p_in"), 48)
            pe.wait_ge(sem("pv_added"), 16)
            for i, (t0, n) in enumerate(TOK):
                for c in range(2):
                    m = pe.transpose(ps[c][:, t0:t0 + n], pN[0:n, i, c * P:(c + 1) * P], ident[0:n, 0:n])
            m.then_inc(sem("pt_done"), 1)
            pe_norm(pe, 2)
            pe.wait_ge(sem("pt_copied"), 1)
            pe.wait_ge(sem("proj_in"), 16)

            def embed(c8):
                for c in range(2 * c8, 2 * c8 + 2):
                    if c >= 2:
                        pe.wait_ge(sem("e_copied"), c - 1)
                    for k in range(2):
                        m = pe.matmul(ps[4 + c % 2][:, 0:T], proj[:, k, c * P:(c + 1) * P], pT[:, k, :],
                                      start=(k == 0), stop=(k == 1))
                    m.then_inc(sem("e_done"), 1)

            for c8 in range(8):
                embed(c8)
            pe.wait_ge(sem("e_copied"), KD)
            pe_triple(pe, "gate", ple_h, ple_l)
            pe_norm_summed(pe, 3)
            for g in range(12):
                i, q = divmod(g, 4)
                t0, n = TOK[i]
                if i == 0:
                    pe.wait_ge(sem("n_ready"), 3 * KD + 4 * (q + 1))
                if g >= 4:
                    pe.wait_ge(sem(f"y_out{g % 2}"), (g - 4) // 2 + 1)
                for j in range(4):
                    m = pe.transpose(ps[g % 4][0:n, j * P:(j + 1) * P], nT[:, 4 * q + j, t0:t0 + n], ident[:])
                m.then_inc(sem("yt_done"), 1)

        eT = wk(14336, KD, T)
        sg = wk(19000, 2, T)

        def act_tail(act, o):
            act.wait_ge(sem("pt_done"), 1)
            for c in range(2):
                o.do(act.copy(pT[:, c, :], ps[c][:, 0:T]), sem("pt_copied") if c else None)
            act.wait_ge(sem("pv_added"), 16)
            act_norm(act, 2, lambda: high_parts(act, o, "gate", None, {}, only_first=True))
            def copy_e(c):
                act.wait_ge(sem("e_done"), c + 1)
                o.do(act.copy(eT[:, c, :], ps[4 + c % 2][:, 0:T]), sem("e_copied"))

            act_norm_high(act, o, 2, ple_h, copy_e)

            def sig(i, c, s):
                b = TRIPLE["gate"][0]
                act.wait_ge(sem("q_used"), i * 8 + 4 * (b + c + 1))
                o.do(act.activation(sg[:, s, :], ps[4 + s][:, 0:T], ACT.Sigmoid), sem("sig_done"))

            o.open = {}
            high_parts(act, o, "gate", sig, {"sig_done": 2}, ahead=True)
            act_norm(act, 3)
            for g in range(0, 12, 2):
                i, q = divmod(g, 4)
                n = TOK[i][1]
                act.wait_ge(sem("yt_done"), g + 1)
                o.do(act.copy(yout[0:n, i, 512 * q:512 * q + 512], ps[g % 4][0:n, 0:512]), sem("y_out0"))

        def dve_tail(v, o):
            low_parts(v, o, "gate", None, None, {}, only_first=True)
            dve_norm(v, o, 2, ple_h, ple_l)
            v.wait_ge(sem("e_copied"), KD)

            squares = dve_squares(v, 3, "h_added")

            def gated(i, c, s):
                v.wait_ge(sem("sig_done"), i * 2 + (c + 1))
                e = work[:, ds(i * (2 * T) + (14336 + c * T), T)]
                h = low[:, ds(i * (2 * T) + c * T, T)]
                o.do(v.tensor_tensor(e, e, sg[:, s, :], ALU.mult), sem("tile_freed"))
                v.wait_ge(sem("tile_freed"), i * 2 + (TRIPLE["gate"][0] + c + 1))
                o.do(v.tensor_tensor(h, h, e, ALU.add), sem("h_added"))
                squares(i, c, s)

            low_parts(v, o, "gate", None, gated, {"tile_freed": 2, "h_added": 2}, ahead=True)
            o.open = {}
            v.wait_ge(sem("h_added"), KD)
            dve_norm(v, o, 3)
            for g in range(1, 12, 2):
                i, q = divmod(g, 4)
                n = TOK[i][1]
                v.wait_ge(sem("yt_done"), g + 1)
                o.do(v.tensor_copy(yout[0:n, i, 512 * q:512 * q + 512], ps[g % 4][0:n, 0:512]), sem("y_out1"))

        block = ctx.enter_context(nc.Block())

        @block.sync
        def _(sp):
            for i, (t0, n) in enumerate(TOK):
                src = ins["x_prompt"][0, t0:t0 + n, :] if i < 2 else ins["x_sample"].rearrange("b s d -> (b s) d")
                sp.dma_start(xin[0:n, i, :], src).then_inc(sem(f"x_in{i}"), 16)
            v = sem("vec_in")
            at = 0
            for name, rows in (("norm_mix", 16), ("norm_ffn", 16), ("norm_ple", 16), ("norm_final", 16),
                               ("mlstm_norm", 8), ("b_glu", 8)):
                a = ins[name] if name == "norm_final" else ins[name][0]
                sp.dma_start(vrow[at:at + rows, :], a.rearrange("(r p) -> r p", p=P)).then_inc(v, 16)
                at += rows
            sp.dma_start(vrow[80:88, :], ins["ssm_D"][0].rearrange("(u r) c -> u (r c)", r=8)).then_inc(v, 16)
            sp.dma_start(gb8[0:4], ins["b_igate"].rearrange("a h -> h a")).then_inc(v, 16)
            sp.dma_start(gb8[4:8], ins["b_fgate"].rearrange("a h -> h a")).then_inc(v, 16)

            def weights(name, src, c0):
                base, nb, kt = STREAM[name]
                w = src.rearrange("(k p) n -> p k n", p=P)
                first = 0
                if base == 0:
                    for s in range(2):
                        sp.dma_start(ring[:, s, 0:kt * WB].rearrange("p (k n) -> p k n", n=WB),
                                     w[:, :, c0 + s * WB:c0 + (s + 1) * WB]).then_inc(sem(f"w_in{s}"), 16)
                    first = 1
                with sp.Fori(first, nb // 2) as i:
                    for s in range(2):
                        sp.wait_ge(sem("mm_done"), i * 4 + 2 * (base + s) - 2)
                        sp.dma_start(ring[:, s, 0:kt * WB].rearrange("p (k n) -> p k n", n=WB),
                                     w[:, :, ds(i * (2 * WB) + (c0 + s * WB), WB)]).then_inc(sem(f"w_in{s}"), 16)

            sp.dma_start(m0b, ins["state_mlstm_m"][0].partition_broadcast(P)).then_inc(sem("m0_in"), 16)
            w_in = ins["w_in"][0]
            s5 = sem("s5_in")
            for q, name in enumerate(AB):
                sp.dma_start(r32[0:NJ, q, :], ins[name][0].rearrange("(j g) p -> j (g p)", g=2)).then_inc(s5, 16)
            sp.dma_start(dtr[0:NJ, :], ins["ssm_log_dt"][0].rearrange("(j g) -> j g", g=2)).then_inc(s5, 16)
            for q, name in enumerate(("re", "im")):
                sp.dma_start(Bn[q], ins[f"ssm_B_{name}"][0].rearrange("(j g) p c -> (g p) j c", g=2)).then_inc(s5, 16)
                sp.dma_start(Cn[q], ins[f"ssm_C_{name}"][0].rearrange("(u r) c p -> (r c) u p", r=8)).then_inc(s5, 16)
                sp.dma_start(s0r[:, :, q, :], ins[f"state_ssm_{name}"][0]
                             .rearrange("b (j g) p -> (b j) (g p)", g=2)
                             .rearrange("(t r) q -> r t q", t=2)).then_inc(s5, 16)
            sp.dma_start(gw, w_in[:, 4 * MW:4 * MW + 8].rearrange("(k p) n -> p k n", p=P)).then_inc(sem("gw_in"), 16)
            weights("u", w_in, 4 * MW + 8)
            weights("z", w_in, 0)
            weights("glu", ins["w_glu"][0], 0)
            sp_mlstm(sp)
            other_tiles(sp, "out", w_out)
            for q in range(3):
                sp.wait_ge(sem("tile_freed"), 4 * (q + 1))
                sp.dma_start(spill[:, 4 * q * T:4 * (q + 1) * T], low[:, 4 * q * T:4 * (q + 1) * T]).then_inc(
                    sem("h_spilled"), 16)
            tile_pair(sp, "wq", w_q, 0)
            sp.wait_ge(sem("tile_freed"), KD)
            sp.dma_start(spill[:, 12 * T:16 * T], low[:, 12 * T:16 * T]).then_inc(sem("rest_spilled"), 16)
            other_tiles(sp, "wq", w_q)
            sp_peer(sp)
            sp_tail(sp)

        @block.gpsimd
        def _(pool):
            o = Own(pool, sem("pool_own"))
            o.do(pool.memset(ident[:], 0.0))
            o.do(pool.memset(ones[:], 1.0))
            o.do(pool.memset(par[:, 0:4], 1.0))
            o.do(pool.memset(bmask, 1.0))
            o.settle()
            o.do(pool.affine_select(out=ident[:], in_=ident[:], compare_op=ALU.not_equal, fill=1.0, base=0,
                                    pattern=[[-1, P]], channel_multiplier=1))
            o.do(pool.iota(iota[:], [[1, P]], base=0, channel_multiplier=0, allow_small_or_imprecise_dtypes=True))
            o.do(pool.affine_select(out=tri, in_=ones[:], compare_op=ALU.is_ge, fill=0.0, base=0,
                                    pattern=[[1, P]], channel_multiplier=-1))
            o.do(pool.affine_select(out=trs, in_=ones[0:TS, 0:TS], compare_op=ALU.is_ge, fill=0.0, base=0,
                                    pattern=[[1, TS]], channel_multiplier=-1))
            o.settle()
            tv = trs.rearrange("p (b s) -> p b s", s=NS)
            o.do(pool.affine_select(out=tv, in_=tv, compare_op=ALU.is_ge, fill=0.0, base=0,
                                    pattern=[[-NS, NB], [0, NS]], channel_multiplier=1))
            o.do(pool.affine_select(out=bmask, in_=bmask, compare_op=ALU.is_ge, fill=0.0, base=0,
                                    pattern=[[-NS, NB]], channel_multiplier=1))
            o.do(pool.affine_select(out=par[:, 0:4], in_=par[:, 0:4], compare_op=ALU.is_ge, fill=0.0, base=0,
                                    pattern=[[-32, 4]], channel_multiplier=1))
            o.settle()
            o.do(pool.affine_select(out=bmask, in_=bmask, compare_op=ALU.is_ge, fill=0.0, base=NS - 1,
                                    pattern=[[NS, NB]], channel_multiplier=-1))
            o.do(pool.affine_select(out=par[:, 0:4], in_=par[:, 0:4], compare_op=ALU.is_ge, fill=0.0, base=15,
                                    pattern=[[32, 4]], channel_multiplier=-1))
            o.settle()
            o.do(pool.memset(par[:, 7:8], 0.0), sem("const_ready"))

        @block.tensor
        def _(pe):
            pe.wait_ge(sem("const_ready"), 1)
            for g in range(12):
                i, q = divmod(g, 4)
                n = TOK[i][1]
                if q == 0:
                    pe.wait_ge(sem(f"x_in{i}"), 16)
                if g >= 4:
                    pe.wait_ge(sem(f"xt_copied{g % 2}"), (g - 4) // 2 + 1)
                for j in range(4):
                    m = pe.transpose(ps[g % 4][:, j * n:(j + 1) * n],
                                     xin[0:n, i, (4 * q + j) * P:(4 * q + j + 1) * P], ident[0:n, 0:n])
                m.then_inc(sem("xt_done"), 1)
            pe.wait_ge(sem("vec_in"), 16 * 9)
            pe.transpose(ps[4][:, 0:88], vrow[0:88, :], ident[0:88, 0:88]).then_inc(sem("vec_done"), 1)
            pe_norm(pe, 0)
            pe.wait_ge(sem("xt_copied0"), 6)
            pe.wait_ge(sem("xt_copied1"), 6)
            pe_linear(pe, "u", nT)
            pe.wait_ge(sem("gw_in"), 16)
            for k in range(KD):
                m = pe.matmul(ps[5][0:8, 0:T], gw[:, k, :], nT[:, k, :], start=(k == 0), stop=(k == KD - 1))
            m.then_inc(sem("gate_done"), 1)
            pe.wait_ge(sem("abf_rows"), 1)
            for q in range(4):
                m = pe.transpose(ps[4][:, q * NJ:(q + 1) * NJ], r32[0:NJ, 10 + q, :], ident[0:NJ, 0:NJ])
            m.then_inc(sem("abf_done"), 1)
            pe.wait_ge(sem("s5_in"), 16 * 9)
            for q in range(2):
                for t in range(2):
                    m = pe.transpose(ps[6][:, (2 * q + t) * P:(2 * q + t + 1) * P], s0r[:, t, q, :], ident[:])
            m.then_inc(sem("s0_done"), 1)
            pe.wait_ge(sem("gate_copied"), 1)
            pe.wait_ge(sem("abf_copied"), 1)
            pe.wait_ge(sem("s0_copied"), 1)
            for g in range(8):
                src, q, half = [Bbd, Cbd][g // 4], (g // 2) % 2, g % 2
                pe.wait_ge(sem("bd_ready"), g // 4 + 1)
                if g >= 4:
                    pe.wait_ge(sem("bct_copied"), g - 3)
                for j in range(4):
                    u = 4 * half + j
                    if g < 4:
                        a = Bbd[q][:, 4 * u:4 * u + 4, :, :].rearrange("p a b c -> p (a b c)")
                    else:
                        a = Cbd[q][:, u, :, :].rearrange("p b c -> p (b c)")
                    m = pe.transpose(ps[4 + g % 4][:, j * P:(j + 1) * P], a, ident[:])
                m.then_inc(sem("bct_done"), 1)
            pe.wait_ge(sem("bct_copied"), 8)
            pe.wait_ge(sem("mm_freed"), 8)
            for j in range(NJ):
                u, r = divmod(j, 4)
                if j >= 2:
                    pe.wait_ge(sem("bu_copied0"), j - 1)
                    pe.wait_ge(sem("bu_copied1"), j - 1)
                for q in range(2):
                    pe.matmul(ps[4 + 2 * (j % 2) + q][:, 0:T], BT[q][32 * r:32 * r + 32, u, :],
                              uT[32 * r:32 * r + 32, u, :], start=True, stop=True).then_inc(sem("bu_done"), 1)
            pe_linear(pe, "z", nT)
            pe.wait_ge(sem("s5_ready"), 1)
            pe.wait_ge(sem("bu_copied0"), NJ)
            pe.wait_ge(sem("bu_copied1"), NJ)
            for u in range(8):
                if u >= 2:
                    pe.wait_ge(sem("y_sum"), u - 1)
                for r in range(4):
                    for q in range(2):
                        m = pe.matmul(ps[4 + u % 2][32 * r:32 * r + 32, 0:T], CT[q][:, u, 32 * r:32 * r + 32],
                                      st[q][:, 4 * u + r, :], start=(q == 0), stop=(q == 1))
                m.then_inc(sem("y_done"), 1)
            pe.wait_ge(sem("send_ready"), 1)
            for q in range(2):
                pe.transpose(ps[6][0:NJ, q * P:(q + 1) * P], send[:, q, 0, :], ident[:])
                for t in range(2):
                    m = pe.transpose(ps[7][:, (2 * q + t) * P:(2 * q + t + 1) * P],
                                     send[:, q, 1 + 4 * t:5 + 4 * t, :].rearrange("p a b -> p (a b)"), ident[:])
            m.then_inc(sem("send_done"), 1)
            for r in range(8):
                if r == 0:
                    pe.wait_ge(sem("sout_ready"), 1)
                if r >= 4:
                    pe.wait_ge(sem("bc_copied"), r - 3)
                pe.matmul(ps[4 + r % 4][:, 0:T], ident[0:8, r:r + 1].to_broadcast([8, P]), rows8,
                          start=True, stop=True).then_inc(sem("bc_done"), 1)
            pe_linear(pe, "glu", uT)
            pe_mlstm(pe)
            pe.wait_ge(sem("glu_ready"), 8)
            pe_triple(pe, "out", mix_h, mix_l)
            pe_norm_summed(pe, 1)
            pe_triple(pe, "wq", ffn_h, ffn_l)
            pe_peer(pe)
            pe_tail(pe)

        @block.scalar
        def _(act):
            o_act.eng = act
            o = o_act
            for g in range(0, 12, 2):
                i, q = divmod(g, 4)
                t0, n = TOK[i]
                act.wait_ge(sem("xt_done"), g + 1)
                o.do(act.copy(hT[:, 4 * q:4 * q + 4, t0:t0 + n],
                              ps[g % 4][:, 0:4 * n].rearrange("p (a b) -> p a b", b=n)), sem("xt_copied0"))
            act.wait_ge(sem("vec_done"), 1)
            o.do(act.copy(gv[:], ps[4][:, 0:88]), sem("vec_copied"))
            act.wait_ge(sem("xt_copied1"), 6)
            o.settle()
            act_norm(act, 0)
            act.wait_ge(sem("s5_in"), 16 * 9)
            o.do(act.activation(dtr[0:NJ, :], dtr[0:NJ, :], ACT.Exp), sem("dt_ready"))

            def copy_tiles(name, dst, fn=None):
                base, nb, kt = STREAM[name]

                def one(i, b, peeled=False):
                    act.wait_ge(sem("mm_done"), i * 4 + (2 * base + b + 1))
                    src = ps[b][:, 0:T]
                    d = dst[:, b, :] if peeled else dst[:, ds(i * 4 + b, 1), :]
                    if not peeled:
                        src = src.unsqueeze(1)
                    o.do(act.copy(d, src), sem("mm_freed"))
                with act.Fori(0, nb // 2) as i:
                    o.loop(i, {"mm_freed": 4})
                    for b in range(4):
                        one(i, b)
                    o.leave(nb // 2)

            copy_tiles("u", uT)
            act.wait_ge(sem("theta_ready"), 1)
            o.do(act.activation(r32[0:NJ, 4, :], r32[0:NJ, 2, :], ACT.Exp))
            o.do(act.activation(r32[0:NJ, 5, :], r32[0:NJ, 3, :], ACT.Sin))
            o.do(act.activation(r32[0:NJ, 6, :], r32[0:NJ, 3, :], ACT.Sin, scale=0.5), sem("trig_ready"))
            o.settle()
            act.wait_ge(sem("s0_done"), 1)
            o.do(act.copy(s0T, ps[6][:, 0:512].rearrange("p (a b) -> p a b", a=2)), sem("s0_copied"))
            for g in range(8):
                dst = [BT, CT][g // 4][(g // 2) % 2]
                half = g % 2
                act.wait_ge(sem("bct_done"), g + 1)
                o.do(act.copy(dst[:, 4 * half:4 * half + 4, :],
                              ps[4 + g % 4][:, 0:512].rearrange("p (a b) -> p a b", b=P)), sem("bct_copied"))
            for j in range(NJ):
                act.wait_ge(sem("bu_done"), 2 * j + 1)
                o.do(act.copy(st[0][:, j, :], ps[4 + 2 * (j % 2)][:, 0:T]), sem("bu_copied0"))
            copy_tiles("z", zT)
            for u in range(8):
                act.wait_ge(sem("y_sum"), u + 1)
                o.do(act.activation(uT[:, u, :], uT[:, u, :], ACT.Gelu_apprx_tanh), sem("yg_ready"))
            o.settle()
            act.wait_ge(sem("send_done"), 1)
            o.do(act.copy(sout[0:NJ, 0:2, :], ps[6][0:NJ, 0:2 * P].rearrange("p (a b) -> p a b", b=P)))
            o.do(act.copy(sout[:, 2:6, :], ps[7][:, 0:512].rearrange("p (a b) -> p a b", b=P)), sem("sout_ready"))
            for r in range(8):
                act.wait_ge(sem("bc_done"), r + 1)
                o.do(act.copy(exf[:, r, :], ps[4 + r % 4][:, 0:T]), sem("bc_copied"))
            o.settle()
            o.do(act.activation(r2, rF, ACT.Abs))
            o.settle()
            o.do(act.activation(r2, r2, ACT.Exp, scale=-1.0))
            o.settle()
            o.do(act.activation(r2, r2, ACT.Ln, bias=1.0), sem("ln_ready"))
            o.do(act.activation(zT[:, 24:32, :], zT[:, 24:32, :], ACT.Sigmoid), sem("og_ready"))
            base = STREAM["glu"][0]
            for c in range(8):
                act.wait_ge(sem("mm_done"), 2 * base + c + 1)
                if c >= 2:
                    act.wait_ge(sem("glu_ready"), c - 1)
                o.do(act.activation(gel[:, c % 2, :], ps[c % 4][:, 0:T], ACT.Sigmoid, bias=gv[:, 72 + c:73 + c]),
                     sem("mm_freed"))
            act_mlstm(act, o)
            high_parts(act, o, "out", None, {}, ahead=True)
            high_parts(act, o, "wq", None, {}, only_first=True)
            act_norm(act, 1)
            act_norm_high(act, o, 1, ffn_h)
            act_peer(act, o)
            act_tail(act, o)

        @block.vector
        def _(v):
            o = Own(v, sem("dve_own"))
            v.wait_ge(sem("const_ready"), 1)
            for g in range(1, 12, 2):
                i, q = divmod(g, 4)
                t0, n = TOK[i]
                v.wait_ge(sem("xt_done"), g + 1)
                o.do(v.tensor_copy(hT[:, 4 * q:4 * q + 4, t0:t0 + n],
                                   ps[g % 4][:, 0:4 * n].rearrange("p (a b) -> p a b", b=n)), sem("xt_copied1"))
            v.wait_ge(sem("vec_copied"), 1)
            v.wait_ge(sem("xt_copied0"), 6)
            dve_norm(v, o, 0)
            dve_s5_setup(v, o)
            for j in range(NJ):
                v.wait_ge(sem("bu_done"), 2 * j + 2)
                o.do(v.tensor_copy(st[1][:, j, :], ps[5 + 2 * (j % 2)][:, 0:T]), sem("bu_copied1"))
            v.wait_ge(sem("bu_copied0"), NJ)
            dve_s5_scan(v, o)
            for u in range(8):
                v.wait_ge(sem("y_done"), u + 1)
                o.do(v.scalar_tensor_tensor(uT[:, u, :], uT[:, u, :], gv[:, 80 + u:81 + u], ps[4 + u % 2][:, 0:T],
                                            ALU.mult, ALU.add), sem("y_sum"))
            dve_gate_rows(v, o)
            base = STREAM["glu"][0]
            for c in range(8):
                v.wait_ge(sem("mm_freed"), 2 * base + c + 1)
                o.do(v.tensor_tensor(mix[:, 8 + c, :], uT[:, c, :], gel[:, c % 2, :], ALU.mult), sem("glu_ready"))
            dve_mlstm(v, o)

            squares = dve_squares(v, 1, "tile_freed")

            def add(i, c, s):
                v.wait_ge(sem("q_used"), i * 8 + (4 * c + 4))
                h = low[:, ds(i * (2 * T) + c * T, T)]
                o.do(v.tensor_tensor(h, h, ps[4 + s][:, 0:T], ALU.add), sem("tile_freed"))
                squares(i, c, s)

            low_parts(v, o, "out", None, add, {"tile_freed": 2}, ahead=True)
            o.settle()
            low_parts(v, o, "wq", None, None, {}, only_first=True)
            dve_norm(v, o, 1, ffn_h, ffn_l)
            dve_peer(v, o)
            dve_tail(v, o)


_INS = ["x_prompt", "x_sample", "state_mlstm_C", "state_mlstm_n", "state_mlstm_m", "state_ssm_re", "state_ssm_im",
        "p_prompt", "p_sample", "norm_mix", "w_in", "b_igate", "b_fgate", "mlstm_norm", "ssm_A_re", "ssm_A_im",
        "ssm_B_re", "ssm_B_im", "ssm_C_re", "ssm_C_im", "ssm_D", "ssm_log_dt", "w_glu", "b_glu", "w_out", "norm_ffn",
        "peer_w_q", "peer_keys", "peer_u", "peer_v", "norm_ple", "w_ple_gate", "w_ple_proj", "norm_final"]
_OUTS = [(1, TP, D), (NB, NS, D),
         (1, 1, H, DH, DH), (1, 1, H, DH), (1, 1, H), (1, 1, G, SP_), (1, 1, G, SP_),
         (1, NB, H, DH, DH), (1, NB, H, DH), (1, NB, H), (1, NB, G, SP_), (1, NB, G, SP_)]


def kernel(**inputs):
    import numpy as np
    import concourse.bacc as bacc
    from concourse.bass_utils import run_bass_kernel_spmd

    nc = bacc.Bacc("TRN2", target_bir_lowering=False, num_devices=1, dynamic_dma_scratch_size=1024)
    arrays, ins = {}, {}
    for name in _INS:
        a = np.ascontiguousarray(inputs[name])
        arrays[f"in_{name}"] = a
        ins[name] = nc.dram_tensor(f"in_{name}", a.shape, mybir.dt.from_np(a.dtype), kind="ExternalInput").ap()
    outs = [nc.dram_tensor(f"out_{i}", shape, F32, kind="ExternalOutput").ap() for i, shape in enumerate(_OUTS)]
    build(nc, ins, outs)
    r = run_bass_kernel_spmd(nc, [arrays], core_ids=[0])
    return tuple(r.results[0][f"out_{i}"] for i in range(len(_OUTS)))
```
